# Optimizing a Trainium2 kernel written in Bass

```python
import jax, jax.numpy as jnp
from jax import lax
import numpy as np

D_MODEL = 1024
BATCH = 1
SEQ = 128
DEPTH = 2
DEC_BATCH = 1
DEC_SEQ = 2048
PAST_LEN = 256

GRID_W = 64
N_MIXERS = 2
N_ATTN_LAYERS = (DEPTH + 1) // 2
N_MLSTM_LAYERS = DEPTH // 2
HEAD_DIM = 64
N_HEADS = D_MODEL // HEAD_DIM
N_KV_HEADS = N_HEADS // 4
GROUP = N_HEADS // N_KV_HEADS
WINDOW = 128
QBLK = 128
KWIN = QBLK + 2 * WINDOW
ROPE_BASE = 10000.0
ATTN_Q_DIM = N_HEADS * HEAD_DIM
ATTN_KV_DIM = N_KV_HEADS * HEAD_DIM
ATTN_IN_DIM = 2 * ATTN_Q_DIM + 2 * ATTN_KV_DIM
M_HEADS = 8
M_HD = D_MODEL // M_HEADS
M_DIM = M_HEADS * M_HD
M_CHUNK = 64
M_IN_DIM = 5 * M_DIM + 4 * M_HEADS
EPS = 1e-6

kernel_name = 'hybrid_dit_swa_mlstm_step'

def _rmsnorm(x, w):
    x32 = x.astype(jnp.float32)
    y = x32 * lax.rsqrt(jnp.mean(x32 * x32, axis=-1, keepdims=True) + EPS)
    return (y * w.astype(jnp.float32)).astype(x.dtype)

def _pre(x, cond, norm_w, ada_w, ada_b):
    mod = jax.nn.silu(cond) @ ada_w + ada_b
    shift, scale, gate = jnp.split(mod, 3, axis=-1)
    h = _rmsnorm(x, norm_w) * (1 + scale[:, None, :]) + shift[:, None, :]
    return h, gate[:, None, :]

def _branch_out(o, g, w_out):
    return (o * jax.nn.silu(g)) @ w_out

def _axial_rope(x):
    T = x.shape[1]
    rows = T // GRID_W
    row = jnp.repeat(jnp.arange(rows), GRID_W).astype(jnp.float32)
    col = jnp.tile(jnp.arange(GRID_W), rows).astype(jnp.float32)
    nf = HEAD_DIM // 4
    inv = ROPE_BASE ** (-jnp.arange(nf, dtype=jnp.float32) / nf)
    shape = (1, T) + (1,) * (x.ndim - 3) + (nf,)
    x32 = x.astype(jnp.float32)

    def rot(xh, pos):
        ang = (pos[:, None] * inv[None, :]).reshape(shape)
        cos, sin = jnp.cos(ang), jnp.sin(ang)
        x1, x2 = xh[..., :nf], xh[..., nf:]
        return jnp.concatenate([x1 * cos - x2 * sin, x1 * sin + x2 * cos], axis=-1)

    half = HEAD_DIM // 2
    out = jnp.concatenate([rot(x32[..., :half], row), rot(x32[..., half:], col)], axis=-1)
    return out.astype(x.dtype)

def _sink_attend(q, k, v, mask, sink):
    s = jnp.einsum('bqhgd,bkhd->bhgqk', q.astype(jnp.float32), k.astype(jnp.float32)) * (HEAD_DIM ** -0.5)
    if mask is not None:
        s = jnp.where(mask, s, -jnp.inf)
    sk = sink.astype(jnp.float32).reshape(1, N_KV_HEADS, GROUP, 1)
    m = jnp.maximum(jnp.max(s, axis=-1), sk)
    p = jnp.exp(s - m[..., None])
    den = jnp.sum(p, axis=-1) + jnp.exp(sk - m)
    o = jnp.einsum('bhgqk,bkhd->bqhgd', p, v.astype(jnp.float32))
    return (o / jnp.transpose(den, (0, 3, 1, 2))[..., None]).astype(q.dtype)

def _attn_project(h, w_in):
    B, T, _ = h.shape
    p = h @ w_in
    q = p[..., :ATTN_Q_DIM].reshape(B, T, N_KV_HEADS, GROUP, HEAD_DIM)
    g = p[..., ATTN_Q_DIM:2 * ATTN_Q_DIM]
    k = p[..., 2 * ATTN_Q_DIM:2 * ATTN_Q_DIM + ATTN_KV_DIM].reshape(B, T, N_KV_HEADS, HEAD_DIM)
    v = p[..., 2 * ATTN_Q_DIM + ATTN_KV_DIM:].reshape(B, T, N_KV_HEADS, HEAD_DIM)
    return q, g, k, v

def _ctx_attention(q, k, v, sink):
    B, S = q.shape[:2]
    nb = S // QBLK
    qb = jnp.moveaxis(q.reshape(B, nb, QBLK, N_KV_HEADS, GROUP, HEAD_DIM), 1, 0)
    o = lax.map(lambda qi: _sink_attend(qi, k, v, None, sink), qb)
    return jnp.moveaxis(o, 0, 1).reshape(B, S, ATTN_Q_DIM)

def _latent_attention(q, k, v, ck, cv, sink):
    B, T = q.shape[:2]
    P = ck.shape[1]
    nb = T // QBLK
    pad = ((0, 0), (WINDOW, WINDOW), (0, 0), (0, 0))
    kp = jnp.pad(k, pad)
    vp = jnp.pad(v, pad)
    qi = jnp.arange(QBLK)[:, None]
    kj = jnp.arange(KWIN)[None, :]
    band = (kj >= qi) & (kj - qi <= 2 * WINDOW)
    ctx_ok = jnp.ones((QBLK, P), dtype=bool)
    qb = jnp.moveaxis(q.reshape(B, nb, QBLK, N_KV_HEADS, GROUP, HEAD_DIM), 1, 0)

    def block(args):
        qblk, b = args
        start = b * QBLK
        kb = lax.dynamic_slice_in_dim(kp, start, KWIN, axis=1)
        vb = lax.dynamic_slice_in_dim(vp, start, KWIN, axis=1)
        pos = start - WINDOW + kj
        valid = band & (pos >= 0) & (pos < T)
        mask = jnp.concatenate([ctx_ok, valid], axis=1)
        keys = jnp.concatenate([ck.astype(kb.dtype), kb], axis=1)
        vals = jnp.concatenate([cv.astype(vb.dtype), vb], axis=1)
        return _sink_attend(qblk, keys, vals, mask, sink)

    o = lax.map(block, (qb, jnp.arange(nb)))
    return jnp.moveaxis(o, 0, 1).reshape(B, T, ATTN_Q_DIM)

def _attn_context_layer(x, cond, norm_w, ada_w, ada_b, w_in, sink, w_out):
    h, gate = _pre(x, cond, norm_w, ada_w, ada_b)
    q, g, k, v = _attn_project(h, w_in)
    o = _ctx_attention(q, k, v, sink)
    return x + gate * _branch_out(o, g, w_out), k, v

def _attn_latent_layer(x, cond, ck, cv, norm_w, ada_w, ada_b, w_in, sink, w_out):
    h, gate = _pre(x, cond, norm_w, ada_w, ada_b)
    q, g, k, v = _attn_project(h, w_in)
    q = _axial_rope(q)
    k = _axial_rope(k)
    o = _latent_attention(q, k, v, ck, cv, sink)
    return x + gate * _branch_out(o, g, w_out)

def _mlstm_scan(q, k, v, ig, fg, init):
    C0, n0, m0 = init
    B, T, H, DK = q.shape
    DV = v.shape[-1]
    nc = T // M_CHUNK

    def chunks(a):
        return jnp.moveaxis(a.astype(jnp.float32).reshape((B, nc, M_CHUNK) + a.shape[2:]), 1, 0)

    xs = (chunks(q), chunks(k) * (DK ** -0.5), chunks(v), chunks(ig),
          chunks(jax.nn.log_sigmoid(fg.astype(jnp.float32))))
    causal = jnp.tril(jnp.ones((M_CHUNK, M_CHUNK), dtype=bool))

    def step(carry, inp):
        C, n, m = carry
        qc, kc, vc, ic, lfc = inp
        b = jnp.transpose(jnp.cumsum(lfc, axis=1), (0, 2, 1))
        it = jnp.transpose(ic, (0, 2, 1))
        a = jnp.where(causal, b[..., :, None] - b[..., None, :] + it[..., None, :], -jnp.inf)
        a0 = b + m[..., None]
        mt = jnp.maximum(a0, jnp.max(a, axis=-1))
        w = jnp.exp(a - mt[..., None])
        w0 = jnp.exp(a0 - mt)
        s = jnp.einsum('blhd,bshd->bhls', qc, kc) * w
        w0t = jnp.transpose(w0, (0, 2, 1))[..., None]
        num = jnp.einsum('bhls,bshe->blhe', s, vc) + w0t * jnp.einsum('blhd,bhde->blhe', qc, C)
        den = jnp.sum(s, axis=-1) + w0 * jnp.einsum('blhd,bhd->bhl', qc, n)
        den = jnp.maximum(jnp.abs(den), jnp.exp(-mt))
        hc = num / jnp.transpose(den, (0, 2, 1))[..., None]
        bl = b[..., -1]
        ak = it + bl[..., None] - b
        m_new = jnp.maximum(bl + m, jnp.max(ak, axis=-1))
        wk = jnp.transpose(jnp.exp(ak - m_new[..., None]), (0, 2, 1))[..., None]
        decay = jnp.exp(bl + m - m_new)
        kw = kc * wk
        C_new = decay[..., None, None] * C + jnp.einsum('bshd,bshe->bhde', kw, vc)
        n_new = decay[..., None] * n + jnp.sum(kw, axis=1)
        return (C_new, n_new, m_new), hc

    init32 = (C0.astype(jnp.float32), n0.astype(jnp.float32), m0.astype(jnp.float32))
    state, hs = lax.scan(step, init32, xs)
    h = jnp.moveaxis(hs, 0, 1).reshape(B, T, H, DV)
    return h, state

def _mlstm_layer(x, cond, init_f, init_b, norm_w, ada_w, ada_b, w_in, b_gates, w_out):
    B, T, _ = x.shape
    h, gate = _pre(x, cond, norm_w, ada_w, ada_b)
    p = h @ w_in
    q = p[..., :M_DIM].reshape(B, T, M_HEADS, M_HD)
    k = p[..., M_DIM:2 * M_DIM].reshape(B, T, M_HEADS, M_HD)
    v = p[..., 2 * M_DIM:3 * M_DIM].reshape(B, T, M_HEADS, M_HD)
    o = p[..., 3 * M_DIM:4 * M_DIM]
    g = p[..., 4 * M_DIM:5 * M_DIM]
    gates = (p[..., 5 * M_DIM:] + b_gates).astype(jnp.float32).reshape(B, T, 4, M_HEADS)
    i_f, f_f, i_b, f_b = gates[..., 0, :], gates[..., 1, :], gates[..., 2, :], gates[..., 3, :]
    hf, sf = _mlstm_scan(q, k, v, i_f, f_f, init_f)
    fl = lambda a: jnp.flip(a, axis=1)
    hb, sb = _mlstm_scan(fl(q), fl(k), fl(v), fl(i_b), fl(f_b), init_b)
    hm = (hf + fl(hb)).reshape(B, T, M_DIM) * jax.nn.sigmoid(o.astype(jnp.float32))
    y = _branch_out(hm.astype(x.dtype), g, w_out)
    return x + gate * y, sf, sb

def setup_inputs(seed: int = 0) -> dict:
    key = jax.random.key(seed)
    ks = jax.random.split(key, 24)

    def nrm(k, shape, s):
        return s * jax.random.normal(k, shape, dtype=jnp.float32)

    D = D_MODEL
    i_bias = nrm(ks[19], (N_MLSTM_LAYERS, 2, M_HEADS), 0.1)
    f_bias = 3.0 + nrm(ks[20], (N_MLSTM_LAYERS, 2, M_HEADS), 0.5)
    b_gates = jnp.stack([i_bias[:, 0], f_bias[:, 0], i_bias[:, 1], f_bias[:, 1]], axis=1).reshape(N_MLSTM_LAYERS, 4 * M_HEADS)
    return {
        'x_prompt': nrm(ks[0], (BATCH, SEQ, D), 1.0),
        'x_sample': nrm(ks[1], (DEC_BATCH, DEC_SEQ, D), 1.0),
        'cache_k': nrm(ks[2], (DEC_BATCH, N_ATTN_LAYERS, PAST_LEN, N_KV_HEADS, HEAD_DIM), 1.0),
        'cache_v': nrm(ks[3], (DEC_BATCH, N_ATTN_LAYERS, PAST_LEN, N_KV_HEADS, HEAD_DIM), 1.0),
        'state_C': nrm(ks[4], (DEC_BATCH, N_MLSTM_LAYERS, 2, M_HEADS, M_HD, M_HD), 0.5),
        'state_n': nrm(ks[5], (DEC_BATCH, N_MLSTM_LAYERS, 2, M_HEADS, M_HD), 0.5),
        'state_m': nrm(ks[6], (DEC_BATCH, N_MLSTM_LAYERS, 2, M_HEADS), 0.5),
        'c': nrm(ks[7], (DEC_BATCH, D), 1.0),
        'c_ctx': nrm(ks[8], (D,), 1.0),
        'attn_norm_w': 1.0 + nrm(ks[9], (N_ATTN_LAYERS, D), 0.02),
        'attn_ada_w': nrm(ks[10], (N_ATTN_LAYERS, D, 3 * D), 0.5 * D ** -0.5),
        'attn_ada_b': nrm(ks[11], (N_ATTN_LAYERS, 3 * D), 0.02),
        'attn_w_in': nrm(ks[12], (N_ATTN_LAYERS, D, ATTN_IN_DIM), D ** -0.5),
        'attn_sink': nrm(ks[13], (N_ATTN_LAYERS, N_HEADS), 0.5),
        'attn_w_out': nrm(ks[14], (N_ATTN_LAYERS, ATTN_Q_DIM, D), ATTN_Q_DIM ** -0.5),
        'mlstm_norm_w': 1.0 + nrm(ks[15], (N_MLSTM_LAYERS, D), 0.02),
        'mlstm_ada_w': nrm(ks[16], (N_MLSTM_LAYERS, D, 3 * D), 0.5 * D ** -0.5),
        'mlstm_ada_b': nrm(ks[17], (N_MLSTM_LAYERS, 3 * D), 0.02),
        'mlstm_w_in': nrm(ks[18], (N_MLSTM_LAYERS, D, M_IN_DIM), D ** -0.5),
        'mlstm_b_gates': b_gates,
        'mlstm_w_out': nrm(ks[21], (N_MLSTM_LAYERS, M_DIM, D), M_DIM ** -0.5),
        'final_norm_w': 1.0 + nrm(ks[22], (D,), 0.02),
    }

def reference(x_prompt, x_sample, cache_k, cache_v, state_C, state_n, state_m, c, c_ctx,
              attn_norm_w, attn_ada_w, attn_ada_b, attn_w_in, attn_sink, attn_w_out,
              mlstm_norm_w, mlstm_ada_w, mlstm_ada_b, mlstm_w_in, mlstm_b_gates, mlstm_w_out,
              final_norm_w):
    B = x_prompt.shape[0]
    ctx_cond = c_ctx[None, :]
    zero_init = (jnp.zeros((B, M_HEADS, M_HD, M_HD), jnp.float32),
                 jnp.zeros((B, M_HEADS, M_HD), jnp.float32),
                 jnp.zeros((B, M_HEADS), jnp.float32))

    x = x_prompt
    ks_, vs_, Cs, ns, ms = [], [], [], [], []
    for i in range(DEPTH):
        j = i // N_MIXERS
        if i % N_MIXERS == 0:
            x, k, v = _attn_context_layer(x, ctx_cond, attn_norm_w[j], attn_ada_w[j], attn_ada_b[j],
                                          attn_w_in[j], attn_sink[j], attn_w_out[j])
            ks_.append(k)
            vs_.append(v)
        else:
            x, sf, sb = _mlstm_layer(x, ctx_cond, zero_init, zero_init, mlstm_norm_w[j], mlstm_ada_w[j],
                                     mlstm_ada_b[j], mlstm_w_in[j], mlstm_b_gates[j], mlstm_w_out[j])
            Cs.append(jnp.stack([sf[0], sb[0]], axis=1))
            ns.append(jnp.stack([sf[1], sb[1]], axis=1))
            ms.append(jnp.stack([sf[2], sb[2]], axis=1))
    y_prompt = _rmsnorm(x, final_norm_w)

    x = x_sample
    for i in range(DEPTH):
        j = i // N_MIXERS
        if i % N_MIXERS == 0:
            x = _attn_latent_layer(x, c, cache_k[:, j], cache_v[:, j], attn_norm_w[j], attn_ada_w[j],
                                   attn_ada_b[j], attn_w_in[j], attn_sink[j], attn_w_out[j])
        else:
            init_f = (state_C[:, j, 0], state_n[:, j, 0], state_m[:, j, 0])
            init_b = (state_C[:, j, 1], state_n[:, j, 1], state_m[:, j, 1])
            x, _, _ = _mlstm_layer(x, c, init_f, init_b, mlstm_norm_w[j], mlstm_ada_w[j], mlstm_ada_b[j],
                                   mlstm_w_in[j], mlstm_b_gates[j], mlstm_w_out[j])
    y_sample = _rmsnorm(x, final_norm_w)

    new_cache_k = jnp.stack(ks_, axis=1)
    new_cache_v = jnp.stack(vs_, axis=1)
    new_state_C = jnp.stack(Cs, axis=1)
    new_state_n = jnp.stack(ns, axis=1)
    new_state_m = jnp.stack(ms, axis=1)
    return (y_prompt, y_sample, new_cache_k, new_cache_v, new_state_C, new_state_n, new_state_m)


_drawn_inputs = setup_inputs


def setup_inputs(seed=0):
    import zlib

    import numpy as np

    out = dict(_drawn_inputs(seed))
    spreads = {}
    factors = {'state_m': 11.548,
     'attn_norm_w': 2.898,
     'attn_sink': 64.0,
     'final_norm_w': 21.443,
     'cache_k': 8.0,
     'cache_v': 8.0,
     'state_C': 3.294,
     'state_n': 3.922}
    for name, (base, spread) in spreads.items():
        noise = np.random.default_rng([zlib.crc32(name.encode()), seed]).standard_normal(out[name].shape)
        drawn = base * np.exp(spread * noise) if base else spread * noise
        out[name] = __import__('jax').numpy.asarray(drawn.astype(out[name].dtype))
    for name, factor in factors.items():
        out[name] = (out[name] * factor).astype(out[name].dtype)
    return out
```

```python
from contextlib import ExitStack

import concourse.bass as bass
from concourse import mybir

F32 = mybir.dt.float32
F32R = mybir.dt.float32r
BF16 = mybir.dt.bfloat16
ALU = mybir.AluOpType
ACT = mybir.ActivationFunctionType
AX = mybir.AxisListType
ds = bass.ds

P = 128
D = 1024
KT = D // P
SAMPLE = 2048
NS = SAMPLE // P
CTX = NS
NT = NS + 1
T = NT * P
PAST = 256
HD = 64
NKV = 4
NHEAD = 16
MH = 8
MHD = 128
EPS = 1e-6
BIG = 1.0e30

GROUPS = [(0, 4), (4, 8), (8, 11), (11, 14), (14, 17)]
NG = len(GROUPS)
KPAD = PAST
KLAT = KPAD + P
KREQ = KLAT + SAMPLE + P
KCOLS = KREQ + P
VT_LAT = KLAT // P
VT_REQ = KREQ // P
VTILES = KCOLS // P
VGROUPS = [(0, 8), (8, 16), (16, 17)]


class Env:
    pass


def pair_loop(eng, body):
    with eng.Fori(0, NS // 2) as i:
        for j in range(2):
            body(i * 2 + j, j, i, False)
    body(CTX, 0, NS // 2, True)


def over(n):
    return n + 3


def free(n):
    return n + 1


def settle(E, eng):
    eng.sem_inc(E.s_tick, 1)


class NormTranspose:

    def __init__(self, E, ctx, layer, src, src_ready):
        nc = E.nc
        self.E, self.layer, self.src, self.src_ready = E, layer, src, src_ready
        sb = lambda n, s, d=F32: ctx.enter_context(nc.sbuf_tensor(f"{n}{layer}", s, d))
        sem = lambda n: E.semaphore(f"{n}{layer}")
        self.xn = [sb(f"xn{j}_", [P, D]) for j in range(2)]
        self.htmp = [sb(f"htmp{j}_", [P, KT, P]) for j in range(2)]
        self.ss = sb("ss", [P, 2])
        self.std = sb("std", [P, 2])
        self.rs = sb("rs", [P, 2])
        self.s_sq = sem("sum_of_squares")
        self.s_std = sem("root_mean_square")
        self.s_rs = sem("rms_reciprocal")
        self.s_xn = sem("normalised")
        self.s_tp = sem("transposed")
        self.s_ha = sem("modulated_act")
        self.s_hd = sem("modulated_dve")
        self.s_hi = sem("hi_part")
        self.s_lo = sem("lo_part")
        self.bank = [E.bank[4:6], E.bank[6:8]]

    def credits_act(self, eng):
        for s in (self.s_sq, self.s_std, self.s_ha):
            eng.sem_inc(s, 2)

    def credits_dve(self, eng):
        for s in (self.s_rs, self.s_xn, self.s_hd, self.s_lo):
            eng.sem_inc(s, 2)

    def act_stats(self, eng, n, j):
        self.src_ready(eng, n, j)
        eng.wait_ge(self.s_tp, free(n))
        eng.activation(self.xn[j][:, :], self.src[j][:, :], ACT.Square,
                       accum_out=self.ss[:, j:j + 1]).then_inc(self.s_sq, 1)
        eng.wait_ge(self.s_sq, over(n))
        eng.wait_ge(self.s_rs, free(n))
        eng.activation(self.std[:, j:j + 1], self.ss[:, j:j + 1], ACT.Sqrt,
                       bias=self.E.eps[:, 0:1], scale=1.0 / D).then_inc(self.s_std, 1)

    def dve_normalise(self, eng, n, j):
        self.src_ready(eng, n, j)
        eng.wait_ge(self.s_std, over(n))
        eng.wait_ge(self.s_xn, free(n))
        eng.reciprocal(self.rs[:, j:j + 1], self.std[:, j:j + 1]).then_inc(self.s_rs, 1)
        eng.wait_ge(self.s_rs, over(n))
        eng.wait_ge(self.s_tp, free(n))
        eng.tensor_scalar(self.xn[j][:, :], self.src[j][:, :], self.rs[:, j:j + 1], None,
                          ALU.mult).then_inc(self.s_xn, 1)

    def pe_transpose(self, eng, n, j):
        eng.wait_ge(self.s_xn, over(n))
        eng.wait_ge(self.s_ha, free(n))
        eng.wait_ge(self.s_hd, free(n))
        for k in range(KT):
            out = self.bank[j][k // 4][:, (k % 4) * P:(k % 4 + 1) * P]
            last = eng.transpose(out, self.xn[j][:, k * P:(k + 1) * P], self.E.ident[:, :])
        last.then_inc(self.s_tp, 1)

    def act_modulate(self, eng, n, j, cond):
        E, l = self.E, self.layer
        eng.wait_ge(self.s_tp, over(n))
        eng.wait_ge(self.s_lo, free(n))
        for k in range(4):
            last = eng.activation(self.htmp[j][:, k, :], self.bank[j][0][:, k * P:(k + 1) * P],
                                  ACT.Identity, bias=E.hshift[:, l, cond, k:k + 1],
                                  scale=E.hscale[:, l, cond, k:k + 1])
        last.then_inc(self.s_ha, 1)

    def dve_modulate(self, eng, n, j, cond):
        E, l = self.E, self.layer
        eng.wait_ge(self.s_tp, over(n))
        for k in range(4, KT):
            last = eng.tensor_scalar(self.htmp[j][:, k, :], self.bank[j][1][:, (k - 4) * P:(k - 3) * P],
                                     E.hscale[:, l, cond, k:k + 1], E.hshift[:, l, cond, k:k + 1],
                                     ALU.mult, ALU.add)
        last.then_inc(self.s_hd, 1)

    def pool_hi(self, eng, n, j):
        eng.wait_ge(self.s_ha, over(n))
        eng.wait_ge(self.s_hd, over(n))
        settle(self.E, eng)
        eng.tensor_copy(self.E.h_hi[:, :, ds(n * P, P)], self.htmp[j][:, :, :]).then_inc(self.s_hi, 1)

    def dve_lo(self, eng, n, j):
        eng.wait_ge(self.s_hi, over(n))
        eng.tensor_tensor(self.E.h_lo[:, :, ds(n * P, P)], self.htmp[j][:, :, :],
                          self.E.h_hi[:, :, ds(n * P, P)], ALU.subtract).then_inc(self.s_lo, 1)


def phase_pre(E):
    nc = E.nc
    with ExitStack() as ctx:
        sb = lambda n, s, d=F32: ctx.enter_context(nc.sbuf_tensor(n, s, d))
        sem = lambda n: E.semaphore(n)
        s_const, s_cmask, s_cond, s_bias_zero, s_bias = (sem(x) for x in (
            "const_loaded", "bf16_masks", "cond_loaded", "bias_rows_zeroed", "bias_rows_loaded"))
        s_exp, s_silu, s_vec, s_vecs = (sem(x) for x in ("cond_exp", "cond_silu", "vec_turned", "vec_copied"))
        s_ck, s_ckt, s_ckc, s_cko = (sem(x) for x in ("ck_loaded", "ck_turned", "ck_copied", "ck_stored"))
        s_ada = [sem(f"ada_loaded{j}") for j in range(2)]
        s_adause, s_grow, s_gpe, s_mod, s_modpe = (sem(x) for x in (
            "ada_used", "gate_row_done", "gate_row_ready", "mod_vectors", "mod_products"))
        s_gst = sem("gate_rows_stored")
        s_x = [sem(f"x_loaded{j}") for j in range(2)]

        xb = [sb(f"xb{j}", [P, D]) for j in range(2)]
        ada = [sb(f"ada{j}", [P, KT, 512]) for j in range(2)]
        vecrows = sb("vecrows", [48, P])
        vecs = sb("vecs", [P, 48])
        cnd = sb("cnd", [P, 2, KT])
        cnd_e = sb("cnd_e", [P, 2, KT])
        silu_c = sb("silu_c", [P, KT, 2])
        silu_pad = sb("silu_pad", [P, KT, 33])
        grow = sb("grow", [33, D])
        gbias = sb("gbias", [33, D])
        ckr = sb("ckr", [P, 2, NKV, 2, HD])
        ckt = xb[0]

        def x_ready(eng, n, j):
            eng.wait_ge(s_x[j], (n - j) * 8 + 16)

        N = NormTranspose(E, ctx, 0, xb, x_ready)
        modps, vecps = E.bank[0], E.bank[1]
        gateps = [E.bank[2], E.bank[3]]

        with nc.Block() as block:
            @block.sync
            def _(sp):
                sp.dma_start(E.ident[:, :], E.a["ident"]).then_inc(s_const, 16)
                sp.dma_start(E.wmaskf[:, :, :], E.a["window_mask"]).then_inc(s_const, 16)
                with nc.allow_non_contiguous_dma(reason="short vectors"):
                    sp.dma_start(vecrows[0:8, :], E.a["attn_norm_w"].rearrange("a (k p) -> (a k) p", p=P)).then_inc(s_const, 16)
                    sp.dma_start(vecrows[8:24, :], E.a["attn_ada_b"][:, 0:2 * D].rearrange("a (k p) -> (a k) p", p=P)).then_inc(s_const, 16)
                    sp.dma_start(vecrows[24:32, :], E.a["mlstm_norm_w"].rearrange("a (k p) -> (a k) p", p=P)).then_inc(s_const, 16)
                    sp.dma_start(vecrows[32:48, :], E.a["mlstm_ada_b"][:, 0:2 * D].rearrange("a (k p) -> (a k) p", p=P)).then_inc(s_const, 16)
                    sp.dma_start(cnd[:, 0, :], E.a["c"].rearrange("a (p k) -> p (a k)", k=KT)).then_inc(s_cond, 16)
                    sp.dma_start(cnd[:, 1, :], E.a["c_ctx"].rearrange("(p k) -> p k", k=KT)).then_inc(s_cond, 16)
                for r in range(2):
                    for k in range(2):
                        sp.dma_start(ckr[:, k, :, r, :], E.a["cache_k"][0, 0, k * P:(k + 1) * P]).then_inc(s_ck, 16)
                for n in range(12):
                    layer, c = n // 6, n % 6
                    w = E.a["attn_ada_w"] if layer == 0 else E.a["mlstm_ada_w"]
                    if n >= 2:
                        sp.wait_ge(s_adause, n - 1)
                    sp.dma_start(ada[n % 2][:, :, :], w[0].rearrange("(p k) m -> p k m", k=KT)[:, :, c * 512:(c + 1) * 512]).then_inc(s_ada[n % 2], 16)
                    if n == 3:
                        sp.wait_ge(s_ckc, 1)
                        sp.dma_start(E.ckt_dram, ckt[:, :]).then_inc(s_cko, 16)
                    if c == 4:
                        if layer == 1:
                            sp.wait_ge(s_gst, 32)
                        sp.wait_ge(s_bias_zero, layer + 1)
                        b = E.a["attn_ada_b"] if layer == 0 else E.a["mlstm_ada_b"]
                        sp.dma_start(gbias[0:1, :], b[:, 2 * D:3 * D]).then_inc(s_bias, 16)
                        sp.dma_start(gbias[32:33, :], b[:, 2 * D:3 * D]).then_inc(s_bias, 16)
                    if c == 5 and layer == 0:
                        sp.wait_ge(s_grow, 2)
                        for r in range(2):
                            sp.dma_start(E.gates_dram[0, r:r + 1, :], grow[32 * r:32 * r + 1, :]).then_inc(s_gst, 16)
                    if n == 11:
                        sp.wait_ge(s_grow, 4)
                        for r in range(2):
                            sp.dma_start(E.gates_dram[1, r:r + 1, :], grow[32 * r:32 * r + 1, :]).then_inc(s_gst, 16)
                        sp.wait_ge(s_gst, 64)

            @block.gpsimd
            def _(pool):
                pool.sem_inc(N.s_hi, 2)
                pair_loop(pool, lambda n, j, i, last: N.pool_hi(pool, n, j))

            @block.scalar
            def _(act):
                N.credits_act(act)
                act.wait_ge(s_cond, 32)
                act.activation(cnd_e[:, :, :], cnd[:, :, :], ACT.Exp, scale=-1.0).then_inc(s_exp, 1)
                act.wait_ge(s_cko, 16)
                for j in range(2):
                    act.dma_start(xb[j][:, :], E.a["x_sample"][0, j * P:(j + 1) * P, :]).then_inc(s_x[j], 16)

                def tile(n, j, i, last):
                    N.act_stats(act, n, j)
                    if not last:
                        act.wait_ge(N.s_xn, over(n))
                        act.dma_start(xb[j][:, :], E.x_tile(n + 2)).then_inc(s_x[j], 16)
                    N.act_modulate(act, n, j, 1 if last else 0)

                act.wait_ge(s_mod, 1)
                with act.Fori(0, NS // 2 - 1) as i:
                    for j in range(2):
                        tile(i * 2 + j, j, i, False)
                N.act_stats(act, NS - 2, 0)
                act.wait_ge(N.s_xn, over(NS - 2))
                act.dma_start(xb[0][:, :], E.a["x_prompt"][0]).then_inc(s_x[0], 16)
                N.act_modulate(act, NS - 2, 0, 0)
                N.act_stats(act, NS - 1, 1)
                N.act_modulate(act, NS - 1, 1, 0)
                N.act_stats(act, CTX, 0)
                N.act_modulate(act, CTX, 0, 1)

            @block.vector
            def _(dve):
                N.credits_dve(dve)
                dve.memset(silu_pad[:, :, :], 0.0).then_inc(s_silu, 1)
                dve.memset(gbias[:, :], 0.0).then_inc(s_bias_zero, 2)
                dve.memset(E.one[:, :], 1.0)
                dve.memset(E.eps[:, :], EPS).then_inc(s_silu, 1)
                dve.wait_ge(s_const, 96)
                dve.tensor_copy(E.wmask[:, :, :], E.wmaskf[:, :, :]).then_inc(s_cmask, 1)
                dve.tensor_copy(E.identb[:, :], E.ident[:, :]).then_inc(s_cmask, 1)
                dve.wait_ge(s_exp, 1)
                dve.tensor_scalar(cnd_e[:, :, :], cnd_e[:, :, :], 1.0, None, ALU.add).then_inc(s_silu, 1)
                dve.wait_ge(s_silu, 3)
                dve.reciprocal(cnd_e[:, :, :], cnd_e[:, :, :]).then_inc(s_silu, 1)
                dve.wait_ge(s_silu, 4)
                dve.tensor_tensor(silu_c[:, :, :].rearrange("p k c -> p c k"), cnd[:, :, :], cnd_e[:, :, :], ALU.mult).then_inc(s_silu, 1)
                dve.wait_ge(s_silu, 5)
                for r in range(2):
                    dve.tensor_copy(silu_pad[:, :, 32 * r:32 * r + 1], silu_c[:, :, r:r + 1]).then_inc(s_silu, 1)
                dve.wait_ge(s_vec, 1)
                dve.tensor_copy(vecs[:, :], vecps[:, 0:48]).then_inc(s_vecs, 1)
                for h in range(2):
                    dve.wait_ge(s_ckt, h + 1)
                    v = ckt[:, :].rearrange("p (h t) -> p h t", h=NKV)[:, :, h * P:(h + 1) * P]
                    ins = dve.tensor_copy(v, E.bank[4 + h][:, :].rearrange("p (h t) -> p h t", h=NKV))
                ins.then_inc(s_ckc, 1)
                dve.wait_ge(s_vecs, 1)

                def mods(layer):
                    dve.wait_ge(s_modpe, layer + 1)
                    m = modps[:, layer * 32:layer * 32 + 32].rearrange("p (b c) -> p c b", c=2)
                    v0 = layer * 24
                    for c in range(2):
                        dve.tensor_tensor(E.hshift[:, layer, c, :], m[:, c, 0:8], vecs[:, v0 + 8:v0 + 16], ALU.add)
                        ins = dve.tensor_tensor(E.hscale[:, layer, c, :], m[:, c, 8:16], vecs[:, v0 + 16:v0 + 24], ALU.add)
                    ins.then_inc(s_vecs, 1)
                    dve.wait_ge(s_vecs, 2 + layer)
                    for c in range(2):
                        ins = dve.scalar_tensor_tensor(E.hscale[:, layer, c, :], E.hscale[:, layer, c, :], 1.0,
                                                       vecs[:, v0:v0 + 8], ALU.add, ALU.mult)
                    ins.then_inc(s_mod, 1)

                def gate_rows(layer):
                    for h in range(2):
                        dve.wait_ge(s_gpe, 2 * layer + h + 1)
                        if h == 0:
                            dve.wait_ge(s_bias, 32 * (layer + 1))
                            if layer == 1:
                                dve.wait_ge(s_gst, 32)
                        dve.tensor_tensor(grow[:, h * 512:(h + 1) * 512], gateps[h][0:33, :],
                                          gbias[:, h * 512:(h + 1) * 512], ALU.add).then_inc(s_grow, 1)

                mods(0)
                gate_rows(0)
                mods(1)
                gate_rows(1)
                dve.wait_ge(s_mod, 1)

                def tile(n, j, i, last):
                    N.dve_normalise(dve, n, j)
                    N.dve_modulate(dve, n, j, 1 if last else 0)
                    N.dve_lo(dve, n, j)
                pair_loop(dve, tile)

            @block.tensor
            def _(pe):
                pe.sem_inc(N.s_tp, 2)
                pe.wait_ge(s_const, 96)
                pe.transpose(vecps[:, 0:48], vecrows[:, :], E.ident[0:48, 0:48]).then_inc(s_vec, 1)
                pe.wait_ge(s_ck, 64)
                for t in range(2):
                    for h in range(NKV):
                        ins = pe.transpose(E.bank[4 + t][:, h * P:(h + 1) * P],
                                           ckr[:, t, h, :, :].rearrange("p r d -> p (r d)"), E.ident[:, :])
                    ins.then_inc(s_ckt, 1)
                pe.wait_ge(s_silu, 7)
                for n in range(12):
                    layer, c = n // 6, n % 6
                    pe.wait_ge(s_ada[n % 2], 16 * (n // 2 + 1))
                    w = ada[n % 2]
                    if c < 4:
                        for b in range(4):
                            col = layer * 32 + (c * 4 + b) * 2
                            for k in range(KT):
                                ins = pe.matmul(modps[:, col:col + 2], w[:, k, b * P:(b + 1) * P], silu_c[:, k, :],
                                                start=(k == 0), stop=(k == KT - 1))
                        ins.then_inc(s_adause, 1)
                        if c == 3:
                            pe.wait_ge(s_adause, n + 1)
                            pe.sem_inc(s_modpe, 1)
                    else:
                        if layer == 1:
                            pe.wait_ge(s_grow, 2)
                        for k in range(KT):
                            ins = pe.matmul(gateps[c - 4][0:33, :], silu_pad[:, k, :], w[:, k, :],
                                            start=(k == 0), stop=(k == KT - 1))
                        ins.then_inc(s_gpe, 1)
                        pe.wait_ge(s_gpe, 2 * layer + c - 3)
                        pe.sem_inc(s_adause, 1)
                pe.wait_ge(s_ckc, 1)
                pair_loop(pe, lambda n, j, i, last: N.pe_transpose(pe, n, j))


class Projection:

    def __init__(self, E, ctx, tag, blocks_per_iter):
        nc = E.nc
        self.E, self.B = E, blocks_per_iter
        sb = lambda n, s, d=F32: ctx.enter_context(nc.sbuf_tensor(f"{tag}_{n}", s, d))
        sem = lambda n: E.semaphore(f"{tag}_{n}")
        self.raw = sb("w_raw", [P, KT, P])
        self.hi = sb("w_hi", [P, KT, P], F32R)
        self.lo = sb("w_lo", [P, KT, P], F32R)
        self.s_raw = sem("w_loaded")
        self.s_hi = sem("w_hi_ready")
        self.s_lo = sem("w_lo_ready")
        self.s_used = sem("w_half_used")
        self.s_unit = sem("unit_done")

    def sp_load(self, sp, n, pieces):
        sp.wait_ge(self.s_lo, n * 2)
        settle(self.E, sp)
        for c0, src in pieces:
            w = src.shape[-1]
            sp.dma_start(self.raw[:, :, c0:c0 + w], src).then_inc(self.s_raw, 16)

    def pool_hi(self, pool, n, loads):
        pool.wait_ge(self.s_raw, loads * 16)
        for half in range(2):
            pool.wait_ge(self.s_used, n * 2 + half + 1)
            settle(self.E, pool)
            k = slice(4 * half, 4 * half + 4)
            pool.tensor_copy(self.hi[:, k, :], self.raw[:, k, :]).then_inc(self.s_hi, 1)

    def dve_lo(self, dve, n):
        for half in range(2):
            dve.wait_ge(self.s_hi, n * 2 + half + 1)
            k = slice(4 * half, 4 * half + 4)
            dve.tensor_tensor(self.lo[:, k, :], self.raw[:, k, :], self.hi[:, k, :],
                              ALU.subtract).then_inc(self.s_lo, 1)

    def pe_unit(self, pe, n, g, bank):
        E = self.E
        t0, t1 = GROUPS[g]
        tok = slice(t0 * P, t1 * P)
        out = bank[:, 0:(t1 - t0) * P]
        for k in range(KT):
            if g == 0 and k % 4 == 0:
                pe.wait_ge(self.s_lo, n * 2 + k // 4 + 1)
            pe.matmul(out, self.lo[:, k, :], E.h_hi[:, k, tok], start=(k == 0), stop=False)
            pe.matmul(out, self.hi[:, k, :], E.h_lo[:, k, tok], start=False, stop=False)
            ins = pe.matmul(out, self.hi[:, k, :], E.h_hi[:, k, tok], start=False, stop=(k == KT - 1))
            if g == NG - 1 and k == 3:
                ins.then_inc(self.s_used, 1)
        ins.then_inc(self.s_unit, 1)
        if g == NG - 1:
            pe.wait_ge(self.s_unit, n * NG + g + 1)
            pe.sem_inc(self.s_used, 1)


def phase_attn(E):
    nc = E.nc
    SWAP = [(p + 16) % 32 for p in range(32)]
    with ExitStack() as ctx:
        sb = lambda n, s, d=F32: ctx.enter_context(nc.sbuf_tensor(n, s, d))
        sem = lambda n: E.semaphore(n)
        kT = sb("kT", [P, KCOLS])
        vS = sb("vS", [P, VTILES, HD])
        qT = sb("qT", [P, T])
        gT = sb("gT", [P, T])
        cs = [sb(f"cs{b}", [P, 2, 512]) for b in range(2)]
        shuf = [sb(f"shuf{b}", [P, 512]) for b in range(2)]
        gexp = [sb(f"gexp{b}", [P, 512]) for b in range(2)]
        prob = [sb(f"prob{b}", [P, 640]) for b in range(2)]
        probT = [sb(f"probT{b}", [P, 640]) for b in range(2)]
        o_sb = [sb(f"o_sb{b}", [P, P]) for b in range(2)]
        sink = sb("sink", [P, NHEAD])
        nsink = sb("nsink", [P, NHEAD])
        mx = sb("mx", [P, 2])
        negm = sb("negm", [P, 2, 2])
        rsum = sb("rsum", [P, 2, 2])
        sarg = sb("sarg", [P, 2, 2])
        esink = sb("esink", [P, 2, 2])
        den = sb("den", [P, 2, 2])
        rden = sb("rden", [P, 2, 2])
        kvout = sb("kvout", [P, 2, HD])

        J = Projection(E, ctx, "attn", 5)
        s_cs = [sem(f"rotary_loaded{b}") for b in range(2)]
        (s_shuf, s_cos, s_rope, s_gexp, s_gden, s_release, s_kdup, s_vT, s_vS, s_kvo, s_kvst, s_ckl, s_cvl,
         s_const, s_pad, s_sin) = (sem(x) for x in (
            "shuffled", "times_cos", "rotated", "gate_exp", "gate_denominator", "proj_bank_free", "k_doubled",
            "v_turned", "v_stored", "kv_out_ready", "kv_out_stored", "cached_k_loaded", "cached_v_loaded",
            "sink_loaded", "pads_zero", "times_sin"))
        s_pTc2 = sem("probsT_last_ready")
        (s_S, s_mx, s_nm, s_p, s_pT, s_pTc, s_pv, s_sarg, s_es, s_den, s_rd, s_on, s_oT, s_og, s_ogst) = (
            sem(x) for x in ("scores", "row_max", "neg_max", "probs", "probs_turned", "probsT_ready", "pv_done",
                             "sink_minus_max", "sink_exp", "denominator", "recip_den", "o_normalised", "o_turned",
                             "o_gated", "o_stored"))
        w_in = E.a["attn_w_in"][0].rearrange("(k p) m -> p k m", p=P)

        NU = 2 * NT
        kinds = ["kv", "q", "g", "q", "g"]
        ROPES = 3 * NG

        def lat_ctx(g):
            t0, t1 = GROUPS[g]
            lat = min(t1, NS) - t0
            return t0 * P, lat * P, (t1 - t0) * P - lat * P

        with nc.Block() as block:
            @block.sync
            def _(sp):
                sp.dma_start(sink[:, :], E.a["attn_sink"].partition_broadcast(P)).then_inc(s_const, 16)
                with sp.Fori(0, NKV) as kv:
                    rope = 0

                    def load_weights(m):
                        if kinds[m] == "kv":
                            pieces = [(0, w_in[:, :, ds(kv * HD + 2 * D, HD)]),
                                      (HD, w_in[:, :, ds(kv * HD + 2 * D + NKV * HD, HD)])]
                        else:
                            col = (0 if kinds[m] == "q" else D) + (m - 1) // 2 * P
                            pieces = [(0, w_in[:, :, ds(kv * (2 * P) + col, P)])]
                        J.sp_load(sp, kv * 5 + m, pieces)

                    load_weights(0)
                    for m, kind in enumerate(kinds):
                        if m < 4:
                            load_weights(m + 1)
                        if kind == "kv":
                            sp.wait_ge(s_S, kv * (2 * NU))
                            settle(E, sp)
                            with nc.allow_non_contiguous_dma(reason="rows of one head"):
                                sp.dma_start(kT[:, 0:PAST], E.ckt_dram[:, ds(kv * PAST, PAST)]).then_inc(s_ckl, 16)
                                sp.wait_ge(s_pv, kv * (2 * NU))
                                settle(E, sp)
                                sp.dma_start(vS[:, 0:2, :], E.cache_v[:, :, ds(kv * HD, HD)]).then_inc(s_cvl, 16)
                        if kind != "g":
                            for g in range(NG):
                                t0, wl, wc = lat_ctx(g)
                                b = rope % 2
                                if rope >= 2:
                                    sp.wait_ge(s_rope, kv * ROPES + rope - 1)
                                else:
                                    sp.wait_ge(s_rope, kv * ROPES)
                                sp.dma_start(cs[b][:, :, 0:wl], E.a["rotary"][:, :, t0:t0 + wl]).then_inc(s_cs[b], 16)
                                rope += 1
                        if kind == "kv":
                            sp.wait_ge(s_kvo, kv * 2 + 2)
                            settle(E, sp)
                            with nc.allow_non_contiguous_dma(reason="rows of one head"):
                                sp.dma_start(E.new_k[:, ds(kv * HD, HD)], kvout[:, 0, :]).then_inc(s_kvst, 16)
                                sp.dma_start(E.new_v[:, ds(kv * HD, HD)], kvout[:, 1, :]).then_inc(s_kvst, 16)
                        if kind == "g":
                            sub = m // 2 - 1
                            sp.wait_ge(s_og, kv * (2 * NT) + (sub + 1) * NT)
                            sp.dma_start(E.ogT_dram[ds(kv * 2 + sub, 1), :, :].rearrange("a p t -> (a p) t"), gT[:, :]).then_inc(s_ogst, 16)
                sp.wait_ge(s_ogst, 16 * 2 * NKV)
                sp.wait_ge(s_kvst, 32 * NKV)

            @block.gpsimd
            def _(pool):
                pool.memset(kT[:, KPAD:KPAD + P], 0.0).then_inc(s_pad, 1)
                pool.memset(kT[:, KREQ - P:KREQ], 0.0).then_inc(s_pad, 1)
                pool.memset(vS[:, KPAD // P, :], 0.0).then_inc(s_pad, 1)
                pool.memset(vS[:, KREQ // P - 1, :], 0.0).then_inc(s_pad, 1)
                with pool.Fori(0, NKV) as kv:
                    rope = 0
                    J.pool_hi(pool, kv * 5, kv * 6 + 2)
                    for m, kind in enumerate(kinds):
                        if kind == "g":
                            if m < 4:
                                J.pool_hi(pool, kv * 5 + m + 1, kv * 6 + m + 3)
                            continue
                        rows, dst, off = (HD, kT, KLAT) if kind == "kv" else (P, qT, 0)
                        for g in range(NG):
                            t0, wl, wc = lat_ctx(g)
                            b = rope % 2
                            if g == NG - 1:
                                J.pool_hi(pool, kv * 5 + m + 1, kv * 6 + m + 3)
                            pool.wait_ge(s_shuf, kv * ROPES + rope + 1)
                            pool.wait_ge(s_cos, kv * ROPES + rope + 1)
                            prod = pool.tensor_tensor(shuf[b][0:rows, 0:wl], shuf[b][0:rows, 0:wl],
                                                      cs[b][0:rows, 1, 0:wl], ALU.mult)
                            prod.then_inc(s_sin, 1)
                            pool.wait_ge(s_sin, kv * ROPES + rope + 1)
                            o = dst[0:rows, off + t0:off + t0 + wl]
                            pool.tensor_tensor(o, o, shuf[b][0:rows, 0:wl], ALU.add).then_inc(s_rope, 1)
                            rope += 1

            @block.scalar
            def _(act):
                act.wait_ge(s_const, 16)
                act.mul(nsink[:, :], sink[:, :], -1.0).then_inc(s_const, 1)
                with act.Fori(0, NKV) as kv:
                    for g in range(NG):
                        t0, wl, wc = lat_ctx(g)
                        act.wait_ge(s_rope, kv * ROPES + g + 1)
                        if wc:
                            act.wait_ge(s_release, kv * (5 * NG) + NG)
                        ins = act.copy(kT[HD:P, KLAT + t0:KLAT + t0 + wl], kT[0:HD, KLAT + t0:KLAT + t0 + wl])
                        if wc:
                            act.copy(kT[HD:P, KREQ:KREQ + P], kT[0:HD, KREQ:KREQ + P]).then_inc(s_kdup, 1)
                        else:
                            ins.then_inc(s_kdup, 1)
                    act.wait_ge(s_pv, kv * (2 * NU))
                    for r, (a, z) in enumerate(VGROUPS):
                        act.wait_ge(s_vT, kv * 4 + r + 1)
                        n_lat = min(z, NS) - a
                        src = E.bank[4 + r][:, 0:(z - a) * HD].rearrange("p (t d) -> p t d", d=HD)
                        if n_lat:
                            ins = act.copy(vS[:, VT_LAT + a:VT_LAT + a + n_lat, :], src[:, 0:n_lat, :])
                        if z > NS:
                            ins = act.copy(vS[:, VT_REQ, :], src[:, CTX - a, :])
                        ins.then_inc(s_vS, 1)
                    act.wait_ge(s_kvst, kv * 32)
                    act.wait_ge(s_vT, kv * 4 + 4)
                    act.copy(kvout[:, 0, :], E.bank[7][:, 0:HD]).then_inc(s_kvo, 1)
                    act.copy(kvout[:, 1, :], E.bank[6][:, 0:HD]).then_inc(s_kvo, 1)
                    for sub in range(2):
                        for g in range(NG):
                            t0, t1 = GROUPS[g]
                            w = (t1 - t0) * P
                            u = NG * (2 + 2 * sub) + g
                            e = (sub * NG + g) % 2
                            act.wait_ge(J.s_unit, kv * (5 * NG) + u + 1)
                            act.wait_ge(s_release, kv * (5 * NG) + u - 1)
                            act.activation(gexp[e][:, 0:w], E.bank[u % 4][:, 0:w], ACT.Exp, scale=-1.0).then_inc(s_gexp, 1)
                        base = kv * (2 * NU) + sub * NU
                        bbase = kv * (2 * NT) + sub * NT

                        def sink_exp(b):
                            act.wait_ge(s_sarg, bbase + b + 1)
                            act.activation(esink[:, b % 2, :], sarg[:, b % 2, :], ACT.Exp).then_inc(s_es, 1)

                        def pT_copy(w):
                            act.wait_ge(s_pT, base + w + 1)
                            act.wait_ge(s_pv, base + (w - 1 if w >= 2 else 0))
                            act.copy(probT[w % 2][:, 512:640], E.bank[5][:, 0:P]).then_inc(s_pTc2, 1)

                        for w in range(NU + 1):
                            if w < NU:
                                b, hh = w // 2, w % 2
                                act.wait_ge(s_nm, base + w + 1)
                                act.wait_ge(s_pT, base + (w - 1 if w >= 2 else 0))
                                act.wait_ge(s_den, bbase + (b - 1 if b >= 2 else 0))
                                s0, s1 = E.bank[2 * (w % 2)], E.bank[2 * (w % 2) + 1]
                                acc = rsum[:, b % 2, hh:hh + 1]
                                if b < CTX:
                                    act.activation(prob[w % 2][:, :].rearrange("p (a n) -> p a n", a=2),
                                                   E.s_pair(w % 2), ACT.Exp, bias=negm[:, b % 2, hh:hh + 1],
                                                   scale=HD ** -0.5, accum_out=acc).then_inc(s_p, 1)
                                else:
                                    act.activation(prob[w % 2][:, 0:P], s0[:, 0:P], ACT.Exp,
                                                   bias=negm[:, b % 2, hh:hh + 1], scale=HD ** -0.5,
                                                   accum_out=acc).then_inc(s_p, 1)
                                if hh == 1:
                                    sink_exp(b)
                            if w >= 1:
                                pT_copy(w - 1)

            @block.vector
            def _(dve):
                dve.wait_ge(s_const, 17)

                def rope_unit(kv, rope, u, rows, dst, off, req, g):
                    t0, wl, wc = lat_ctx(g)
                    b = rope % 2
                    bank = E.bank[u % 4]
                    dve.wait_ge(J.s_unit, kv * (5 * NG) + u + 1)
                    dve.wait_ge(s_rope, kv * ROPES + (rope - 1 if rope >= 2 else 0))
                    settle(E, dve)
                    dve.stream_shuffle(shuf[b][0:rows, 0:wl], bank[0:rows, 0:wl], SWAP).then_inc(s_shuf, 1)
                    dve.wait_ge(s_cs[b], kv * (16 * (8 - b)) + 16 * (rope // 2 + 1))
                    ins = dve.tensor_tensor(dst[0:rows, off + t0:off + t0 + wl], bank[0:rows, 0:wl],
                                            cs[b][0:rows, 0, 0:wl], ALU.mult)
                    ins.then_inc(s_cos, 1)
                    if wc:
                        ins = dve.tensor_copy(dst[0:rows, req:req + P], bank[0:rows, wl:wl + P])
                    return ins

                with dve.Fori(0, NKV) as kv:
                    J.dve_lo(dve, kv * 5)
                    rope = 0
                    for m, kind in enumerate(kinds):
                        for g in range(NG):
                            u = NG * m + g
                            t0, t1 = GROUPS[g]
                            w = (t1 - t0) * P
                            tok = slice(t0 * P, t1 * P)
                            if g == NG - 1 and m < 4:
                                J.dve_lo(dve, kv * 5 + m + 1)
                            if kind == "kv":
                                if g == 0:
                                    dve.wait_ge(s_ogst, kv * 32)
                                    dve.wait_ge(s_S, kv * (2 * NU))
                                rope_unit(kv, rope, u, HD, kT, KLAT, KREQ, g)
                                dve.tensor_copy(gT[HD:P, tok], E.bank[u % 4][HD:P, 0:w]).then_inc(s_release, 1)
                                rope += 1
                            elif kind == "q":
                                if g == 0 and m == 3:
                                    dve.wait_ge(s_S, kv * (2 * NU) + NU)
                                ins = rope_unit(kv, rope, u, P, qT, 0, CTX * P, g)
                                if lat_ctx(g)[2]:
                                    ins.then_inc(s_release, 1)
                                else:
                                    dve.wait_ge(s_cos, kv * ROPES + rope + 1)
                                    dve.sem_inc(s_release, 1)
                                rope += 1
                            else:
                                e = ((m // 2 - 1) * NG + g) % 2
                                if g == 0 and m == 2:
                                    dve.wait_ge(s_vT, kv * 4 + 4)
                                if g == 0 and m == 4:
                                    dve.wait_ge(s_ogst, kv * 32 + 16)
                                k = kv * (2 * NG) + (m // 2 - 1) * NG + g
                                dve.wait_ge(s_gexp, k + 1)
                                dve.tensor_scalar(gexp[e][:, 0:w], gexp[e][:, 0:w], 1.0, None, ALU.add).then_inc(s_gden, 1)
                                dve.wait_ge(s_gden, 2 * k + 1)
                                dve.reciprocal(gexp[e][:, 0:w], gexp[e][:, 0:w]).then_inc(s_gden, 1)
                                dve.wait_ge(s_gden, 2 * k + 2)
                                dve.tensor_tensor(gT[:, tok], E.bank[u % 4][:, 0:w], gexp[e][:, 0:w], ALU.mult).then_inc(s_release, 1)
                        if m not in (2, 4):
                            continue
                        sub = m // 2 - 1
                        base = kv * (2 * NU) + sub * NU
                        bbase = kv * (2 * NT) + sub * NT

                        def softmax_max(w):
                            b, hh = w // 2, w % 2
                            head = kv * 4 + (2 * sub + hh)
                            dve.wait_ge(s_S, base + w + 1)
                            src = E.s_pair(w % 2) if b < CTX else E.bank[2 * (w % 2)][:, 0:P]
                            dve.tensor_reduce(mx[:, w % 2:w % 2 + 1], src, AX.XY if b < CTX else AX.X, ALU.max).then_inc(s_mx, 1)
                            dve.wait_ge(s_mx, base + w + 1)
                            dve.wait_ge(s_p, base + (2 * b - 2 if b >= 2 else 0))
                            dve.wait_ge(s_sarg, bbase + (b - 1 if b >= 2 else 0))
                            dve.tensor_scalar(negm[:, b % 2, hh:hh + 1], mx[:, w % 2:w % 2 + 1], -(HD ** -0.5),
                                              nsink[:, ds(head, 1)], ALU.mult, ALU.min).then_inc(s_nm, 1)
                            if hh == 1:
                                dve.wait_ge(s_nm, base + w + 1)
                                dve.wait_ge(s_es, bbase + (b - 1 if b >= 2 else 0))
                                dve.tensor_tensor(sarg[:, b % 2, :], negm[:, b % 2, :],
                                                  sink[:, ds(kv * 4 + 2 * sub, 2)], ALU.add).then_inc(s_sarg, 1)

                        def pT_copy(w):
                            dve.wait_ge(s_pT, base + w + 1)
                            dve.wait_ge(s_pv, base + (w - 1 if w >= 2 else 0))
                            n = 4 if w // 2 < CTX else 1
                            dve.tensor_copy(probT[w % 2][:, 0:n * P], E.bank[4][:, 0:n * P]).then_inc(s_pTc, 1)

                        def finish(b):
                            p = b % 2
                            dve.wait_ge(s_p, base + 2 * b + 2)
                            dve.wait_ge(s_es, bbase + b + 1)
                            dve.tensor_tensor(den[:, p, :], rsum[:, p, :], esink[:, p, :], ALU.add).then_inc(s_den, 1)
                            dve.wait_ge(s_den, bbase + b + 1)
                            dve.reciprocal(rden[:, p, :], den[:, p, :]).then_inc(s_rd, 1)
                            dve.wait_ge(s_rd, bbase + b + 1)
                            dve.wait_ge(s_pv, base + 2 * b + 2)
                            dve.wait_ge(s_oT, bbase + (b - 1 if b >= 2 else 0))
                            dve.tensor_tensor(o_sb[p][:, :].rearrange("q (h d) -> q h d", h=2),
                                              E.bank[6][:, p * P:(p + 1) * P].rearrange("q (h d) -> q h d", h=2),
                                              rden[:, p, :].unsqueeze(2).to_broadcast([P, 2, HD]), ALU.mult).then_inc(s_on, 1)

                        def gate(b):
                            dve.wait_ge(s_oT, bbase + b + 1)
                            g = gT[:, b * P:(b + 1) * P]
                            dve.tensor_tensor(g, E.bank[7][:, 0:P], g, ALU.mult).then_inc(s_og, 1)

                        for s in range(NU + 6):
                            if s < NU:
                                softmax_max(s)
                            if 1 <= s <= NU:
                                pT_copy(s - 1)
                            if s >= 3 and s % 2 == 1 and (s - 3) // 2 < NT:
                                finish((s - 3) // 2)
                            if s >= 5 and s % 2 == 1 and (s - 5) // 2 < NT:
                                gate((s - 5) // 2)

            @block.tensor
            def _(pe):
                pe.sem_inc(J.s_used, 2)
                pe.wait_ge(s_pad, 4)
                with pe.Fori(0, NKV) as kv:
                    for m, kind in enumerate(kinds):
                        for g in range(NG):
                            u = NG * m + g
                            if u >= 4:
                                pe.wait_ge(s_release, kv * (5 * NG) + u - 3)
                            if u < 4 and m == 0:
                                pe.wait_ge(s_p, kv * (2 * NU))
                            if m == 3:
                                pe.wait_ge(s_p, kv * (2 * NU) + NU)
                            J.pe_unit(pe, kv * 5 + m, g, E.bank[u % 4])
                        if kind == "kv":
                            pe.wait_ge(s_release, kv * (5 * NG) + NG)
                            pe.wait_ge(s_og, kv * (2 * NT))
                            pe.wait_ge(s_pTc, kv * (2 * NU))
                            pe.wait_ge(s_pTc2, kv * (2 * NU))
                            settle(E, pe)
                            for r, (a, z) in enumerate(VGROUPS):
                                for t in range(a, z):
                                    ins = pe.transpose(E.bank[4 + r][:, (t - a) * HD:(t - a + 1) * HD],
                                                       gT[HD:P, t * P:(t + 1) * P], E.ident[HD:P, HD:P])
                                ins.then_inc(s_vT, 1)
                            pe.wait_ge(s_kdup, kv * NG + NG)
                            pe.transpose(E.bank[7][:, 0:P], kT[:, KREQ:KREQ + P], E.ident[:, :]).then_inc(s_vT, 1)
                        if m not in (2, 4):
                            continue
                        sub = m // 2 - 1
                        base = kv * (2 * NU) + sub * NU
                        bbase = kv * (2 * NT) + sub * NT
                        pe.wait_ge(s_rope, kv * ROPES + NG * (2 + sub))
                        pe.wait_ge(s_release, kv * (5 * NG) + NG * (m + 1))
                        if sub == 0:
                            pe.wait_ge(s_kdup, kv * NG + NG)
                            pe.wait_ge(s_vS, kv * 3 + 3)
                            pe.wait_ge(s_kvo, kv * 2 + 2)
                            pe.wait_ge(s_ckl, kv * 16 + 16)
                            pe.wait_ge(s_cvl, kv * 16 + 16)

                        def scores(w):
                            b, hh = w // 2, w % 2
                            if w >= 2:
                                pe.wait_ge(s_p, base + w - 1)
                            r = slice(HD * hh, HD * hh + HD)
                            q = qT[r, b * P:(b + 1) * P]
                            s0, s1 = E.bank[2 * (w % 2)], E.bank[2 * (w % 2) + 1]
                            mm = lambda out, k0, n, start: pe.matmul(out, q, kT[r, k0:k0 + n], start=start, stop=True,
                                                                     skip_group_check=True)
                            if b == CTX:
                                mm(s0[:, 0:P], KREQ, P, True).then_inc(s_S, 1)
                                return
                            mask = 0 if b == 0 else 2 if b == NS - 1 else 1
                            mm(s0[:, 0:P], KLAT + (b - 1) * P, P, True)
                            mm(s0[:, P:2 * P], KLAT + (b + 1) * P, P, False)
                            mm(s0[:, 256:320], 0, 64, False)
                            pe.matmul(s0[:, 0:2 * P], E.identb[:, :], E.wmask[:, mask, :], start=False, stop=True,
                                      skip_group_check=True)
                            mm(s1[:, 0:192], 64, 192, True)
                            mm(s1[:, 192:320], KLAT + b * P, P, False).then_inc(s_S, 1)

                        def turn(w):
                            b = w // 2
                            pe.wait_ge(s_p, base + w + 1)
                            if w >= 1:
                                pe.wait_ge(s_pTc, base + w)
                                pe.wait_ge(s_pTc2, base + w)
                            for t in range(5 if b < CTX else 1):
                                out = E.bank[4][:, t * P:(t + 1) * P] if t < 4 else E.bank[5][:, 0:P]
                                ins = pe.transpose(out, prob[w % 2][:, t * P:(t + 1) * P], E.ident[:, :])
                            ins.then_inc(s_pT, 1)

                        def pv(w):
                            b, hh = w // 2, w % 2
                            pe.wait_ge(s_pTc, base + w + 1)
                            pe.wait_ge(s_pTc2, base + w + 1)
                            pe.wait_ge(s_on, bbase + b)
                            out = E.bank[6][:, (b % 2) * P + hh * HD:(b % 2) * P + (hh + 1) * HD]
                            tiles = [VT_LAT + b - 1, VT_LAT + b + 1, 0, 1, VT_LAT + b] if b < CTX else [VT_REQ]
                            for t, v in enumerate(tiles):
                                ins = pe.matmul(out, probT[w % 2][:, t * P:(t + 1) * P], vS[:, v, :],
                                                start=(t == 0), stop=(t == len(tiles) - 1), skip_group_check=True)
                            ins.then_inc(s_pv, 1)

                        def turn_o(b):
                            pe.wait_ge(s_on, bbase + b + 1)
                            if b >= 1:
                                pe.wait_ge(s_og, bbase + b)
                            pe.transpose(E.bank[7][:, 0:P], o_sb[b % 2][:, :], E.ident[:, :]).then_inc(s_oT, 1)

                        for s in range(NU + 5):
                            if s < NU:
                                scores(s)
                            if 1 <= s <= NU:
                                turn(s - 1)
                            if 2 <= s <= NU + 1:
                                pv(s - 2)
                            if s >= 4 and s % 2 == 0 and (s - 4) // 2 < NT:
                                turn_o((s - 4) // 2)


def phase_out(E, layer):
    nc = E.nc
    last_layer = layer == 1
    with ExitStack() as ctx:
        sb = lambda n, s, d=F32: ctx.enter_context(nc.sbuf_tensor(f"{n}_out{layer}", s, d))
        sem = lambda n: E.semaphore(f"{n}_out{layer}")
        w = sb("w", [P, KT, D])
        og = [sb(f"og{j}", [P, KT, P]) for j in range(2)]
        xb = [sb(f"xb{j}", [P, D]) for j in range(2)]
        scaled = sb("scaled", [P, D])
        gbc = sb("gbc", [P, D])
        s_w, s_g, s_y, s_t, s_x1 = (sem(x) for x in (
            "w_loaded", "gate_loaded", "y_done", "y_gated", "residual_added"))
        s_og = [sem(f"og_loaded{j}") for j in range(2)]
        s_x = [sem(f"x_loaded{j}") for j in range(2)]
        s_st = [sem(f"stored{j}") for j in range(2)]
        if last_layer:
            w_hi, w_lo = sb("w_hi", [P, KT, D], F32R), sb("w_lo", [P, KT, D], F32R)
            og_hi = [sb(f"og_hi{j}", [P, KT, P], F32R) for j in range(2)]
            og_lo = [sb(f"og_lo{j}", [P, KT, P], F32R) for j in range(2)]
            fw = sb("fw", [P, D])
            y = [sb(f"y{j}", [P, D]) for j in range(2)]
            ss, std, rs = sb("ss", [P, 2]), sb("std", [P, 2]), sb("rs", [P, 2])
            s_whi, s_wlo, s_oghi, s_oglo, s_sq, s_std, s_rs, s_xn, s_junk = (sem(x) for x in (
                "w_hi_ready", "w_lo_ready", "og_hi_ready", "og_lo_ready", "sum_of_squares",
                "root_mean_square", "rms_reciprocal", "normalised", "junk"))
            x_read = s_xn

        def residual_ready(eng, n, j):
            eng.wait_ge(s_x1, over(n))

        if not last_layer:
            N = NormTranspose(E, ctx, 1, xb, residual_ready)
            x_read = N.s_xn
        ybank = [E.PS[:, 0:2, :], E.PS[:, 2:4, :]]
        w_out = (E.a["mlstm_w_out"] if last_layer else E.a["attn_w_out"])[0]

        with nc.Block() as block:
            @block.sync
            def _(sp):
                sp.dma_start(w[:, :, :], w_out.rearrange("(k p) m -> p k m", p=P)).then_inc(s_w, 16)
                sp.dma_start(gbc[:, :], E.gates_dram[layer, 0:1, :].partition_broadcast(P)).then_inc(s_g, 16)
                if last_layer:
                    sp.dma_start(fw[:, :], E.a["final_norm_w"].rearrange("(a n) -> a n", a=1).partition_broadcast(P)).then_inc(s_w, 16)

                def tile(n, j, i, last):
                    sp.wait_ge(s_oglo if last_layer else s_y, free(n))
                    settle(E, sp)
                    with nc.allow_non_contiguous_dma(reason="512-byte rows"):
                        sp.dma_start(og[j][:, :, :], E.ogT_dram[:, :, ds(n * P, P)].rearrange("k p t -> p k t")).then_inc(s_og[j], 16)
                    sp.wait_ge(x_read, free(n))
                    settle(E, sp)
                    sp.wait_ge(s_st[j], i * 16)
                    settle(E, sp)
                    if last_layer:
                        src = E.x1_dram[ds(n * P, P), :]
                    else:
                        src = E.a["x_prompt"][0] if last else E.x_tile(n)
                    sp.dma_start(xb[j][:, :], src).then_inc(s_x[j], 16)
                    if last:
                        sp.wait_ge(s_t, over(NS - 1))
                        sp.dma_start(gbc[:, :], E.gates_dram[layer, 1:2, :].partition_broadcast(P)).then_inc(s_g, 16)
                pair_loop(sp, tile)
                sp.wait_ge(s_st[0], 16 * (NS // 2 + 1))
                sp.wait_ge(s_st[1], 16 * (NS // 2))

            @block.gpsimd
            def _(pool):
                pool.sem_inc(s_x1, 2)
                if last_layer:
                    pool.sem_inc(s_oghi, 2)
                    pool.wait_ge(s_w, 32)
                    for k in range(KT):
                        pool.tensor_copy(w_hi[:, k, :], w[:, k, :]).then_inc(s_whi, 1)
                else:
                    pool.sem_inc(N.s_hi, 2)

                def tile(n, j, i, last):
                    if last_layer:
                        pool.wait_ge(s_og[j], i * 16 + 16)
                        pool.wait_ge(s_y, free(n))
                        settle(E, pool)
                        pool.tensor_copy(og_hi[j][:, :, :], og[j][:, :, :]).then_inc(s_oghi, 1)
                    pool.wait_ge(s_t, over(n))
                    pool.wait_ge(s_x[j], i * 16 + 16)
                    pool.tensor_tensor(xb[j][:, :], xb[j][:, :], scaled[:, :], ALU.add).then_inc(s_x1, 1)
                    if not last_layer:
                        N.pool_hi(pool, n, j)
                pair_loop(pool, tile)

            @block.scalar
            def _(act):
                if last_layer:
                    act.sem_inc(s_sq, 2)
                    act.sem_inc(s_std, 2)
                else:
                    N.credits_act(act)

                def tile(n, j, i, last):
                    residual_ready(act, n, j)
                    if not last_layer:
                        act.dma_start(E.x1_dram[ds(n * P, P), :], xb[j][:, :]).then_inc(s_st[j], 16)
                        N.act_stats(act, n, j)
                        N.act_modulate(act, n, j, 1 if last else 0)
                        return
                    act.wait_ge(s_xn, free(n))
                    act.wait_ge(s_st[j], i * 16)
                    act.activation(y[j][:, :], xb[j][:, :], ACT.Square, accum_out=ss[:, j:j + 1]).then_inc(s_sq, 1)
                    act.wait_ge(s_sq, over(n))
                    act.wait_ge(s_rs, free(n))
                    act.activation(std[:, j:j + 1], ss[:, j:j + 1], ACT.Sqrt, bias=E.eps[:, 0:1],
                                   scale=1.0 / D).then_inc(s_std, 1)
                    act.wait_ge(s_xn, over(n))
                    act.dma_start(E.out_prompt if last else E.out_sample[ds(n * P, P), :], y[j][:, :]).then_inc(s_st[j], 16)
                pair_loop(act, tile)

            @block.vector
            def _(dve):
                dve.sem_inc(s_t, 2)
                if last_layer:
                    for s in (s_oglo, s_rs, s_xn):
                        dve.sem_inc(s, 2)
                    for k in range(KT):
                        dve.wait_ge(s_whi, k + 1)
                        dve.tensor_tensor(w_lo[:, k, :], w[:, k, :], w_hi[:, k, :], ALU.subtract).then_inc(s_wlo, 1)
                else:
                    N.credits_dve(dve)

                def tile(n, j, i, last):
                    if last_layer:
                        dve.wait_ge(s_oghi, over(n))
                        dve.tensor_tensor(og_lo[j][:, :, :], og[j][:, :, :], og_hi[j][:, :, :], ALU.subtract).then_inc(s_oglo, 1)
                    dve.wait_ge(s_y, over(n))
                    dve.wait_ge(s_g, 32 if last else 16)
                    dve.wait_ge(s_x1, free(n + 1))
                    dve.tensor_tensor(scaled[:, :].rearrange("p (a n) -> p a n", a=2), ybank[j],
                                      gbc[:, :].rearrange("p (a n) -> p a n", a=2), ALU.mult).then_inc(s_t, 1)
                    if not last_layer:
                        N.dve_normalise(dve, n, j)
                        N.dve_modulate(dve, n, j, 1 if last else 0)
                        N.dve_lo(dve, n, j)
                        return
                    dve.wait_ge(s_std, over(n))
                    dve.wait_ge(s_xn, free(n))
                    dve.reciprocal(rs[:, j:j + 1], std[:, j:j + 1]).then_inc(s_rs, 1)
                    dve.wait_ge(s_rs, over(n))
                    dve.wait_ge(s_sq, over(n))
                    dve.scalar_tensor_tensor(y[j][:, :], xb[j][:, :], rs[:, j:j + 1], fw[:, :],
                                             ALU.mult, ALU.mult).then_inc(s_xn, 1)
                pair_loop(dve, tile)

            @block.tensor
            def _(pe):
                pe.sem_inc(s_y, 2)
                if not last_layer:
                    pe.sem_inc(N.s_tp, 2)
                    pe.wait_ge(s_w, 16)
                else:
                    pe.wait_ge(s_wlo, KT)

                def products(n, j, i):
                    if last_layer:
                        pe.wait_ge(s_oglo, over(n))
                    else:
                        pe.wait_ge(s_og[j], i * 16 + 16)
                    pe.wait_ge(s_t, free(n))
                    for half in range(2):
                        out = E.bank[2 * j + half][:, :]
                        c = slice(half * 512, half * 512 + 512)
                        for k in range(KT):
                            first, end = k == 0, k == KT - 1
                            if last_layer:
                                pe.matmul(out, og_lo[j][:, k, :], w_hi[:, k, c], start=first, stop=False)
                                pe.matmul(out, og_hi[j][:, k, :], w_lo[:, k, c], start=False, stop=False)
                                ins = pe.matmul(out, og_hi[j][:, k, :], w_hi[:, k, c], start=False, stop=end)
                            else:
                                ins = pe.matmul(out, og[j][:, k, :], w[:, k, c], start=first, stop=end)
                    ins.then_inc(s_y, 1)

                if last_layer:
                    pair_loop(pe, lambda n, j, i, last: products(n, j, i))
                else:
                    products(0, 0, 0)
                    with pe.Fori(0, NS // 2) as i:
                        products(i * 2 + 1, 1, i)
                        N.pe_transpose(pe, i * 2, 0)
                        products(i * 2 + 2, 0, i + 1)
                        N.pe_transpose(pe, i * 2 + 1, 1)
                    N.pe_transpose(pe, CTX, 0)


FWD, BWD = 0, 32
ROWS = 64
U_COL, WK_COL, EM_COL = 0, 1, 2


def reversed_cols(tile, width, p0, rows, first, n):
    return bass.AP(tensor=tile[:, :].tensor, offset=p0 * width + first + n - 1, ap=[[width, rows], [-1, n]])


def phase_gates(E):
    nc = E.nc
    with ExitStack() as ctx:
        sb = lambda n, s, d=F32: ctx.enter_context(nc.sbuf_tensor(f"gt_{n}", s, d))
        sem = lambda n: E.semaphore(f"gt_{n}")
        raw, w_hi, w_lo = sb("w", [P, KT, P]), sb("w_hi", [P, KT, P], F32R), sb("w_lo", [P, KT, P], F32R)
        bias = sb("bias", [P, 1])
        nat4 = sb("nat4", [P, 512])
        ig, lf, b, M, tmp, z, r = (sb(n, [ROWS, T]) for n in ("ig", "lf", "b", "M", "tmp", "z", "r"))
        entry, last_M, dec, m_out = sb("entry", [ROWS, NT]), sb("last_M", [ROWS, NT]), sb("dec", [ROWS, NT]), sb("m_out", [ROWS, 1])
        s_zero, s_w, s_hi, s_lo, s_unit, s_nat, s_spread, s_m0, s_d, s_a, s_dma, s_tr, s_col = (
            sem(x) for x in ("zeroed", "w_loaded", "w_hi", "w_lo", "unit", "biased", "spread", "m0_loaded",
                             "dve_step", "act_step", "rows_stored", "turned", "columns"))
        w_in = E.a["mlstm_w_in"][0].rearrange("(k p) m -> p k m", p=P)
        chunks = lambda t: t[:, :].rearrange("p (c t) -> p c t", t=P)

        with nc.Block() as block:
            @block.sync
            def _(sp):
                sp.dma_start(E.causal[:, :, :], E.a["causal_mask"]).then_inc(s_m0, 16)
                sp.wait_ge(s_zero, 4)
                with nc.allow_non_contiguous_dma(reason="gate columns and short vectors"):
                    for q in range(4):
                        sp.dma_start(raw[:, :, 32 * q:32 * q + MH], w_in[:, :, 5 * D + MH * q:5 * D + MH * (q + 1)]).then_inc(s_w, 16)
                        sp.dma_start(bias[32 * q:32 * q + MH, :], E.a["mlstm_b_gates"][0, MH * q:MH * (q + 1)].rearrange("(p a) -> p a", a=1)).then_inc(s_w, 16)
                    for d, row in enumerate((FWD, BWD)):
                        sp.dma_start(entry[row:row + MH, 0:1], E.a["state_m"][0, 0, d].rearrange("(p a) -> p a", a=1)).then_inc(s_m0, 16)
                    sp.wait_ge(s_d, 10)
                    for d, row in enumerate((FWD, BWD)):
                        sp.dma_start(E.new_m[0, 0, d].rearrange("(p a) -> p a", a=1), m_out[row:row + MH, :]).then_inc(s_dma, 16)
                    sp.wait_ge(s_a, 4)
                    for d, row in enumerate((FWD, BWD)):
                        sp.dma_start(E.decay_dram[d], dec[row:row + MH, :]).then_inc(s_dma, 16)
                    rows = E.rows_dram.rearrange("h c q t -> q h c t")
                    sp.dma_start(rows[0], chunks(M)[FWD:FWD + MH]).then_inc(s_dma, 16)
                    sp.wait_ge(s_a, 5)
                    sp.dma_start(rows[2], chunks(tmp)[FWD:FWD + MH]).then_inc(s_dma, 16)
                    sp.wait_ge(s_d, 14)
                    sp.dma_start(rows[1], chunks(r)[BWD:BWD + MH]).then_inc(s_dma, 16)
                    sp.dma_start(rows[3], chunks(b)[BWD:BWD + MH]).then_inc(s_dma, 16)
                sp.wait_ge(s_dma, 128)
                sp.dma_start(E.decay[:, :, :, :], E.decay_dram.rearrange("d h c -> (d h c)").rearrange("(a n) -> a n", a=1).partition_broadcast(P)).then_inc(s_dma, 16)
                sp.wait_ge(s_dma, 144)

            @block.gpsimd
            def _(pool):
                pool.memset(raw[:, :, :], 0.0).then_inc(s_zero, 1)
                pool.memset(bias[:, :], 0.0).then_inc(s_zero, 1)
                pool.memset(entry[:, :], 0.0).then_inc(s_zero, 1)
                pool.memset(ig[:, :], 0.0).then_inc(s_zero, 1)
                pool.memset(lf[:, :], 0.0).then_inc(s_zero, 1)
                pool.memset(z[:, :], 0.0).then_inc(s_zero, 1)
                pool.memset(r[:, :], 1.0).then_inc(s_zero, 1)
                pool.wait_ge(s_zero, 7)
                pool.memset(chunks(r)[:, :, 0:1], 0.0).then_inc(s_zero, 1)
                pool.wait_ge(s_w, 128)
                pool.tensor_copy(w_hi[:, :, :], raw[:, :, :]).then_inc(s_hi, 1)

            @block.tensor
            def _(pe):
                pe.wait_ge(s_lo, 1)
                for g, (t0, t1) in enumerate(GROUPS):
                    tok = slice(t0 * P, t1 * P)
                    out = E.bank[g][:, 0:(t1 - t0) * P]
                    for k in range(KT):
                        pe.matmul(out, w_lo[:, k, :], E.h_hi[:, k, tok], start=(k == 0), stop=False)
                        pe.matmul(out, w_hi[:, k, :], E.h_lo[:, k, tok], start=False, stop=False)
                        ins = pe.matmul(out, w_hi[:, k, :], E.h_hi[:, k, tok], start=False, stop=(k == KT - 1))
                    ins.then_inc(s_unit, 1)
                for q, (src, ready) in enumerate(((lf, 18), (ig, 20), (M, 20))):
                    pe.wait_ge(s_d, ready)
                    if q == 0:
                        pe.wait_ge(s_nat, NG)
                    for c in range(NT):
                        g = 3 * q + c // 8
                        if g == 8 and c == 16:
                            pe.wait_ge(s_col, 1)
                        ins = pe.transpose(E.bank[g % 8][:, (c % 8) * ROWS:(c % 8 + 1) * ROWS],
                                           src[:, c * P:(c + 1) * P], E.ident[0:ROWS, 0:ROWS])
                    ins.then_inc(s_tr, 1)

            @block.scalar
            def _(act):
                act.wait_ge(s_w, 128)
                for g, (t0, t1) in enumerate(GROUPS):
                    act.wait_ge(s_unit, g + 1)
                    act.wait_ge(s_spread, g)
                    act.activation(nat4[:, 0:(t1 - t0) * P], E.bank[g][:, 0:(t1 - t0) * P], ACT.Identity,
                                   bias=bias[:, 0:1]).then_inc(s_nat, 1)
                act.wait_ge(s_spread, NG)
                act.activation(tmp[:, :], lf[:, :], ACT.Abs).then_inc(s_a, 1)
                act.wait_ge(s_a, 1)
                act.activation(tmp[:, :], tmp[:, :], ACT.Exp, scale=-1.0).then_inc(s_a, 1)
                act.wait_ge(s_a, 2)
                act.activation(tmp[:, :], tmp[:, :], ACT.Ln, bias=E.one[0:ROWS, 0:1]).then_inc(s_a, 1)
                act.wait_ge(s_d, 10)
                act.activation(dec[:, :], dec[:, :], ACT.Exp).then_inc(s_a, 1)
                act.wait_ge(s_d, 11)
                act.activation(tmp[:, :], tmp[:, :], ACT.Exp).then_inc(s_a, 1)
                act.wait_ge(s_d, 12)
                act.activation(z[:, :], z[:, :], ACT.Exp).then_inc(s_a, 1)
                act.wait_ge(s_d, 13)
                act.activation(lf[:, :], lf[:, :], ACT.Exp, scale=-1.0).then_inc(s_a, 1)

            @block.vector
            def _(dve):
                count = [0]

                def step(ins):
                    count[0] += 1
                    ins.then_inc(s_d, 1)
                    dve.wait_ge(s_d, count[0])

                dve.wait_ge(s_hi, 1)
                dve.tensor_tensor(w_lo[:, :, :], raw[:, :, :], w_hi[:, :, :], ALU.subtract).then_inc(s_lo, 1)
                dve.wait_ge(s_zero, 8)
                for g, (t0, t1) in enumerate(GROUPS):
                    dve.wait_ge(s_nat, g + 1)
                    lat = (min(t1, NS) - t0) * P
                    a = t0 * P
                    for dst, q in ((ig, 0), (lf, 1)):
                        dve.tensor_copy(dst[FWD:FWD + MH, a:t1 * P], nat4[32 * q:32 * q + MH, 0:(t1 - t0) * P])
                        if t1 > NS:
                            dve.tensor_copy(dst[BWD:BWD + MH, SAMPLE:T],
                                            reversed_cols(nat4, 512, 64 + 32 * q, MH, lat, P))
                        ins = dve.tensor_copy(dst[BWD:BWD + MH, SAMPLE - a - lat:SAMPLE - a],
                                              reversed_cols(nat4, 512, 64 + 32 * q, MH, 0, lat))
                    ins.then_inc(s_spread, 1)
                dve.wait_ge(s_a, 3)
                step(dve.scalar_tensor_tensor(lf[:, :], lf[:, :], 0.0, tmp[:, :], ALU.min, ALU.subtract))
                step(dve.tensor_tensor_scan(b[:, :], r[:, :], lf[:, :], 0.0, ALU.mult, ALU.add))
                step(dve.tensor_tensor(ig[:, :], ig[:, :], b[:, :], ALU.subtract))
                step(dve.tensor_copy(chunks(z)[:, 1:NS, 0:1], chunks(b)[:, 0:NS - 1, P - 1:P]))
                dve.wait_ge(s_m0, 48)
                step(dve.tensor_tensor_scan(M[:, 0:SAMPLE], z[:, 0:SAMPLE], ig[:, 0:SAMPLE], entry[:, 0:1],
                                            ALU.add, ALU.max))
                step(dve.tensor_tensor_scan(M[:, SAMPLE:T], z[:, SAMPLE:T], ig[:, SAMPLE:T], 0.0,
                                            ALU.add, ALU.max))
                step(dve.tensor_tensor(entry[:, 1:NS].unsqueeze(2), chunks(M)[:, 0:NS - 1, P - 1:P],
                                       chunks(b)[:, 0:NS - 1, P - 1:P], ALU.add))
                step(dve.tensor_copy(last_M[:, :].unsqueeze(2), chunks(M)[:, :, P - 1:P]))
                step(dve.tensor_tensor(m_out[:, :], M[:, T - 1:T], b[:, T - 1:T], ALU.add))
                step(dve.tensor_tensor(dec[:, :], entry[:, :], last_M[:, :], ALU.subtract))
                bc = lambda t: t[:, :].unsqueeze(2).to_broadcast([ROWS, NT, P])
                step(dve.tensor_tensor(chunks(tmp), bc(entry), chunks(M), ALU.subtract))
                step(dve.tensor_tensor(chunks(z), chunks(ig), bc(last_M), ALU.subtract))
                step(dve.tensor_tensor(lf[:, :], b[:, :], M[:, :], ALU.add))
                dve.wait_ge(s_a, 7)

                def turned(dst, src):
                    dve.tensor_copy(dst[BWD:BWD + MH, SAMPLE:T], reversed_cols(src, T, BWD, MH, SAMPLE, P))
                    return dve.tensor_copy(dst[BWD:BWD + MH, 0:SAMPLE], reversed_cols(src, T, BWD, MH, 0, SAMPLE))
                turned(r, M)
                step(turned(b, tmp))
                dve.wait_ge(s_dma, 128)
                step(dve.tensor_copy(M[:, :], lf[:, :]))
                step(turned(M, lf))
                step(dve.tensor_copy(lf[:, :], ig[:, :]))
                step(turned(lf, ig))
                step(dve.tensor_copy(ig[:, :], z[:, :]))
                step(turned(ig, z))
                for q in range(3):
                    dve.wait_ge(s_tr, q + 1)
                    for x in range(3):
                        n = min(8, NT - 8 * x)
                        src = E.bank[(3 * q + x) % 8][:, 0:n * ROWS].rearrange("p (c d y) -> p c d y", d=2, y=32)
                        ins = dve.tensor_copy(E.cols[:, 8 * x:8 * x + n, q, :, :], src[:, :, :, 0:MH])
                    ins.then_inc(s_col, 1)


def phase_mlstm(E):
    nc = E.nc
    E1 = MHD + 1
    with ExitStack() as ctx:
        sb = lambda n, s, d=F32: ctx.enter_context(nc.sbuf_tensor(f"m_{n}", s, d))
        sem = lambda n: E.semaphore(f"m_{n}")
        kT, qT, gT = sb("kT", [P, T]), sb("qT", [P, T]), sb("gT", [P, T])
        v1 = sb("v1", [P, NT, E1])
        CC = sb("states", [P, 2, NS + 1, E1])
        cout = sb("cout", [P, 2, E1])
        gexp = sb("gexp", [P, 512])
        kw = [sb(f"kw{j}", [P, 2, MHD]) for j in range(2)]
        bc = [sb(f"bc{x}", [P, 4, P]) for x in range(3)]
        hc = sb("hc", [P, NT, 3, 2])
        dech = sb("dech", [P, 2, NT])
        den = [sb(f"den{j}", [P, 2]) for j in range(2)]
        rec = [sb(f"rec{j}", [P, 2]) for j in range(2)]
        part = [sb(f"part{j}", [P, MHD]) for j in range(2)]
        hm = [sb(f"hm{j}", [P, MHD]) for j in range(2)]
        J = Projection(E, ctx, "mlstm", 5)
        (s_ones, s_relA, s_relD, s_vT, s_v1, s_hc, s_st, s_kT, s_kw, s_kv, s_cf, s_kvb, s_rev, s_cst,
         s_gexp, s_gd) = (sem(x) for x in (
            "ones", "bank_free_act", "bank_free_dve", "v_turned", "v_stored", "head_columns", "state_loaded",
            "k_turned", "weighted_keys", "kv_products", "forward_state", "kv_stored",
            "backward_state", "state_stored", "gate_exp", "gate_steps"))
        s_bc = [sem(f"rows_loaded{x}") for x in range(3)]
        (s_E, s_qw, s_W, s_S, s_P, s_num, s_den, s_rec, s_part, s_hm, s_hT, s_og, s_ogst) = (sem(x) for x in (
            "exponent", "q_weighted", "weights", "scores", "products", "num_done", "den", "recip", "part",
            "h_ready", "h_turned", "gated", "stored"))
        w_in = E.a["mlstm_w_in"][0].rearrange("(k p) m -> p k m", p=P)
        COL = {"k": D, "v": 2 * D, "q": 0, "o": 3 * D, "g": 4 * D}
        kinds = ["k", "v", "q", "o", "g"]
        NU = 5 * NG
        VG = [(0, 4), (4, 8), (8, 12), (12, 16), (16, 17)]
        VB = [4, 5, 6, 7, 4]

        def span(g):
            return slice(GROUPS[g][0] * P, GROUPS[g][1] * P), (GROUPS[g][1] - GROUPS[g][0]) * P

        with nc.Block() as block:
            @block.sync
            def _(sp):
                with sp.Fori(0, MH) as h:
                    def load(m):
                        J.sp_load(sp, h * 5 + m, [(0, w_in[:, :, ds(h * P + COL[kinds[m]], P)])])
                    load(0)
                    load(1)
                    sp.wait_ge(s_num, h * NT)
                    settle(E, sp)
                    with nc.allow_non_contiguous_dma(reason="normaliser columns"):
                        for d, slot in ((0, 0), (1, NS)):
                            sp.dma_start(CC[:, d, slot, 0:MHD], E.a["state_C"][0, 0, d, ds(h, 1)].rearrange("a d e -> d (a e)")).then_inc(s_st, 16)
                            sp.dma_start(CC[:, d, slot, MHD:E1], E.a["state_n"][0, 0, d, ds(h, 1)].rearrange("a d -> d a")).then_inc(s_st, 16)
                    for m in (2, 3, 4):
                        load(m)
                    with nc.allow_non_contiguous_dma(reason="normaliser columns"):
                        sp.wait_ge(s_kvb, h * NT + NT)
                        settle(E, sp)
                        for d in range(2):
                            sp.dma_start(E.new_C[0, 0, d, ds(h, 1)].rearrange("a d e -> d (a e)"), cout[:, d, 0:MHD]).then_inc(s_cst, 16)
                            sp.dma_start(E.new_n[0, 0, d, ds(h, 1)].rearrange("a d -> d a"), cout[:, d, MHD:E1]).then_inc(s_cst, 16)
                    for c in range(NT):
                        x = c % 3
                        sp.wait_ge(s_num, h * NT + max(c - 2, 0))
                        settle(E, sp)
                        row = E.rows_dram[ds(h, 1), c, :, :].rearrange("a q t -> a (q t)")
                        sp.dma_start(bc[x][:, :, :].rearrange("p q t -> p (q t)"), row.partition_broadcast(P)).then_inc(s_bc[x], 16)
                    sp.wait_ge(s_og, h * NT + NT)
                    settle(E, sp)
                    sp.dma_start(E.ogT_dram[ds(h, 1), :, :].rearrange("a p t -> (a p) t"), gT[:, :]).then_inc(s_ogst, 16)
                sp.wait_ge(s_ogst, 16 * MH)
                sp.wait_ge(s_cst, 64 * MH)

            @block.gpsimd
            def _(pool):
                pool.memset(v1[:, :, MHD:E1], 1.0).then_inc(s_ones, 1)
                with pool.Fori(0, MH) as h:
                    J.pool_hi(pool, h * 5, h * 5 + 1)
                    pool.wait_ge(s_og, h * NT)
                    settle(E, pool)
                    pool.tensor_copy(hc[:, :, :, :], E.cols[:, :, :, :, ds(h, 1)].rearrange("p c q d a -> p c q (d a)")).then_inc(s_hc, 1)
                    pool.tensor_copy(dech[:, :, :], E.decay[:, :, ds(h, 1), :].rearrange("p d a c -> p d (a c)")).then_inc(s_hc, 1)
                    for m in range(1, 5):
                        J.pool_hi(pool, h * 5 + m, h * 5 + m + 1)
                    pool.wait_ge(s_relA, h * (4 * NG) + 3 * NG)
                    for c in range(NT):
                        x = c % 3
                        per = [6, 6, 5][x]
                        pool.wait_ge(s_bc[x], h * (16 * per) + 16 * (c // 3 + 1))
                        pool.tensor_tensor(bc[x][:, 0:2, :], bc[x][:, 0:2, :], E.causal[:, :, :], ALU.add).then_inc(s_E, 1)
                        q = qT[:, c * P:(c + 1) * P].unsqueeze(1).to_broadcast([P, 2, P])
                        pool.tensor_tensor(bc[x][:, 2:4, :], bc[x][:, 2:4, :], q, ALU.mult).then_inc(s_qw, 1)

            @block.scalar
            def _(act):
                with act.Fori(0, MH) as h:
                    def evac(u):
                        m, g = u // NG, u % NG
                        tok, w = span(g)
                        act.wait_ge(J.s_unit, h * NU + u + 1)
                        src = E.bank[u % 4][:, 0:w]
                        if kinds[m] == "k":
                            act.activation(kT[:, tok], src, ACT.Copy, scale=MHD ** -0.5).then_inc(s_relA, 1)
                        elif kinds[m] == "v":
                            act.copy(gT[:, tok], src).then_inc(s_relA, 1)
                        elif kinds[m] == "q":
                            act.copy(qT[:, tok], src).then_inc(s_relA, 1)
                        elif kinds[m] == "o":
                            act.activation(gT[:, tok], src, ACT.Exp, scale=-1.0).then_inc(s_relA, 1)
                        else:
                            act.wait_ge(s_relD, h * NG + g)
                            act.activation(gexp[:, 0:w], src, ACT.Exp, scale=-1.0).then_inc(s_gexp, 1)

                    act.wait_ge(s_S, h * NT)
                    for u in range(NG):
                        evac(u)
                    act.wait_ge(s_ogst, h * 16)
                    for u in range(NG, 2 * NG):
                        evac(u)
                    act.wait_ge(s_num, h * NT)
                    for r, (a, z) in enumerate(VG):
                        act.wait_ge(s_vT, h * 5 + r + 1)
                        act.copy(v1[:, a:z, 0:MHD], E.bank[VB[r]][:, 0:(z - a) * P].rearrange("p (c e) -> p c e", e=P)).then_inc(s_v1, 1)
                    act.wait_ge(s_qw, h * NT)
                    act.wait_ge(s_hc, h * 2 + 2)
                    for s in range(NT + 1):
                        if 2 * NG + s < NU:
                            evac(2 * NG + s)
                        c = s - 1
                        if c >= 0:
                            act.wait_ge(s_kv, h * NT + c + 1)
                            if c < CTX:
                                dst = bass.AP(tensor=CC[:, :, :, :].tensor, offset=(c + 1) * E1,
                                              ap=[[2 * (NS + 1) * E1, P], [NS * E1, 2], [1, E1]])
                            else:
                                act.wait_ge(s_cst, h * 64)
                                dst = cout[:, :, :]
                            act.copy(dst, E.bank[6 + c % 2][:, 0:2 * E1].rearrange("p (d e) -> p d e", d=2)).then_inc(s_kvb, 1)
                    for s in range(NT + 1):
                        if s < NT:
                            act.wait_ge(s_E, h * NT + s + 1)
                            for d in range(2):
                                x = bc[s % 3][:, d, :]
                                ins = act.activation(x, x, ACT.Exp, bias=hc[:, s, U_COL, d:d + 1], scale=-1.0)
                            ins.then_inc(s_W, 1)
                        c = s - 1
                        if c >= 0:
                            act.wait_ge(s_rec, h * NT + c + 1)
                            act.wait_ge(s_hm, h * NT + max(c - 1, 0))
                            act.activation(part[c % 2][:, :], E.bank[2 + c % 2][:, 0:MHD], ACT.Copy,
                                           scale=rec[c % 2][:, 0:1]).then_inc(s_part, 1)

            @block.vector
            def _(dve):
                with dve.Fori(0, MH) as h:
                    J.dve_lo(dve, h * 5)
                    J.dve_lo(dve, h * 5 + 1)
                    J.dve_lo(dve, h * 5 + 2)
                    dve.wait_ge(s_hc, h * 2 + 2)
                    dve.wait_ge(s_st, h * 64 + 64)
                    for s in range(NT + 1):
                        u = 2 * NG + s
                        if u < NU:
                            m, g = u // NG, u % NG
                            if g == NG - 1 and m < 4:
                                J.dve_lo(dve, h * 5 + m + 1)
                            if m == 4:
                                tok, w = span(g)
                                k = h * (3 * NG) + 3 * g
                                dve.wait_ge(s_relA, h * (4 * NG) + 4 * NG)
                                dve.tensor_scalar(gT[:, tok], gT[:, tok], 1.0, None, ALU.add).then_inc(s_gd, 1)
                                dve.wait_ge(s_gexp, h * NG + g + 1)
                                dve.wait_ge(s_gd, k + 1)
                                dve.scalar_tensor_tensor(gexp[:, 0:w], gexp[:, 0:w], 1.0, gT[:, tok], ALU.add, ALU.mult).then_inc(s_gd, 1)
                                dve.wait_ge(s_gd, k + 2)
                                dve.reciprocal(gexp[:, 0:w], gexp[:, 0:w]).then_inc(s_gd, 1)
                                dve.wait_ge(s_gd, k + 3)
                                dve.tensor_tensor(gT[:, tok], E.bank[u % 4][:, 0:w], gexp[:, 0:w], ALU.mult).then_inc(s_relD, 1)
                        if s < NT:
                            dve.wait_ge(s_kT, h * NT + s + 1)
                            dve.wait_ge(s_kv, h * NT + max(s - 1, 0))
                            keys = E.bank[4 + s % 2][:, 0:P].unsqueeze(1).to_broadcast([P, 2, P])
                            weights = hc[:, s, WK_COL, :].unsqueeze(2).to_broadcast([P, 2, P])
                            dve.tensor_tensor(kw[s % 2][:, :, :], keys, weights, ALU.mult).then_inc(s_kw, 1)
                        c = s - 2
                        if 0 <= c < NS - 1:
                            dve.wait_ge(s_kvb, h * NT + c + 1)
                            dve.wait_ge(s_cf, h * (NS - 1) + c)
                            dve.scalar_tensor_tensor(CC[:, 0, c + 1, :], CC[:, 0, c, :], dech[:, 0, c:c + 1],
                                                     CC[:, 0, c + 1, :], ALU.mult, ALU.add).then_inc(s_cf, 1)
                    dve.wait_ge(s_kvb, h * NT + NT)
                    for n, c in enumerate(range(NS - 1, 0, -1)):
                        dve.wait_ge(s_rev, h * (NS - 1) + n)
                        dve.scalar_tensor_tensor(CC[:, 1, c, :], CC[:, 1, c + 1, :], dech[:, 1, n:n + 1],
                                                 CC[:, 1, c, :], ALU.mult, ALU.add).then_inc(s_rev, 1)
                    for s in range(NT + 2):
                        if s < NT:
                            dve.wait_ge(s_S, h * NT + s + 1)
                            dve.wait_ge(s_W, h * NT + s + 1)
                            x = bc[s % 3][:, 0:2, :]
                            S = E.bank[s % 2][:, 0:P].unsqueeze(1).to_broadcast([P, 2, P])
                            dve.tensor_tensor(x, S, x, ALU.mult).then_inc(s_P, 1)
                        c = s - 1
                        if 0 <= c < NT:
                            num = E.bank[2 + c % 2][:, 0:2 * E1].rearrange("p (d e) -> p d e", d=2)
                            dve.wait_ge(s_num, h * NT + c + 1)
                            floor = hc[:, c, EM_COL, :].unsqueeze(2)
                            d = den[c % 2][:, :].unsqueeze(2)
                            dve.scalar_tensor_tensor(d, num[:, :, MHD:E1], -1.0, floor, ALU.mult, ALU.max).then_inc(s_den, 1)
                            dve.wait_ge(s_den, h * (2 * NT) + 2 * c + 1)
                            dve.tensor_tensor(d, num[:, :, MHD:E1], d, ALU.max).then_inc(s_den, 1)
                            dve.wait_ge(s_den, h * (2 * NT) + 2 * c + 2)
                            dve.wait_ge(s_part, h * NT + max(c - 1, 0))
                            dve.reciprocal(rec[c % 2][:, :], den[c % 2][:, :]).then_inc(s_rec, 1)
                            dve.wait_ge(s_part, h * NT + c + 1)
                            dve.wait_ge(s_hT, h * NT + max(c - 1, 0))
                            dve.scalar_tensor_tensor(hm[c % 2][:, :], num[:, 1, 0:MHD], rec[c % 2][:, 1:2],
                                                     part[c % 2][:, :], ALU.mult, ALU.add).then_inc(s_hm, 1)
                        c = s - 2
                        if c >= 0:
                            dve.wait_ge(s_hT, h * NT + c + 1)
                            gtile = gT[:, c * P:(c + 1) * P]
                            dve.tensor_tensor(gtile, E.bank[4 + c % 2][:, 0:P], gtile, ALU.mult).then_inc(s_og, 1)

            @block.tensor
            def _(pe):
                pe.sem_inc(J.s_used, 2)
                pe.wait_ge(s_ones, 1)
                with pe.Fori(0, MH) as h:
                    def unit(u):
                        if u < 4:
                            pe.wait_ge(s_relD, h * NG)
                            pe.wait_ge(s_P, h * NT)
                            pe.wait_ge(s_hm, h * NT)
                        elif u - 4 < 4 * NG:
                            pe.wait_ge(s_relA, h * (4 * NG) + u - 3)
                        else:
                            pe.wait_ge(s_relD, h * NG + u - 3 - 4 * NG)
                        J.pe_unit(pe, h * 5 + u // NG, u % NG, E.bank[u % 4])

                    for u in range(2 * NG):
                        unit(u)
                    pe.wait_ge(s_relA, h * (4 * NG) + 2 * NG)
                    pe.wait_ge(s_og, h * NT)
                    for r, (a, z) in enumerate(VG):
                        if r == 4:
                            pe.wait_ge(s_v1, h * 5 + 1)
                        for t in range(a, z):
                            ins = pe.transpose(E.bank[VB[r]][:, (t - a) * P:(t - a + 1) * P], gT[:, t * P:(t + 1) * P], E.ident[:, :])
                        ins.then_inc(s_vT, 1)
                    for s in range(NT + 1):
                        if 2 * NG + s < NU:
                            unit(2 * NG + s)
                        if s < NT:
                            if s == 0:
                                pe.wait_ge(s_v1, h * 5 + 5)
                            if s >= 2:
                                pe.wait_ge(s_kw, h * NT + s - 1)
                            pe.transpose(E.bank[4 + s % 2][:, 0:P], kT[:, s * P:(s + 1) * P], E.ident[:, :]).then_inc(s_kT, 1)
                        c = s - 1
                        if c >= 0:
                            pe.wait_ge(s_kw, h * NT + c + 1)
                            if c >= 2:
                                pe.wait_ge(s_kvb, h * NT + c - 1)
                            for d in range(2):
                                ins = pe.matmul(E.bank[6 + c % 2][:, d * E1:(d + 1) * E1], kw[c % 2][:, d, :],
                                                v1[:, c, :], start=True, stop=True, skip_group_check=True)
                            ins.then_inc(s_kv, 1)
                    pe.wait_ge(s_relA, h * (4 * NG) + 4 * NG)
                    pe.wait_ge(s_relD, h * NG + NG)
                    for s in range(NT + 2):
                        if s < NT:
                            if s >= 2:
                                pe.wait_ge(s_P, h * NT + s - 1)
                            tok = slice(s * P, (s + 1) * P)
                            pe.matmul(E.bank[s % 2][:, 0:P], kT[:, tok], qT[:, tok], start=True, stop=True).then_inc(s_S, 1)
                        c = s - 1
                        if 0 <= c < NT:
                            pe.wait_ge(s_P, h * NT + c + 1)
                            pe.wait_ge(s_qw, h * NT + c + 1)
                            if c == 0:
                                pe.wait_ge(s_cf, h * (NS - 1) + NS - 1)
                                pe.wait_ge(s_rev, h * (NS - 1) + NS - 1)
                            if c >= 2:
                                pe.wait_ge(s_hm, h * NT + c - 1)
                            for d in range(2):
                                out = E.bank[2 + c % 2][:, d * E1:(d + 1) * E1]
                                ins = pe.matmul(out, bc[c % 3][:, d, :], v1[:, c, :], start=True, stop=(c == CTX),
                                                skip_group_check=True)
                                if c < CTX:
                                    ins = pe.matmul(out, bc[c % 3][:, 2 + d, :], CC[:, d, c + d, :], start=False, stop=True,
                                                    skip_group_check=True)
                            ins.then_inc(s_num, 1)
                        c = s - 2
                        if c >= 0:
                            pe.wait_ge(s_hm, h * NT + c + 1)
                            if c >= 2:
                                pe.wait_ge(s_og, h * NT + c - 1)
                            pe.transpose(E.bank[4 + c % 2][:, 0:P], hm[c % 2][:, :], E.ident[:, :]).then_inc(s_hT, 1)


def build(nc, a, outs, phases=("pre", "attn", "out0", "gates", "mlstm", "out1"), debug=None):
    E = Env()
    E.nc, E.a = nc, a
    (E.out_prompt, E.out_sample, new_k, new_v, E.new_C, E.new_n, E.new_m) = outs
    E.out_prompt = E.out_prompt[0]
    E.out_sample = E.out_sample[0]
    E.new_k = new_k[0, 0].rearrange("s h d -> s (h d)")
    E.new_v = new_v[0, 0].rearrange("s h d -> s (h d)")
    E.cache_v = a["cache_v"][0, 0].rearrange("(t p) h d -> p t (h d)", p=P)
    E.x_tile = lambda n: a["x_sample"][0, ds(n * P, P), :] if not isinstance(n, int) else a["x_sample"][0, n * P:(n + 1) * P, :]
    dram = lambda n, s: nc.dram_tensor(n, s, F32, kind="Internal").ap()
    E.gates_dram = dram("gate_rows", [2, 2, D])
    E.ckt_dram = dram("cached_keys_turned", [P, NKV * PAST])
    E.ogT_dram = dram("gated_output", [KT, P, T])
    E.x1_dram = dram("layer0_output", [T, D])
    E.rows_dram = dram("gate_rows_mlstm", [MH, NT, 4, P])
    E.decay_dram = dram("decays", [2, MH, NT])
    if debug:
        for k, v in debug.items():
            if k == "ogT": E.ogT_dram = v
            if k == "x1": E.x1_dram = v
            if k == "rows": E.rows_dram = v
    with ExitStack() as ctx:
        sb = lambda n, s, d=F32: ctx.enter_context(nc.sbuf_tensor(n, s, d))
        E.s_tick = ctx.enter_context(nc.semaphore("tick"))
        phase_semaphores = []

        def semaphore(name):
            phase_semaphores.append(nc.alloc_semaphore(name=name))
            return phase_semaphores[-1]
        E.semaphore = semaphore

        def run(phase, *args):
            phase(E, *args)
            nc.clear_and_free_semaphores(list(phase_semaphores))
            nc.all_engine_barrier()
            phase_semaphores.clear()
        E.PS = ctx.enter_context(nc.psum_tensor("psum", [P, 8, 512], F32))
        E.bank = [E.PS[:, b, :] for b in range(8)]
        E.s_pair = lambda p: E.PS[:, 2 * p:2 * p + 2, 0:320]
        E.ident = sb("ident", [P, P])
        E.eps = sb("eps", [P, 1])
        E.one = sb("one", [P, 1])
        E.hscale = sb("hscale", [P, 2, 2, KT])
        E.hshift = sb("hshift", [P, 2, 2, KT])
        with ExitStack() as c1:
            E.h_hi = c1.enter_context(nc.sbuf_tensor("h_hi", [P, KT, T], F32R))
            E.h_lo = c1.enter_context(nc.sbuf_tensor("h_lo", [P, KT, T], F32R))
            with ExitStack() as c2:
                E.wmask = c2.enter_context(nc.sbuf_tensor("wmask", [P, 3, 2 * P], BF16))
                E.identb = c2.enter_context(nc.sbuf_tensor("identb", [P, P], BF16))
                with ExitStack() as c3:
                    E.wmaskf = c3.enter_context(nc.sbuf_tensor("wmaskf", [P, 3, 2 * P], F32))
                    run(phase_pre)
                if "attn" in phases:
                    run(phase_attn)
            if "out0" in phases:
                run(phase_out, 0)
            with ExitStack() as c2:
                E.causal = c2.enter_context(nc.sbuf_tensor("causal", [P, 2, P], F32))
                E.cols = c2.enter_context(nc.sbuf_tensor("gate_columns", [P, NT, 3, 2, MH], F32))
                E.decay = c2.enter_context(nc.sbuf_tensor("decay_factors", [P, 2, MH, NT], F32))
                if "gates" in phases:
                    run(phase_gates)
                if "mlstm" in phases:
                    run(phase_mlstm)
        if "out1" in phases:
            run(phase_out, 1)


_INS = ["x_prompt", "x_sample", "cache_k", "cache_v", "state_C", "state_n", "state_m", "c", "c_ctx",
        "attn_norm_w", "attn_ada_w", "attn_ada_b", "attn_w_in", "attn_sink", "attn_w_out",
        "mlstm_norm_w", "mlstm_ada_w", "mlstm_ada_b", "mlstm_w_in", "mlstm_b_gates", "mlstm_w_out",
        "final_norm_w"]
_OUTS = [(1, P, D), (1, SAMPLE, D), (1, 1, P, NKV, HD), (1, 1, P, NKV, HD),
         (1, 1, 2, MH, MHD, MHD), (1, 1, 2, MH, MHD), (1, 1, 2, MH)]


def shape_constants():
    import numpy as np
    f = np.float32
    q, j = np.arange(P)[:, None], np.arange(P)[None, :]
    prev = np.where(j >= q, 0, -BIG).astype(f)
    nxt = np.where(j <= q, 0, -BIG).astype(f)
    none = np.full((P, P), -BIG, f)
    window = np.stack([np.concatenate(x, 1) for x in ((none, nxt), (prev, nxt), (prev, none))], 1)
    causal = np.stack([np.where(q <= j, 0, BIG), np.where(q >= j, 0, BIG)], 1).astype(f)
    nf = HD // 4
    inv = (f(10000.0) ** (-np.arange(nf, dtype=f) / f(nf))).astype(f)
    t = np.arange(SAMPLE)
    row, col = (t // 64).astype(f), (t % 64).astype(f)
    ar, ac = inv[:, None] * row[None, :], inv[:, None] * col[None, :]
    ang = np.concatenate([ar, ar, ac, ac] * 2, 0).astype(f)
    sign = np.concatenate([-np.ones(nf), np.ones(nf)] * 4)[:, None].astype(f)
    rotary = np.stack([np.cos(ang), np.sin(ang) * sign], 1).astype(f)
    return {"ident": np.eye(P, dtype=f), "window_mask": window, "causal_mask": causal, "rotary": rotary}


def kernel(**inputs):
    import numpy as np
    import concourse.bacc as bacc
    from concourse.bass_utils import run_bass_kernel_spmd

    nc = bacc.Bacc("TRN2", target_bir_lowering=False, num_devices=1, dynamic_dma_scratch_size=1024)
    arrays = {k: np.ascontiguousarray(inputs[k]) for k in _INS}
    arrays.update(shape_constants())
    a = {k: nc.dram_tensor(f"in_{k}", v.shape, F32, kind="ExternalInput").ap() for k, v in arrays.items()}
    outs = [nc.dram_tensor(f"out_{i}", s, F32, kind="ExternalOutput").ap() for i, s in enumerate(_OUTS)]
    build(nc, a, outs)
    r = run_bass_kernel_spmd(nc, [{f"in_{k}": v for k, v in arrays.items()}], core_ids=[0])
    return tuple(r.results[0][f"out_{i}"] for i in range(len(_OUTS)))
```

```python
from contextlib import ExitStack

import concourse.bass as bass
from concourse import mybir

F32 = mybir.dt.float32
F32R = mybir.dt.float32r
BF16 = mybir.dt.bfloat16
ALU = mybir.AluOpType
ACT = mybir.ActivationFunctionType
AX = mybir.AxisListType
ds = bass.ds

P = 128
D = 1024
KT = D // P
SAMPLE = 2048
NS = SAMPLE // P
CTX = NS
NT = NS + 1
T = NT * P
PAST = 256
HD = 64
NKV = 4
NHEAD = 16
MH = 8
MHD = 128
EPS = 1e-6
BIG = 1.0e30

GROUPS = [(0, 4), (4, 8), (8, 11), (11, 14), (14, 17)]
NG = len(GROUPS)
KPAD = PAST
KLAT = KPAD + P
KREQ = KLAT + SAMPLE + P
KCOLS = KREQ + P
VT_LAT = KLAT // P
VT_REQ = KREQ // P
VTILES = KCOLS // P
VGROUPS = [(0, 8), (8, 16), (16, 17)]


class Env:
    pass


def pair_loop(eng, body):
    with eng.Fori(0, NS // 2) as i:
        for j in range(2):
            body(i * 2 + j, j, i, False)
    body(CTX, 0, NS // 2, True)


def over(n):
    return n + 3


def free(n):
    return n + 1


def at(n):
    return n + 1


def settle(E, eng):
    eng.sem_inc(E.s_tick, 1)


class NormTranspose:

    def __init__(self, E, ctx, layer, src, src_ready):
        nc = E.nc
        self.E, self.layer, self.src, self.src_ready = E, layer, src, src_ready
        sb = lambda n, s, d=F32: ctx.enter_context(nc.sbuf_tensor(f"{n}{layer}", s, d))
        sem = lambda n: E.semaphore(f"{n}{layer}")
        self.xn = [sb(f"xn{j}_", [P, D]) for j in range(2)]
        self.htmp = [sb(f"htmp{j}_", [P, KT, P]) for j in range(2)]
        self.ss = sb("ss", [P, 2])
        self.std = sb("std", [P, 2])
        self.rs = sb("rs", [P, 2])
        self.s_sq = sem("sum_of_squares")
        self.s_std = sem("root_mean_square")
        self.s_rs = sem("rms_reciprocal")
        self.s_xn = sem("normalised")
        self.s_tp = sem("transposed")
        self.s_ha = sem("modulated_act")
        self.s_hd = sem("modulated_dve")
        self.s_hi = sem("hi_part")
        self.s_lo = sem("lo_part")
        self.bank = [E.bank[4:6], E.bank[6:8]]

    def credits_act(self, eng):
        for s in (self.s_sq, self.s_std, self.s_ha):
            eng.sem_inc(s, 2)

    def credits_dve(self, eng):
        for s in (self.s_rs, self.s_xn, self.s_hd, self.s_lo):
            eng.sem_inc(s, 2)

    def act_stats(self, eng, n, j):
        self.src_ready(eng, n, j)
        eng.wait_ge(self.s_tp, free(n))
        eng.activation(self.xn[j][:, :], self.src[j][:, :], ACT.Square,
                       accum_out=self.ss[:, j:j + 1]).then_inc(self.s_sq, 1)
        eng.wait_ge(self.s_sq, over(n))
        eng.wait_ge(self.s_rs, free(n))
        eng.activation(self.std[:, j:j + 1], self.ss[:, j:j + 1], ACT.Sqrt,
                       bias=self.E.eps[:, 0:1], scale=1.0 / D).then_inc(self.s_std, 1)

    def dve_normalise(self, eng, n, j):
        self.src_ready(eng, n, j)
        eng.wait_ge(self.s_std, over(n))
        eng.wait_ge(self.s_xn, free(n))
        eng.reciprocal(self.rs[:, j:j + 1], self.std[:, j:j + 1]).then_inc(self.s_rs, 1)
        eng.wait_ge(self.s_rs, over(n))
        eng.wait_ge(self.s_tp, free(n))
        eng.tensor_scalar(self.xn[j][:, :], self.src[j][:, :], self.rs[:, j:j + 1], None,
                          ALU.mult).then_inc(self.s_xn, 1)

    def pe_transpose(self, eng, n, j):
        eng.wait_ge(self.s_xn, over(n))
        eng.wait_ge(self.s_ha, free(n))
        eng.wait_ge(self.s_hd, free(n))
        for k in range(KT):
            out = self.bank[j][k // 4][:, (k % 4) * P:(k % 4 + 1) * P]
            last = eng.transpose(out, self.xn[j][:, k * P:(k + 1) * P], self.E.ident[:, :])
        last.then_inc(self.s_tp, 1)

    def act_modulate(self, eng, n, j, cond):
        E, l = self.E, self.layer
        eng.wait_ge(self.s_tp, over(n))
        eng.wait_ge(self.s_lo, free(n))
        for k in range(4):
            last = eng.activation(self.htmp[j][:, k, :], self.bank[j][0][:, k * P:(k + 1) * P],
                                  ACT.Identity, bias=E.hshift[:, l, cond, k:k + 1],
                                  scale=E.hscale[:, l, cond, k:k + 1])
        last.then_inc(self.s_ha, 1)

    def dve_modulate(self, eng, n, j, cond):
        E, l = self.E, self.layer
        eng.wait_ge(self.s_tp, over(n))
        for k in range(4, KT):
            last = eng.tensor_scalar(self.htmp[j][:, k, :], self.bank[j][1][:, (k - 4) * P:(k - 3) * P],
                                     E.hscale[:, l, cond, k:k + 1], E.hshift[:, l, cond, k:k + 1],
                                     ALU.mult, ALU.add)
        last.then_inc(self.s_hd, 1)

    def pool_hi(self, eng, n, j):
        eng.wait_ge(self.s_ha, over(n))
        eng.wait_ge(self.s_hd, over(n))
        settle(self.E, eng)
        eng.tensor_copy(self.E.h_hi[:, :, ds(n * P, P)], self.htmp[j][:, :, :]).then_inc(self.s_hi, 1)

    def dve_lo(self, eng, n, j):
        eng.wait_ge(self.s_hi, over(n))
        eng.tensor_tensor(self.E.h_lo[:, :, ds(n * P, P)], self.htmp[j][:, :, :],
                          self.E.h_hi[:, :, ds(n * P, P)], ALU.subtract).then_inc(self.s_lo, 1)


def phase_pre(E):
    nc = E.nc
    with ExitStack() as ctx:
        sb = lambda n, s, d=F32: ctx.enter_context(nc.sbuf_tensor(n, s, d))
        sem = lambda n: E.semaphore(n)
        s_const, s_cmask, s_cond, s_bias_zero, s_bias = (sem(x) for x in (
            "const_loaded", "bf16_masks", "cond_loaded", "bias_rows_zeroed", "bias_rows_loaded"))
        s_exp, s_silu, s_vec, s_vecs = (sem(x) for x in ("cond_exp", "cond_silu", "vec_turned", "vec_copied"))
        s_ck, s_ckt, s_ckc, s_cko = (sem(x) for x in ("ck_loaded", "ck_turned", "ck_copied", "ck_stored"))
        s_ada = [sem(f"ada_loaded{j}") for j in range(2)]
        s_adause, s_grow, s_gpe, s_mod, s_modpe = (sem(x) for x in (
            "ada_used", "gate_row_done", "gate_row_ready", "mod_vectors", "mod_products"))
        s_gst = sem("gate_rows_stored")
        s_x = [sem(f"x_loaded{j}") for j in range(2)]

        xb = [sb(f"xb{j}", [P, D]) for j in range(2)]
        ada = [sb(f"ada{j}", [P, KT, 512]) for j in range(2)]
        vecrows = sb("vecrows", [48, P])
        vecs = sb("vecs", [P, 48])
        cnd = sb("cnd", [P, 2, KT])
        cnd_e = sb("cnd_e", [P, 2, KT])
        silu_c = sb("silu_c", [P, KT, 2])
        silu_pad = sb("silu_pad", [P, KT, 33])
        grow = sb("grow", [33, D])
        gbias = sb("gbias", [33, D])
        ckr = sb("ckr", [P, 2, NKV, 2, HD])
        ckt = xb[0]

        def x_ready(eng, n, j):
            eng.wait_ge(s_x[j], (n - j) * 8 + 16)

        N = NormTranspose(E, ctx, 0, xb, x_ready)
        modps, vecps = E.bank[0], E.bank[1]
        gateps = [E.bank[2], E.bank[3]]

        with nc.Block() as block:
            @block.sync
            def _(sp):
                sp.dma_start(E.ident[:, :], E.a["ident"]).then_inc(s_const, 16)
                sp.dma_start(E.wmaskf[:, :, :], E.a["window_mask"]).then_inc(s_const, 16)
                with nc.allow_non_contiguous_dma(reason="short vectors"):
                    sp.dma_start(vecrows[0:8, :], E.a["attn_norm_w"].rearrange("a (k p) -> (a k) p", p=P)).then_inc(s_const, 16)
                    sp.dma_start(vecrows[8:24, :], E.a["attn_ada_b"][:, 0:2 * D].rearrange("a (k p) -> (a k) p", p=P)).then_inc(s_const, 16)
                    sp.dma_start(vecrows[24:32, :], E.a["mlstm_norm_w"].rearrange("a (k p) -> (a k) p", p=P)).then_inc(s_const, 16)
                    sp.dma_start(vecrows[32:48, :], E.a["mlstm_ada_b"][:, 0:2 * D].rearrange("a (k p) -> (a k) p", p=P)).then_inc(s_const, 16)
                    sp.dma_start(cnd[:, 0, :], E.a["c"].rearrange("a (p k) -> p (a k)", k=KT)).then_inc(s_cond, 16)
                    sp.dma_start(cnd[:, 1, :], E.a["c_ctx"].rearrange("(p k) -> p k", k=KT)).then_inc(s_cond, 16)
                for r in range(2):
                    for k in range(2):
                        sp.dma_start(ckr[:, k, :, r, :], E.a["cache_k"][0, 0, k * P:(k + 1) * P]).then_inc(s_ck, 16)
                for n in range(12):
                    layer, c = n // 6, n % 6
                    w = E.a["attn_ada_w"] if layer == 0 else E.a["mlstm_ada_w"]
                    if n >= 2:
                        sp.wait_ge(s_adause, n - 1)
                    sp.dma_start(ada[n % 2][:, :, :], w[0].rearrange("(p k) m -> p k m", k=KT)[:, :, c * 512:(c + 1) * 512]).then_inc(s_ada[n % 2], 16)
                    if n == 3:
                        sp.wait_ge(s_ckc, 1)
                        sp.dma_start(E.ckt_dram, ckt[:, :]).then_inc(s_cko, 16)
                    if c == 4:
                        if layer == 1:
                            sp.wait_ge(s_gst, 32)
                        sp.wait_ge(s_bias_zero, layer + 1)
                        b = E.a["attn_ada_b"] if layer == 0 else E.a["mlstm_ada_b"]
                        sp.dma_start(gbias[0:1, :], b[:, 2 * D:3 * D]).then_inc(s_bias, 16)
                        sp.dma_start(gbias[32:33, :], b[:, 2 * D:3 * D]).then_inc(s_bias, 16)
                    if c == 5 and layer == 0:
                        sp.wait_ge(s_grow, 2)
                        for r in range(2):
                            sp.dma_start(E.gates_dram[0, r:r + 1, :], grow[32 * r:32 * r + 1, :]).then_inc(s_gst, 16)
                    if n == 11:
                        sp.wait_ge(s_grow, 4)
                        for r in range(2):
                            sp.dma_start(E.gates_dram[1, r:r + 1, :], grow[32 * r:32 * r + 1, :]).then_inc(s_gst, 16)
                        sp.wait_ge(s_gst, 64)

            @block.gpsimd
            def _(pool):
                pool.sem_inc(N.s_hi, 2)
                pair_loop(pool, lambda n, j, i, last: N.pool_hi(pool, n, j))

            @block.scalar
            def _(act):
                N.credits_act(act)
                act.wait_ge(s_cond, 32)
                act.activation(cnd_e[:, :, :], cnd[:, :, :], ACT.Exp, scale=-1.0).then_inc(s_exp, 1)
                act.wait_ge(s_cko, 16)
                for j in range(2):
                    act.dma_start(xb[j][:, :], E.a["x_sample"][0, j * P:(j + 1) * P, :]).then_inc(s_x[j], 16)

                def tile(n, j, i, last):
                    N.act_stats(act, n, j)
                    if not last:
                        act.wait_ge(N.s_xn, over(n))
                        act.dma_start(xb[j][:, :], E.x_tile(n + 2)).then_inc(s_x[j], 16)
                    N.act_modulate(act, n, j, 1 if last else 0)

                act.wait_ge(s_mod, 1)
                with act.Fori(0, NS // 2 - 1) as i:
                    for j in range(2):
                        tile(i * 2 + j, j, i, False)
                N.act_stats(act, NS - 2, 0)
                act.wait_ge(N.s_xn, over(NS - 2))
                act.dma_start(xb[0][:, :], E.a["x_prompt"][0]).then_inc(s_x[0], 16)
                N.act_modulate(act, NS - 2, 0, 0)
                N.act_stats(act, NS - 1, 1)
                N.act_modulate(act, NS - 1, 1, 0)
                N.act_stats(act, CTX, 0)
                N.act_modulate(act, CTX, 0, 1)

            @block.vector
            def _(dve):
                N.credits_dve(dve)
                dve.memset(silu_pad[:, :, :], 0.0).then_inc(s_silu, 1)
                dve.memset(gbias[:, :], 0.0).then_inc(s_bias_zero, 2)
                dve.memset(E.one[:, :], 1.0)
                dve.memset(E.eps[:, :], EPS).then_inc(s_silu, 1)
                dve.wait_ge(s_const, 96)
                dve.tensor_copy(E.wmask[:, :, :], E.wmaskf[:, :, :]).then_inc(s_cmask, 1)
                dve.tensor_copy(E.identb[:, :], E.ident[:, :]).then_inc(s_cmask, 1)
                dve.wait_ge(s_exp, 1)
                dve.tensor_scalar(cnd_e[:, :, :], cnd_e[:, :, :], 1.0, None, ALU.add).then_inc(s_silu, 1)
                dve.wait_ge(s_silu, 3)
                dve.reciprocal(cnd_e[:, :, :], cnd_e[:, :, :]).then_inc(s_silu, 1)
                dve.wait_ge(s_silu, 4)
                dve.tensor_tensor(silu_c[:, :, :].rearrange("p k c -> p c k"), cnd[:, :, :], cnd_e[:, :, :], ALU.mult).then_inc(s_silu, 1)
                dve.wait_ge(s_silu, 5)
                for r in range(2):
                    dve.tensor_copy(silu_pad[:, :, 32 * r:32 * r + 1], silu_c[:, :, r:r + 1]).then_inc(s_silu, 1)
                dve.wait_ge(s_vec, 1)
                dve.tensor_copy(vecs[:, :], vecps[:, 0:48]).then_inc(s_vecs, 1)
                for h in range(2):
                    dve.wait_ge(s_ckt, h + 1)
                    v = ckt[:, :].rearrange("p (h t) -> p h t", h=NKV)[:, :, h * P:(h + 1) * P]
                    ins = dve.tensor_copy(v, E.bank[4 + h][:, :].rearrange("p (h t) -> p h t", h=NKV))
                ins.then_inc(s_ckc, 1)
                dve.wait_ge(s_vecs, 1)

                def mods(layer):
                    dve.wait_ge(s_modpe, layer + 1)
                    m = modps[:, layer * 32:layer * 32 + 32].rearrange("p (b c) -> p c b", c=2)
                    v0 = layer * 24
                    for c in range(2):
                        dve.tensor_tensor(E.hshift[:, layer, c, :], m[:, c, 0:8], vecs[:, v0 + 8:v0 + 16], ALU.add)
                        ins = dve.tensor_tensor(E.hscale[:, layer, c, :], m[:, c, 8:16], vecs[:, v0 + 16:v0 + 24], ALU.add)
                    ins.then_inc(s_vecs, 1)
                    dve.wait_ge(s_vecs, 2 + layer)
                    for c in range(2):
                        ins = dve.scalar_tensor_tensor(E.hscale[:, layer, c, :], E.hscale[:, layer, c, :], 1.0,
                                                       vecs[:, v0:v0 + 8], ALU.add, ALU.mult)
                    ins.then_inc(s_mod, 1)

                def gate_rows(layer):
                    for h in range(2):
                        dve.wait_ge(s_gpe, 2 * layer + h + 1)
                        if h == 0:
                            dve.wait_ge(s_bias, 32 * (layer + 1))
                            if layer == 1:
                                dve.wait_ge(s_gst, 32)
                        dve.tensor_tensor(grow[:, h * 512:(h + 1) * 512], gateps[h][0:33, :],
                                          gbias[:, h * 512:(h + 1) * 512], ALU.add).then_inc(s_grow, 1)

                mods(0)
                gate_rows(0)
                mods(1)
                gate_rows(1)
                dve.wait_ge(s_mod, 1)

                def tile(n, j, i, last):
                    N.dve_normalise(dve, n, j)
                    N.dve_modulate(dve, n, j, 1 if last else 0)
                    N.dve_lo(dve, n, j)
                pair_loop(dve, tile)

            @block.tensor
            def _(pe):
                pe.sem_inc(N.s_tp, 2)
                pe.wait_ge(s_const, 96)
                pe.transpose(vecps[:, 0:48], vecrows[:, :], E.ident[0:48, 0:48]).then_inc(s_vec, 1)
                pe.wait_ge(s_ck, 64)
                for t in range(2):
                    for h in range(NKV):
                        ins = pe.transpose(E.bank[4 + t][:, h * P:(h + 1) * P],
                                           ckr[:, t, h, :, :].rearrange("p r d -> p (r d)"), E.ident[:, :])
                    ins.then_inc(s_ckt, 1)
                pe.wait_ge(s_silu, 7)
                for n in range(12):
                    layer, c = n // 6, n % 6
                    pe.wait_ge(s_ada[n % 2], 16 * (n // 2 + 1))
                    w = ada[n % 2]
                    if c < 4:
                        for b in range(4):
                            col = layer * 32 + (c * 4 + b) * 2
                            for k in range(KT):
                                ins = pe.matmul(modps[:, col:col + 2], w[:, k, b * P:(b + 1) * P], silu_c[:, k, :],
                                                start=(k == 0), stop=(k == KT - 1))
                        ins.then_inc(s_adause, 1)
                        if c == 3:
                            pe.wait_ge(s_adause, n + 1)
                            pe.sem_inc(s_modpe, 1)
                    else:
                        if layer == 1:
                            pe.wait_ge(s_grow, 2)
                        for k in range(KT):
                            ins = pe.matmul(gateps[c - 4][0:33, :], silu_pad[:, k, :], w[:, k, :],
                                            start=(k == 0), stop=(k == KT - 1))
                        ins.then_inc(s_gpe, 1)
                        pe.wait_ge(s_gpe, 2 * layer + c - 3)
                        pe.sem_inc(s_adause, 1)
                pe.wait_ge(s_ckc, 1)
                pair_loop(pe, lambda n, j, i, last: N.pe_transpose(pe, n, j))


class Projection:

    def __init__(self, E, ctx, tag, blocks_per_iter):
        nc = E.nc
        self.E, self.B = E, blocks_per_iter
        sb = lambda n, s, d=F32: ctx.enter_context(nc.sbuf_tensor(f"{tag}_{n}", s, d))
        sem = lambda n: E.semaphore(f"{tag}_{n}")
        self.raw = sb("w_raw", [P, KT, P])
        self.hi = sb("w_hi", [P, KT, P], F32R)
        self.lo = sb("w_lo", [P, KT, P], F32R)
        self.s_raw = sem("w_loaded")
        self.s_hi = sem("w_hi_ready")
        self.s_lo = sem("w_lo_ready")
        self.s_used = sem("w_half_used")
        self.s_unit = sem("unit_done")

    def sp_load(self, sp, n, pieces):
        sp.wait_ge(self.s_lo, at(n * 2))
        settle(self.E, sp)
        for c0, src in pieces:
            w = src.shape[-1]
            sp.dma_start(self.raw[:, :, c0:c0 + w], src).then_inc(self.s_raw, 16)

    def pool_hi(self, pool, n, loads):
        pool.wait_ge(self.s_raw, at(loads * 16))
        for half in range(2):
            pool.wait_ge(self.s_used, at(n * 2 + half + 1))
            settle(self.E, pool)
            k = slice(4 * half, 4 * half + 4)
            pool.tensor_copy(self.hi[:, k, :], self.raw[:, k, :]).then_inc(self.s_hi, 1)

    def dve_lo(self, dve, n):
        for half in range(2):
            dve.wait_ge(self.s_hi, at(n * 2 + half + 1))
            k = slice(4 * half, 4 * half + 4)
            dve.tensor_tensor(self.lo[:, k, :], self.raw[:, k, :], self.hi[:, k, :],
                              ALU.subtract).then_inc(self.s_lo, 1)

    def pe_unit(self, pe, n, g, bank):
        E = self.E
        t0, t1 = GROUPS[g]
        tok = slice(t0 * P, t1 * P)
        out = bank[:, 0:(t1 - t0) * P]
        for k in range(KT):
            if g == 0 and k % 4 == 0:
                pe.wait_ge(self.s_lo, at(n * 2 + k // 4 + 1))
            pe.matmul(out, self.lo[:, k, :], E.h_hi[:, k, tok], start=(k == 0), stop=False)
            pe.matmul(out, self.hi[:, k, :], E.h_lo[:, k, tok], start=False, stop=False)
            ins = pe.matmul(out, self.hi[:, k, :], E.h_hi[:, k, tok], start=False, stop=(k == KT - 1))
            if g == NG - 1 and k == 3:
                ins.then_inc(self.s_used, 1)
        ins.then_inc(self.s_unit, 1)
        if g == NG - 1:
            pe.wait_ge(self.s_unit, at(n * NG + g + 1))
            pe.sem_inc(self.s_used, 1)


def phase_attn(E):
    nc = E.nc
    SWAP = [(p + 16) % 32 for p in range(32)]
    with ExitStack() as ctx:
        sb = lambda n, s, d=F32: ctx.enter_context(nc.sbuf_tensor(n, s, d))
        sem = lambda n: E.semaphore(n)
        kT = sb("kT", [P, KCOLS])
        vS = sb("vS", [P, VTILES, 2, HD])
        qT = sb("qT", [P, T])
        gT = sb("gT", [P, T])
        cs = [sb(f"cs{b}", [P, 2, 512]) for b in range(2)]
        shuf = [sb(f"shuf{b}", [P, 512]) for b in range(2)]
        prob = [sb(f"prob{b}", [P, 640]) for b in range(4)]
        gexp = prob[0:2]
        probT = [sb(f"probT{b}", [P, 5, 2, P]) for b in range(2)]
        sink = sb("sink", [P, NHEAD])
        nsink = sb("nsink", [P, NHEAD])
        mx = sb("mx", [P, 2])
        negm = sb("negm", [P, 2, 2])
        rsum = sb("rsum", [P, 2, 2])
        sarg = sb("sarg", [P, 2, 2])
        esink = sb("esink", [P, 2, 2])
        den = sb("den", [P, 2, 2])
        rden = sb("rden", [P, 2, 2])
        kvout = sb("kvout", [P, 2, HD])

        J = Projection(E, ctx, "attn", 5)
        s_cs = [sem(f"rotary_loaded{b}") for b in range(2)]
        (s_shuf, s_cos, s_rope, s_gexp, s_gden, s_release, s_kdup, s_vT, s_vS, s_kvo, s_kvst, s_ckl, s_cvl,
         s_const, s_pad, s_sin) = (sem(x) for x in (
            "shuffled", "times_cos", "rotated", "gate_exp", "gate_denominator", "proj_bank_free", "k_doubled",
            "v_turned", "v_stored", "kv_out_ready", "kv_out_stored", "cached_k_loaded", "cached_v_loaded",
            "sink_loaded", "pads_zero", "times_sin"))
        s_pTc2 = sem("probsT_last_ready")
        (s_S, s_mx, s_nm, s_p, s_pn, s_pT, s_pTc, s_pv, s_sarg, s_es, s_den, s_rd, s_og, s_ogst) = (
            sem(x) for x in ("scores", "row_max", "neg_max", "probs", "probs_normalised", "probs_turned",
                             "probsT_ready", "pv_done", "sink_minus_max", "sink_exp", "denominator", "recip_den",
                             "o_gated", "o_stored"))
        w_in = E.a["attn_w_in"][0].rearrange("(k p) m -> p k m", p=P)

        NU = 2 * NT
        kinds = ["kv", "q", "g", "q", "g"]
        ROPES = 3 * NG

        def scores_of(w):
            pair = E.PS[:, 2 * (w % 2):2 * (w % 2) + 2, :].rearrange("p a n -> p (a n)")
            return pair[:, 256:896] if w // 2 < CTX else pair[:, 512:512 + P]

        def lat_ctx(g):
            t0, t1 = GROUPS[g]
            lat = min(t1, NS) - t0
            return t0 * P, lat * P, (t1 - t0) * P - lat * P

        E.start_at_one()
        with nc.Block() as block:
            @block.sync
            def _(sp):
                sp.dma_start(sink[:, :], E.a["attn_sink"].partition_broadcast(P)).then_inc(s_const, 16)
                with sp.Fori(0, NKV) as kv:
                    rope = 0

                    def load_weights(m):
                        if kinds[m] == "kv":
                            pieces = [(0, w_in[:, :, ds(kv * HD + 2 * D, HD)]),
                                      (HD, w_in[:, :, ds(kv * HD + 2 * D + NKV * HD, HD)])]
                        else:
                            col = (0 if kinds[m] == "q" else D) + (m - 1) // 2 * P
                            pieces = [(0, w_in[:, :, ds(kv * (2 * P) + col, P)])]
                        J.sp_load(sp, kv * 5 + m, pieces)

                    load_weights(0)
                    for m, kind in enumerate(kinds):
                        if m < 4:
                            load_weights(m + 1)
                        if kind == "kv":
                            sp.wait_ge(s_S, at(kv * (2 * NU)))
                            settle(E, sp)
                            with nc.allow_non_contiguous_dma(reason="rows of one head"):
                                sp.dma_start(kT[:, 0:PAST], E.ckt_dram[:, ds(kv * PAST, PAST)]).then_inc(s_ckl, 16)
                                sp.wait_ge(s_pv, at(kv * (2 * NT)))
                                settle(E, sp)
                                for copy in range(2):
                                    sp.dma_start(vS[:, 0:2, copy, :], E.cache_v[:, :, ds(kv * HD, HD)]).then_inc(s_cvl, 16)
                        if kind != "g":
                            for g in range(NG):
                                t0, wl, wc = lat_ctx(g)
                                b = rope % 2
                                if rope >= 2:
                                    sp.wait_ge(s_rope, at(kv * ROPES + rope - 1))
                                else:
                                    sp.wait_ge(s_rope, at(kv * ROPES))
                                sp.dma_start(cs[b][:, :, 0:wl], E.a["rotary"][:, :, t0:t0 + wl]).then_inc(s_cs[b], 16)
                                rope += 1
                        if kind == "kv":
                            sp.wait_ge(s_kvo, at(kv * 2 + 2))
                            settle(E, sp)
                            with nc.allow_non_contiguous_dma(reason="rows of one head"):
                                sp.dma_start(E.new_k[:, ds(kv * HD, HD)], kvout[:, 0, :]).then_inc(s_kvst, 16)
                                sp.dma_start(E.new_v[:, ds(kv * HD, HD)], kvout[:, 1, :]).then_inc(s_kvst, 16)
                        if kind == "g":
                            sub = m // 2 - 1
                            sp.wait_ge(s_og, at(kv * (2 * NT) + (sub + 1) * NT))
                            sp.dma_start(E.ogT_dram[ds(kv * 2 + sub, 1), :, :].rearrange("a p t -> (a p) t"), gT[:, :]).then_inc(s_ogst, 16)
                sp.wait_ge(s_ogst, at(16 * 2 * NKV))
                sp.wait_ge(s_kvst, at(32 * NKV))

            @block.gpsimd
            def _(pool):
                pool.memset(kT[:, KPAD:KPAD + P], 0.0).then_inc(s_pad, 1)
                pool.memset(kT[:, KREQ - P:KREQ], 0.0).then_inc(s_pad, 1)
                pool.memset(vS[:, KPAD // P, :, :], 0.0).then_inc(s_pad, 1)
                pool.memset(vS[:, KREQ // P - 1, :, :], 0.0).then_inc(s_pad, 1)
                with pool.Fori(0, NKV) as kv:
                    rope = 0
                    J.pool_hi(pool, kv * 5, kv * 6 + 2)
                    for m, kind in enumerate(kinds):
                        if kind == "g":
                            if m < 4:
                                J.pool_hi(pool, kv * 5 + m + 1, kv * 6 + m + 3)
                            base = kv * (2 * NU) + (m // 2 - 1) * NU
                            bbase = kv * (2 * NT) + (m // 2 - 1) * NT
                            for w in range(NU):
                                b, hh = w // 2, w % 2
                                pool.wait_ge(s_rd, at(bbase + b + 1))
                                settle(E, pool)
                                x = prob[w % 4][:, 0:(640 if b < CTX else P)]
                                pool.tensor_scalar(x, x, rden[:, b % 2, hh:hh + 1], None, ALU.mult).then_inc(s_pn, 1)
                            continue
                        rows, dst, off = (HD, kT, KLAT) if kind == "kv" else (P, qT, 0)
                        for g in range(NG):
                            t0, wl, wc = lat_ctx(g)
                            b = rope % 2
                            if g == NG - 1:
                                J.pool_hi(pool, kv * 5 + m + 1, kv * 6 + m + 3)
                            pool.wait_ge(s_shuf, at(kv * ROPES + rope + 1))
                            pool.wait_ge(s_cos, at(kv * ROPES + rope + 1))
                            prod = pool.tensor_tensor(shuf[b][0:rows, 0:wl], shuf[b][0:rows, 0:wl],
                                                      cs[b][0:rows, 1, 0:wl], ALU.mult)
                            prod.then_inc(s_sin, 1)
                            pool.wait_ge(s_sin, at(kv * ROPES + rope + 1))
                            o = dst[0:rows, off + t0:off + t0 + wl]
                            pool.tensor_tensor(o, o, shuf[b][0:rows, 0:wl], ALU.add).then_inc(s_rope, 1)
                            rope += 1

            @block.scalar
            def _(act):
                act.wait_ge(s_const, at(16))
                act.mul(nsink[:, :], sink[:, :], -1.0).then_inc(s_const, 1)
                with act.Fori(0, NKV) as kv:
                    for g in range(NG):
                        t0, wl, wc = lat_ctx(g)
                        act.wait_ge(s_rope, at(kv * ROPES + g + 1))
                        if wc:
                            act.wait_ge(s_release, at(kv * (5 * NG) + NG))
                        ins = act.copy(kT[HD:P, KLAT + t0:KLAT + t0 + wl], kT[0:HD, KLAT + t0:KLAT + t0 + wl])
                        if wc:
                            act.copy(kT[HD:P, KREQ:KREQ + P], kT[0:HD, KREQ:KREQ + P]).then_inc(s_kdup, 1)
                        else:
                            ins.then_inc(s_kdup, 1)
                    act.wait_ge(s_pv, at(kv * (2 * NT)))
                    for r, (a, z) in enumerate(VGROUPS):
                        act.wait_ge(s_vT, at(kv * 4 + r + 1))
                        n_lat = min(z, NS) - a
                        src = E.bank[4 + r][:, 0:(z - a) * HD].rearrange("p (t d) -> p t d", d=HD)
                        twice = lambda x, n: x.unsqueeze(2).to_broadcast([P, n, 2, HD])
                        if n_lat:
                            ins = act.copy(vS[:, VT_LAT + a:VT_LAT + a + n_lat, :, :], twice(src[:, 0:n_lat, :], n_lat))
                        if z > NS:
                            ins = act.copy(vS[:, VT_REQ:VT_REQ + 1, :, :], twice(src[:, CTX - a:CTX - a + 1, :], 1))
                        ins.then_inc(s_vS, 1)
                    act.wait_ge(s_kvst, at(kv * 32))
                    act.wait_ge(s_vT, at(kv * 4 + 4))
                    act.copy(kvout[:, 0, :], E.bank[7][:, 0:HD]).then_inc(s_kvo, 1)
                    act.copy(kvout[:, 1, :], E.bank[6][:, 0:HD]).then_inc(s_kvo, 1)
                    for sub in range(2):
                        for g in range(NG):
                            t0, t1 = GROUPS[g]
                            w = (t1 - t0) * P
                            u = NG * (2 + 2 * sub) + g
                            e = (sub * NG + g) % 2
                            act.wait_ge(J.s_unit, at(kv * (5 * NG) + u + 1))
                            act.wait_ge(s_release, at(kv * (5 * NG) + u - 1))
                            act.activation(gexp[e][:, 0:w], E.bank[u % 4][:, 0:w], ACT.Exp, scale=-1.0).then_inc(s_gexp, 1)
                        base = kv * (2 * NU) + sub * NU
                        bbase = kv * (2 * NT) + sub * NT

                        def sink_exp(b):
                            act.wait_ge(s_sarg, at(bbase + b + 1))
                            act.activation(esink[:, b % 2, :], sarg[:, b % 2, :], ACT.Exp).then_inc(s_es, 1)

                        def pT_copy(w):
                            b, hh = w // 2, w % 2
                            act.wait_ge(s_pT, at(base + w + 1))
                            if b < CTX:
                                act.wait_ge(s_pv, at(bbase + (b - 1 if b >= 2 else 0)))
                                act.copy(probT[b % 2][:, 3:5, hh, :],
                                         E.bank[5][:, 0:2 * P].rearrange("p (t q) -> p t q", t=2)).then_inc(s_pTc2, 1)
                            else:
                                act.sem_inc(s_pTc2, 1)

                        for s in range(NU + 3):
                            if s < NU:
                                w = s
                                b, hh = w // 2, w % 2
                                act.wait_ge(s_nm, at(base + w + 1))
                                act.wait_ge(s_pT, at(base + (w - 3 if w >= 4 else 0)))
                                act.wait_ge(s_den, at(bbase + (b - 1 if b >= 2 else 0)))
                                n = 640 if b < CTX else P
                                act.activation(prob[w % 4][:, 0:n], scores_of(w), ACT.Exp,
                                               bias=negm[:, b % 2, hh:hh + 1], scale=HD ** -0.5,
                                               accum_out=rsum[:, b % 2, hh:hh + 1]).then_inc(s_p, 1)
                                if hh == 1:
                                    sink_exp(b)
                            if s >= 3:
                                pT_copy(s - 3)

            @block.vector
            def _(dve):
                dve.wait_ge(s_const, at(17))

                def rope_unit(kv, rope, u, rows, dst, off, req, g):
                    t0, wl, wc = lat_ctx(g)
                    b = rope % 2
                    bank = E.bank[u % 4]
                    dve.wait_ge(J.s_unit, at(kv * (5 * NG) + u + 1))
                    dve.wait_ge(s_rope, at(kv * ROPES + (rope - 1 if rope >= 2 else 0)))
                    settle(E, dve)
                    dve.stream_shuffle(shuf[b][0:rows, 0:wl], bank[0:rows, 0:wl], SWAP).then_inc(s_shuf, 1)
                    dve.wait_ge(s_cs[b], at(kv * (16 * (8 - b)) + 16 * (rope // 2 + 1)))
                    ins = dve.tensor_tensor(dst[0:rows, off + t0:off + t0 + wl], bank[0:rows, 0:wl],
                                            cs[b][0:rows, 0, 0:wl], ALU.mult)
                    ins.then_inc(s_cos, 1)
                    if wc:
                        ins = dve.tensor_copy(dst[0:rows, req:req + P], bank[0:rows, wl:wl + P])
                    return ins

                with dve.Fori(0, NKV) as kv:
                    J.dve_lo(dve, kv * 5)
                    rope = 0
                    for m, kind in enumerate(kinds):
                        for g in range(NG):
                            u = NG * m + g
                            t0, t1 = GROUPS[g]
                            w = (t1 - t0) * P
                            tok = slice(t0 * P, t1 * P)
                            if g == NG - 1 and m < 4:
                                J.dve_lo(dve, kv * 5 + m + 1)
                            if kind == "kv":
                                if g == 0:
                                    dve.wait_ge(s_ogst, at(kv * 32))
                                    dve.wait_ge(s_S, at(kv * (2 * NU)))
                                rope_unit(kv, rope, u, HD, kT, KLAT, KREQ, g)
                                dve.tensor_copy(gT[HD:P, tok], E.bank[u % 4][HD:P, 0:w]).then_inc(s_release, 1)
                                rope += 1
                            elif kind == "q":
                                if g == 0 and m == 3:
                                    dve.wait_ge(s_S, at(kv * (2 * NU) + NU))
                                ins = rope_unit(kv, rope, u, P, qT, 0, CTX * P, g)
                                if lat_ctx(g)[2]:
                                    ins.then_inc(s_release, 1)
                                else:
                                    dve.wait_ge(s_cos, at(kv * ROPES + rope + 1))
                                    dve.sem_inc(s_release, 1)
                                rope += 1
                            else:
                                e = ((m // 2 - 1) * NG + g) % 2
                                if g == 0 and m == 2:
                                    dve.wait_ge(s_vT, at(kv * 4 + 4))
                                if g == 0 and m == 4:
                                    dve.wait_ge(s_ogst, at(kv * 32 + 16))
                                k = kv * (2 * NG) + (m // 2 - 1) * NG + g
                                dve.wait_ge(s_gexp, at(k + 1))
                                dve.tensor_scalar(gexp[e][:, 0:w], gexp[e][:, 0:w], 1.0, None, ALU.add).then_inc(s_gden, 1)
                                dve.wait_ge(s_gden, at(2 * k + 1))
                                dve.reciprocal(gexp[e][:, 0:w], gexp[e][:, 0:w]).then_inc(s_gden, 1)
                                dve.wait_ge(s_gden, at(2 * k + 2))
                                dve.tensor_tensor(gT[:, tok], E.bank[u % 4][:, 0:w], gexp[e][:, 0:w], ALU.mult).then_inc(s_release, 1)
                        if m not in (2, 4):
                            continue
                        sub = m // 2 - 1
                        base = kv * (2 * NU) + sub * NU
                        bbase = kv * (2 * NT) + sub * NT

                        def softmax_max(w):
                            b, hh = w // 2, w % 2
                            head = kv * 4 + (2 * sub + hh)
                            dve.wait_ge(s_S, at(base + w + 1))
                            dve.tensor_reduce(mx[:, w % 2:w % 2 + 1], scores_of(w), AX.X, ALU.max).then_inc(s_mx, 1)
                            dve.wait_ge(s_mx, at(base + w + 1))
                            dve.wait_ge(s_p, at(base + (2 * b - 2 if b >= 2 else 0)))
                            dve.wait_ge(s_sarg, at(bbase + (b - 1 if b >= 2 else 0)))
                            dve.tensor_scalar(negm[:, b % 2, hh:hh + 1], mx[:, w % 2:w % 2 + 1], -(HD ** -0.5),
                                              nsink[:, ds(head, 1)], ALU.mult, ALU.min).then_inc(s_nm, 1)
                            if hh == 1:
                                dve.wait_ge(s_nm, at(base + w + 1))
                                dve.wait_ge(s_es, at(bbase + (b - 1 if b >= 2 else 0)))
                                dve.tensor_tensor(sarg[:, b % 2, :], negm[:, b % 2, :],
                                                  sink[:, ds(kv * 4 + 2 * sub, 2)], ALU.add).then_inc(s_sarg, 1)

                        def pT_copy(w):
                            b, hh = w // 2, w % 2
                            dve.wait_ge(s_pT, at(base + w + 1))
                            dve.wait_ge(s_pv, at(bbase + (b - 1 if b >= 2 else 0)))
                            n = 3 if b < CTX else 1
                            dve.tensor_copy(probT[b % 2][:, 0:n, hh, :],
                                            E.bank[4][:, 0:n * P].rearrange("p (t q) -> p t q", t=n)).then_inc(s_pTc, 1)

                        def denominators(b):
                            p = b % 2
                            dve.wait_ge(s_p, at(base + 2 * b + 2))
                            dve.wait_ge(s_es, at(bbase + b + 1))
                            dve.tensor_tensor(den[:, p, :], rsum[:, p, :], esink[:, p, :], ALU.add).then_inc(s_den, 1)
                            dve.wait_ge(s_den, at(bbase + b + 1))
                            dve.wait_ge(s_pn, at(base + (2 * b - 2 if b >= 2 else 0)))
                            dve.reciprocal(rden[:, p, :], den[:, p, :]).then_inc(s_rd, 1)

                        def gate(b):
                            dve.wait_ge(s_pv, at(bbase + b + 1))
                            for hh in range(2):
                                g = gT[HD * hh:HD * hh + HD, b * P:(b + 1) * P]
                                ins = dve.tensor_tensor(g, E.bank[6 + b % 2][HD * hh:HD * hh + HD, hh * P:(hh + 1) * P],
                                                        g, ALU.mult)
                            ins.then_inc(s_og, 1)

                        for s in range(NU + 5):
                            if s < NU:
                                softmax_max(s)
                            if s >= 2 and s % 2 == 0 and (s - 2) // 2 < NT:
                                denominators((s - 2) // 2)
                            if 3 <= s < NU + 3:
                                pT_copy(s - 3)
                            if s >= 6 and s % 2 == 0:
                                gate((s - 6) // 2)

            @block.tensor
            def _(pe):
                pe.sem_inc(J.s_used, 2)
                pe.wait_ge(s_pad, at(4))
                with pe.Fori(0, NKV) as kv:
                    for m, kind in enumerate(kinds):
                        for g in range(NG):
                            u = NG * m + g
                            if u >= 4:
                                pe.wait_ge(s_release, at(kv * (5 * NG) + u - 3))
                            if u < 4 and m == 0:
                                pe.wait_ge(s_p, at(kv * (2 * NU)))
                            if m == 3:
                                pe.wait_ge(s_p, at(kv * (2 * NU) + NU))
                            J.pe_unit(pe, kv * 5 + m, g, E.bank[u % 4])
                        if kind == "kv":
                            pe.wait_ge(s_release, at(kv * (5 * NG) + NG))
                            pe.wait_ge(s_og, at(kv * (2 * NT)))
                            pe.wait_ge(s_pTc, at(kv * (2 * NU)))
                            pe.wait_ge(s_pTc2, at(kv * (2 * NU)))
                            settle(E, pe)
                            for r, (a, z) in enumerate(VGROUPS):
                                for t in range(a, z):
                                    ins = pe.transpose(E.bank[4 + r][:, (t - a) * HD:(t - a + 1) * HD],
                                                       gT[HD:P, t * P:(t + 1) * P], E.ident[HD:P, HD:P])
                                ins.then_inc(s_vT, 1)
                            pe.wait_ge(s_kdup, at(kv * NG + NG))
                            pe.transpose(E.bank[7][:, 0:P], kT[:, KREQ:KREQ + P], E.ident[:, :]).then_inc(s_vT, 1)
                        if m not in (2, 4):
                            continue
                        sub = m // 2 - 1
                        base = kv * (2 * NU) + sub * NU
                        bbase = kv * (2 * NT) + sub * NT
                        pe.wait_ge(s_rope, at(kv * ROPES + NG * (2 + sub)))
                        pe.wait_ge(s_release, at(kv * (5 * NG) + NG * (m + 1)))
                        if sub == 0:
                            pe.wait_ge(s_kdup, at(kv * NG + NG))
                            pe.wait_ge(s_vS, at(kv * 3 + 3))
                            pe.wait_ge(s_kvo, at(kv * 2 + 2))
                            pe.wait_ge(s_ckl, at(kv * 16 + 16))
                            pe.wait_ge(s_cvl, at(kv * 32 + 32))

                        def scores(w):
                            b, hh = w // 2, w % 2
                            if w >= 2:
                                pe.wait_ge(s_p, at(base + w - 1))
                            r = slice(HD * hh, HD * hh + HD)
                            q = qT[r, b * P:(b + 1) * P]
                            s0, s1 = E.bank[2 * (w % 2)], E.bank[2 * (w % 2) + 1]
                            if b == CTX:
                                pe.matmul(s1[:, 0:P], q, kT[r, KREQ:KREQ + P], start=True, stop=True).then_inc(s_S, 1)
                                return
                            mask = 0 if b == 0 else 2 if b == NS - 1 else 1
                            k0 = KLAT + (b - 1) * P
                            pe.matmul(s0[:, 256:512], q, kT[r, 0:PAST], start=True, stop=True)
                            pe.matmul(s1[:, 0:3 * P], q, kT[r, k0:k0 + 3 * P], start=True, stop=False)
                            pe.matmul(s1[:, 0:3 * P], E.identb[:, :], E.wmask[:, mask, :], start=False,
                                      stop=True).then_inc(s_S, 1)

                        def turn(w):
                            b = w // 2
                            pe.wait_ge(s_pn, at(base + w + 1))
                            if w >= 1:
                                pe.wait_ge(s_pTc, at(base + w))
                                pe.wait_ge(s_pTc2, at(base + w))
                            for t in range(5 if b < CTX else 1):
                                out = E.bank[4 + t // 3][:, (t % 3) * P:(t % 3 + 1) * P]
                                ins = pe.transpose(out, prob[w % 4][:, t * P:(t + 1) * P], E.ident[:, :])
                            ins.then_inc(s_pT, 1)

                        def pv(b):
                            pe.wait_ge(s_pTc, at(base + 2 * b + 2))
                            pe.wait_ge(s_pTc2, at(base + 2 * b + 2))
                            pe.wait_ge(s_og, at(bbase + (b - 1 if b >= 2 else 0)))
                            tiles = [0, 1] + [VT_LAT + b + x for x in (-1, 0, 1)] if b < CTX else [VT_REQ]
                            for t, v in enumerate(tiles):
                                ins = pe.matmul(E.bank[6 + b % 2][:, 0:2 * P], vS[:, v, :, :].rearrange("p a d -> p (a d)"),
                                                probT[b % 2][:, t, :, :].rearrange("p h q -> p (h q)"),
                                                start=(t == 0), stop=(t == len(tiles) - 1))
                            ins.then_inc(s_pv, 1)

                        for s in range(NU + 4):
                            if s < NU:
                                scores(s)
                            if s >= 5 and s % 2 == 1:
                                pv((s - 5) // 2)
                            if 3 <= s < NU + 3:
                                turn(s - 3)


def phase_out(E, layer):
    nc = E.nc
    last_layer = layer == 1
    with ExitStack() as ctx:
        sb = lambda n, s, d=F32: ctx.enter_context(nc.sbuf_tensor(f"{n}_out{layer}", s, d))
        sem = lambda n: E.semaphore(f"{n}_out{layer}")
        w = sb("w", [P, KT, D])
        og = [sb(f"og{j}", [P, KT, P]) for j in range(2)]
        xb = [sb(f"xb{j}", [P, D]) for j in range(2)]
        scaled = sb("scaled", [P, D])
        gbc = sb("gbc", [P, D])
        s_w = [sem(f"w_loaded{half}") for half in range(2)]
        s_fw, s_g, s_y, s_t, s_x1 = (sem(x) for x in (
            "final_weight_loaded", "gate_loaded", "y_done", "y_gated", "residual_added"))
        s_og = [sem(f"og_loaded{j}") for j in range(2)]
        s_x = [sem(f"x_loaded{j}") for j in range(2)]
        s_st = [sem(f"stored{j}") for j in range(2)]
        if last_layer:
            w_hi, w_lo = sb("w_hi", [P, KT, D], F32R), sb("w_lo", [P, KT, D], F32R)
            og_hi = [sb(f"og_hi{j}", [P, KT, P], F32R) for j in range(2)]
            og_lo = [sb(f"og_lo{j}", [P, KT, P], F32R) for j in range(2)]
            fw = sb("fw", [P, D])
            y = [sb(f"y{j}", [P, D]) for j in range(2)]
            ss, std, rs = sb("ss", [P, 2]), sb("std", [P, 2]), sb("rs", [P, 2])
            s_whi, s_wlo, s_oghi, s_oglo, s_sq, s_std, s_rs, s_xn, s_junk = (sem(x) for x in (
                "w_hi_ready", "w_lo_ready", "og_hi_ready", "og_lo_ready", "sum_of_squares",
                "root_mean_square", "rms_reciprocal", "normalised", "junk"))
            x_read = s_xn

        def residual_ready(eng, n, j):
            eng.wait_ge(s_x1, over(n))

        if not last_layer:
            N = NormTranspose(E, ctx, 1, xb, residual_ready)
            x_read = N.s_xn
        def split_hi(act, n, j, i):
            act.wait_ge(s_og[j], i * 16 + 16)
            act.wait_ge(s_y, free(n))
            act.copy(og_hi[j][:, :, :], og[j][:, :, :]).then_inc(s_oghi, 1)

        def split_lo(dve, n, j):
            dve.wait_ge(s_oghi, over(n))
            dve.tensor_tensor(og_lo[j][:, :, :], og[j][:, :, :], og_hi[j][:, :, :], ALU.subtract).then_inc(s_oglo, 1)

        ybank = [E.PS[:, 0:2, :], E.PS[:, 2:4, :]]
        w_out = (E.a["mlstm_w_out"] if last_layer else E.a["attn_w_out"])[0]

        with nc.Block() as block:
            @block.sync
            def _(sp):
                for half in range(2):
                    k = slice(4 * half, 4 * half + 4)
                    sp.dma_start(w[:, k, :], w_out.rearrange("(k p) m -> p k m", p=P)[:, k, :]).then_inc(s_w[half], 16)
                sp.dma_start(gbc[:, :], E.gates_dram[layer, 0:1, :].partition_broadcast(P)).then_inc(s_g, 16)
                if last_layer:
                    sp.dma_start(fw[:, :], E.a["final_norm_w"].rearrange("(a n) -> a n", a=1).partition_broadcast(P)).then_inc(s_fw, 16)

                for s in s_st:
                    sp.sem_inc(s, 1)

                def tile(n, j, i, last):
                    sp.wait_ge(s_oglo if last_layer else s_y, free(n))
                    settle(E, sp)
                    with nc.allow_non_contiguous_dma(reason="512-byte rows"):
                        sp.dma_start(og[j][:, :, :], E.ogT_dram[:, :, ds(n * P, P)].rearrange("k p t -> p k t")).then_inc(s_og[j], 16)
                    sp.wait_ge(x_read, free(n))
                    settle(E, sp)
                    sp.wait_ge(s_st[j], i * 16 + 1)
                    settle(E, sp)
                    if last_layer:
                        src = E.x1_dram[ds(n * P, P), :]
                    else:
                        src = E.a["x_prompt"][0] if last else E.x_tile(n)
                    sp.dma_start(xb[j][:, :], src).then_inc(s_x[j], 16)
                    if last:
                        sp.wait_ge(s_t, over(NS - 1))
                        sp.dma_start(gbc[:, :], E.gates_dram[layer, 1:2, :].partition_broadcast(P)).then_inc(s_g, 16)
                pair_loop(sp, tile)
                sp.wait_ge(s_st[0], 16 * (NS // 2 + 1) + 1)
                sp.wait_ge(s_st[1], 16 * (NS // 2) + 1)

            @block.gpsimd
            def _(pool):
                pool.sem_inc(s_x1, 2)
                if not last_layer:
                    pool.sem_inc(N.s_hi, 2)

                def tile(n, j, i, last):
                    pool.wait_ge(s_t, over(n))
                    pool.wait_ge(s_x[j], i * 16 + 16)
                    pool.tensor_tensor(xb[j][:, :], xb[j][:, :], scaled[:, :], ALU.add).then_inc(s_x1, 1)
                    if not last_layer:
                        N.pool_hi(pool, n, j)
                pair_loop(pool, tile)

            @block.scalar
            def _(act):
                if last_layer:
                    for s in (s_sq, s_std, s_oghi):
                        act.sem_inc(s, 2)
                    for k in range(KT):
                        if k % 4 == 0:
                            act.wait_ge(s_w[k // 4], 16)
                        act.copy(w_hi[:, k, :], w[:, k, :]).then_inc(s_whi, 1)
                        if k == 0:
                            split_hi(act, 0, 0, 0)
                else:
                    N.credits_act(act)

                def tile(n, j, i, last):
                    if last_layer and not last:
                        split_hi(act, n + 1, 1 - j, i + j)
                    residual_ready(act, n, j)
                    if not last_layer:
                        act.dma_start(E.x1_dram[ds(n * P, P), :], xb[j][:, :]).then_inc(s_st[j], 16)
                        N.act_stats(act, n, j)
                        N.act_modulate(act, n, j, 1 if last else 0)
                        return
                    act.wait_ge(s_xn, free(n))
                    act.wait_ge(s_st[j], i * 16 + 1)
                    act.activation(y[j][:, :], xb[j][:, :], ACT.Square, accum_out=ss[:, j:j + 1]).then_inc(s_sq, 1)
                    act.wait_ge(s_sq, over(n))
                    act.wait_ge(s_rs, free(n))
                    act.activation(std[:, j:j + 1], ss[:, j:j + 1], ACT.Sqrt, bias=E.eps[:, 0:1],
                                   scale=1.0 / D).then_inc(s_std, 1)
                    act.wait_ge(s_xn, over(n))
                    act.dma_start(E.out_prompt if last else E.out_sample[ds(n * P, P), :], y[j][:, :]).then_inc(s_st[j], 16)
                pair_loop(act, tile)

            @block.vector
            def _(dve):
                dve.sem_inc(s_t, 2)
                if last_layer:
                    for s in (s_oglo, s_rs, s_xn):
                        dve.sem_inc(s, 2)
                    for k in range(KT):
                        dve.wait_ge(s_whi, k + 1)
                        dve.tensor_tensor(w_lo[:, k, :], w[:, k, :], w_hi[:, k, :], ALU.subtract).then_inc(s_wlo, 1)
                        if k == 0:
                            split_lo(dve, 0, 0)
                    dve.wait_ge(s_fw, 16)
                else:
                    N.credits_dve(dve)

                def tile(n, j, i, last):
                    if last_layer and not last:
                        split_lo(dve, n + 1, 1 - j)
                    dve.wait_ge(s_y, over(n))
                    dve.wait_ge(s_g, 32 if last else 16)
                    dve.wait_ge(s_x1, free(n + 1))
                    dve.tensor_tensor(scaled[:, :].rearrange("p (a n) -> p a n", a=2), ybank[j],
                                      gbc[:, :].rearrange("p (a n) -> p a n", a=2), ALU.mult).then_inc(s_t, 1)
                    if not last_layer:
                        N.dve_normalise(dve, n, j)
                        N.dve_modulate(dve, n, j, 1 if last else 0)
                        N.dve_lo(dve, n, j)
                        return
                    dve.wait_ge(s_std, over(n))
                    dve.wait_ge(s_xn, free(n))
                    dve.reciprocal(rs[:, j:j + 1], std[:, j:j + 1]).then_inc(s_rs, 1)
                    dve.wait_ge(s_rs, over(n))
                    dve.wait_ge(s_sq, over(n))
                    dve.scalar_tensor_tensor(y[j][:, :], xb[j][:, :], rs[:, j:j + 1], fw[:, :],
                                             ALU.mult, ALU.mult).then_inc(s_xn, 1)
                pair_loop(dve, tile)

            @block.tensor
            def _(pe):
                pe.sem_inc(s_y, 2)
                if not last_layer:
                    pe.sem_inc(N.s_tp, 2)
                    pe.wait_ge(s_w[0], 16)
                    pe.wait_ge(s_w[1], 16)
                else:
                    pe.wait_ge(s_wlo, KT)

                def products(n, j, i):
                    if last_layer:
                        pe.wait_ge(s_oglo, over(n))
                    else:
                        pe.wait_ge(s_og[j], i * 16 + 16)
                    pe.wait_ge(s_t, free(n))
                    for half in range(2):
                        out = E.bank[2 * j + half][:, :]
                        c = slice(half * 512, half * 512 + 512)
                        for k in range(KT):
                            first, end = k == 0, k == KT - 1
                            if last_layer:
                                pe.matmul(out, og_lo[j][:, k, :], w_hi[:, k, c], start=first, stop=False)
                                pe.matmul(out, og_hi[j][:, k, :], w_lo[:, k, c], start=False, stop=False)
                                ins = pe.matmul(out, og_hi[j][:, k, :], w_hi[:, k, c], start=False, stop=end)
                            else:
                                ins = pe.matmul(out, og[j][:, k, :], w[:, k, c], start=first, stop=end)
                    ins.then_inc(s_y, 1)

                if last_layer:
                    pair_loop(pe, lambda n, j, i, last: products(n, j, i))
                else:
                    products(0, 0, 0)
                    with pe.Fori(0, NS // 2) as i:
                        products(i * 2 + 1, 1, i)
                        N.pe_transpose(pe, i * 2, 0)
                        products(i * 2 + 2, 0, i + 1)
                        N.pe_transpose(pe, i * 2 + 1, 1)
                    N.pe_transpose(pe, CTX, 0)


FWD, BWD = 0, 32
ROWS = 64
U_COL, WK_COL, EM_COL = 0, 1, 2


def reversed_cols(tile, width, p0, rows, first, n):
    return bass.AP(tensor=tile[:, :].tensor, offset=p0 * width + first + n - 1, ap=[[width, rows], [-1, n]])


def phase_gates(E):
    nc = E.nc
    with ExitStack() as ctx:
        sb = lambda n, s, d=F32: ctx.enter_context(nc.sbuf_tensor(f"gt_{n}", s, d))
        sem = lambda n: E.semaphore(f"gt_{n}")
        raw, w_hi, w_lo = sb("w", [P, KT, P]), sb("w_hi", [P, KT, P], F32R), sb("w_lo", [P, KT, P], F32R)
        bias = sb("bias", [P, 1])
        nat4 = sb("nat4", [P, 512])
        ig, lf, b, M, tmp, z, r = (sb(n, [ROWS, T]) for n in ("ig", "lf", "b", "M", "tmp", "z", "r"))
        entry, last_M, dec, m_out = sb("entry", [ROWS, NT]), sb("last_M", [ROWS, NT]), sb("dec", [ROWS, NT]), sb("m_out", [ROWS, 1])
        s_zero, s_w, s_hi, s_lo, s_unit, s_nat, s_spread, s_m0, s_d, s_a, s_dma, s_tr, s_col = (
            sem(x) for x in ("zeroed", "w_loaded", "w_hi", "w_lo", "unit", "biased", "spread", "m0_loaded",
                             "dve_step", "act_step", "rows_stored", "turned", "columns"))
        w_in = E.a["mlstm_w_in"][0].rearrange("(k p) m -> p k m", p=P)
        chunks = lambda t: t[:, :].rearrange("p (c t) -> p c t", t=P)

        with nc.Block() as block:
            @block.sync
            def _(sp):
                sp.dma_start(E.causal[:, :, :], E.a["causal_mask"]).then_inc(s_m0, 16)
                sp.wait_ge(s_zero, 4)
                with nc.allow_non_contiguous_dma(reason="gate columns and short vectors"):
                    for q in range(4):
                        sp.dma_start(raw[:, :, 32 * q:32 * q + MH], w_in[:, :, 5 * D + MH * q:5 * D + MH * (q + 1)]).then_inc(s_w, 16)
                        sp.dma_start(bias[32 * q:32 * q + MH, :], E.a["mlstm_b_gates"][0, MH * q:MH * (q + 1)].rearrange("(p a) -> p a", a=1)).then_inc(s_w, 16)
                    for d, row in enumerate((FWD, BWD)):
                        sp.dma_start(entry[row:row + MH, 0:1], E.a["state_m"][0, 0, d].rearrange("(p a) -> p a", a=1)).then_inc(s_m0, 16)
                    sp.wait_ge(s_d, 10)
                    for d, row in enumerate((FWD, BWD)):
                        sp.dma_start(E.new_m[0, 0, d].rearrange("(p a) -> p a", a=1), m_out[row:row + MH, :]).then_inc(s_dma, 16)
                    sp.wait_ge(s_a, 4)
                    for d, row in enumerate((FWD, BWD)):
                        sp.dma_start(E.decay_dram[d], dec[row:row + MH, :]).then_inc(s_dma, 16)
                    rows = E.rows_dram.rearrange("h c q t -> q h c t")
                    sp.dma_start(rows[0], chunks(M)[FWD:FWD + MH]).then_inc(s_dma, 16)
                    sp.wait_ge(s_a, 5)
                    sp.dma_start(rows[2], chunks(tmp)[FWD:FWD + MH]).then_inc(s_dma, 16)
                    sp.wait_ge(s_d, 14)
                    sp.dma_start(rows[1], chunks(r)[BWD:BWD + MH]).then_inc(s_dma, 16)
                    sp.dma_start(rows[3], chunks(b)[BWD:BWD + MH]).then_inc(s_dma, 16)
                sp.wait_ge(s_dma, 128)
                sp.dma_start(E.decay[:, :, :, :], E.decay_dram.rearrange("d h c -> (d h c)").rearrange("(a n) -> a n", a=1).partition_broadcast(P)).then_inc(s_dma, 16)
                sp.wait_ge(s_dma, 144)

            @block.gpsimd
            def _(pool):
                pool.memset(raw[:, :, :], 0.0).then_inc(s_zero, 1)
                pool.memset(bias[:, :], 0.0).then_inc(s_zero, 1)
                pool.memset(entry[:, :], 0.0).then_inc(s_zero, 1)
                pool.memset(ig[:, :], 0.0).then_inc(s_zero, 1)
                pool.memset(lf[:, :], 0.0).then_inc(s_zero, 1)
                pool.memset(z[:, :], 0.0).then_inc(s_zero, 1)
                pool.memset(r[:, :], 1.0).then_inc(s_zero, 1)
                pool.wait_ge(s_zero, 7)
                pool.memset(chunks(r)[:, :, 0:1], 0.0).then_inc(s_zero, 1)
                pool.wait_ge(s_w, 128)
                pool.tensor_copy(w_hi[:, :, :], raw[:, :, :]).then_inc(s_hi, 1)

            @block.tensor
            def _(pe):
                pe.wait_ge(s_lo, 1)
                for g, (t0, t1) in enumerate(GROUPS):
                    tok = slice(t0 * P, t1 * P)
                    out = E.bank[g][:, 0:(t1 - t0) * P]
                    for k in range(KT):
                        pe.matmul(out, w_lo[:, k, :], E.h_hi[:, k, tok], start=(k == 0), stop=False)
                        pe.matmul(out, w_hi[:, k, :], E.h_lo[:, k, tok], start=False, stop=False)
                        ins = pe.matmul(out, w_hi[:, k, :], E.h_hi[:, k, tok], start=False, stop=(k == KT - 1))
                    ins.then_inc(s_unit, 1)
                for q, (src, ready) in enumerate(((lf, 18), (ig, 20), (M, 20))):
                    pe.wait_ge(s_d, ready)
                    if q == 0:
                        pe.wait_ge(s_nat, NG)
                    for c in range(NT):
                        g = 3 * q + c // 8
                        if g == 8 and c == 16:
                            pe.wait_ge(s_col, 1)
                        ins = pe.transpose(E.bank[g % 8][:, (c % 8) * ROWS:(c % 8 + 1) * ROWS],
                                           src[:, c * P:(c + 1) * P], E.ident[0:ROWS, 0:ROWS])
                    ins.then_inc(s_tr, 1)

            @block.scalar
            def _(act):
                act.wait_ge(s_w, 128)
                for g, (t0, t1) in enumerate(GROUPS):
                    act.wait_ge(s_unit, g + 1)
                    if g:
                        act.wait_ge(s_spread, g)
                    act.activation(nat4[:, 0:(t1 - t0) * P], E.bank[g][:, 0:(t1 - t0) * P], ACT.Identity,
                                   bias=bias[:, 0:1]).then_inc(s_nat, 1)
                act.wait_ge(s_spread, NG)
                act.activation(tmp[:, :], lf[:, :], ACT.Abs).then_inc(s_a, 1)
                act.wait_ge(s_a, 1)
                act.activation(tmp[:, :], tmp[:, :], ACT.Exp, scale=-1.0).then_inc(s_a, 1)
                act.wait_ge(s_a, 2)
                act.activation(tmp[:, :], tmp[:, :], ACT.Ln, bias=E.one[0:ROWS, 0:1]).then_inc(s_a, 1)
                act.wait_ge(s_d, 10)
                act.activation(dec[:, :], dec[:, :], ACT.Exp).then_inc(s_a, 1)
                act.wait_ge(s_d, 11)
                act.activation(tmp[:, :], tmp[:, :], ACT.Exp).then_inc(s_a, 1)
                act.wait_ge(s_d, 12)
                act.activation(z[:, :], z[:, :], ACT.Exp).then_inc(s_a, 1)
                act.wait_ge(s_d, 13)
                act.activation(lf[:, :], lf[:, :], ACT.Exp, scale=-1.0).then_inc(s_a, 1)

            @block.vector
            def _(dve):
                count = [0]

                def step(ins):
                    count[0] += 1
                    ins.then_inc(s_d, 1)
                    dve.wait_ge(s_d, count[0])

                dve.wait_ge(s_hi, 1)
                dve.tensor_tensor(w_lo[:, :, :], raw[:, :, :], w_hi[:, :, :], ALU.subtract).then_inc(s_lo, 1)
                dve.wait_ge(s_zero, 8)
                for g, (t0, t1) in enumerate(GROUPS):
                    dve.wait_ge(s_nat, g + 1)
                    lat = (min(t1, NS) - t0) * P
                    a = t0 * P
                    for dst, q in ((ig, 0), (lf, 1)):
                        dve.tensor_copy(dst[FWD:FWD + MH, a:t1 * P], nat4[32 * q:32 * q + MH, 0:(t1 - t0) * P])
                        if t1 > NS:
                            dve.tensor_copy(dst[BWD:BWD + MH, SAMPLE:T],
                                            reversed_cols(nat4, 512, 64 + 32 * q, MH, lat, P))
                        ins = dve.tensor_copy(dst[BWD:BWD + MH, SAMPLE - a - lat:SAMPLE - a],
                                              reversed_cols(nat4, 512, 64 + 32 * q, MH, 0, lat))
                    ins.then_inc(s_spread, 1)
                dve.wait_ge(s_a, 3)
                step(dve.scalar_tensor_tensor(lf[:, :], lf[:, :], 0.0, tmp[:, :], ALU.min, ALU.subtract))
                step(dve.tensor_tensor_scan(b[:, :], r[:, :], lf[:, :], 0.0, ALU.mult, ALU.add))
                step(dve.tensor_tensor(ig[:, :], ig[:, :], b[:, :], ALU.subtract))
                step(dve.tensor_copy(chunks(z)[:, 1:NS, 0:1], chunks(b)[:, 0:NS - 1, P - 1:P]))
                dve.wait_ge(s_m0, 48)
                step(dve.tensor_tensor_scan(M[:, 0:SAMPLE], z[:, 0:SAMPLE], ig[:, 0:SAMPLE], entry[:, 0:1],
                                            ALU.add, ALU.max))
                step(dve.tensor_tensor_scan(M[:, SAMPLE:T], z[:, SAMPLE:T], ig[:, SAMPLE:T], 0.0,
                                            ALU.add, ALU.max))
                step(dve.tensor_tensor(entry[:, 1:NS].unsqueeze(2), chunks(M)[:, 0:NS - 1, P - 1:P],
                                       chunks(b)[:, 0:NS - 1, P - 1:P], ALU.add))
                step(dve.tensor_copy(last_M[:, :].unsqueeze(2), chunks(M)[:, :, P - 1:P]))
                step(dve.tensor_tensor(m_out[:, :], M[:, T - 1:T], b[:, T - 1:T], ALU.add))
                step(dve.tensor_tensor(dec[:, :], entry[:, :], last_M[:, :], ALU.subtract))
                bc = lambda t: t[:, :].unsqueeze(2).to_broadcast([ROWS, NT, P])
                step(dve.tensor_tensor(chunks(tmp), bc(entry), chunks(M), ALU.subtract))
                step(dve.tensor_tensor(chunks(z), chunks(ig), bc(last_M), ALU.subtract))
                step(dve.tensor_tensor(lf[:, :], b[:, :], M[:, :], ALU.add))
                dve.wait_ge(s_a, 7)

                def turned(dst, src):
                    dve.tensor_copy(dst[BWD:BWD + MH, SAMPLE:T], reversed_cols(src, T, BWD, MH, SAMPLE, P))
                    return dve.tensor_copy(dst[BWD:BWD + MH, 0:SAMPLE], reversed_cols(src, T, BWD, MH, 0, SAMPLE))
                turned(r, M)
                step(turned(b, tmp))
                dve.wait_ge(s_dma, 128)
                step(dve.tensor_copy(M[:, :], lf[:, :]))
                step(turned(M, lf))
                step(dve.tensor_copy(lf[:, :], ig[:, :]))
                step(turned(lf, ig))
                step(dve.tensor_copy(ig[:, :], z[:, :]))
                step(turned(ig, z))
                for q in range(3):
                    dve.wait_ge(s_tr, q + 1)
                    for x in range(3):
                        n = min(8, NT - 8 * x)
                        src = E.bank[(3 * q + x) % 8][:, 0:n * ROWS].rearrange("p (c d y) -> p c d y", d=2, y=32)
                        ins = dve.tensor_copy(E.cols[:, 8 * x:8 * x + n, q, :, :], src[:, :, :, 0:MH])
                    ins.then_inc(s_col, 1)


def phase_mlstm(E):
    nc = E.nc
    E1 = MHD + 1
    with ExitStack() as ctx:
        sb = lambda n, s, d=F32: ctx.enter_context(nc.sbuf_tensor(f"m_{n}", s, d))
        sem = lambda n: E.semaphore(f"m_{n}")
        kT, qT, gT = sb("kT", [P, T]), sb("qT", [P, T]), sb("gT", [P, T])
        v1 = sb("v1", [P, NT, E1])
        CC = sb("states", [P, 2, NS + 1, E1])
        cout = sb("cout", [P, 2, E1])
        gexp = sb("gexp", [P, 512])
        kw = [sb(f"kw{j}", [P, 2, MHD]) for j in range(2)]
        bc = [sb(f"bc{x}", [P, 4, P]) for x in range(3)]
        hc = sb("hc", [P, NT, 3, 2])
        dech = sb("dech", [P, 2, NT])
        den = [sb(f"den{j}", [P, 2]) for j in range(2)]
        rec = [sb(f"rec{j}", [P, 2]) for j in range(2)]
        part = [sb(f"part{j}", [P, MHD]) for j in range(2)]
        hm = [sb(f"hm{j}", [P, MHD]) for j in range(2)]
        J = Projection(E, ctx, "mlstm", 5)
        (s_ones, s_relA, s_relD, s_vT, s_v1, s_hc, s_st, s_kT, s_kw, s_kv, s_cf, s_kvb, s_rev, s_cst,
         s_gexp, s_gd) = (sem(x) for x in (
            "ones", "bank_free_act", "bank_free_dve", "v_turned", "v_stored", "head_columns", "state_loaded",
            "k_turned", "weighted_keys", "kv_products", "forward_state", "kv_stored",
            "backward_state", "state_stored", "gate_exp", "gate_steps"))
        s_bc = [sem(f"rows_loaded{x}") for x in range(3)]
        (s_E, s_qw, s_W, s_S, s_P, s_num, s_den, s_rec, s_part, s_hm, s_hT, s_og, s_ogst) = (sem(x) for x in (
            "exponent", "q_weighted", "weights", "scores", "products", "num_done", "den", "recip", "part",
            "h_ready", "h_turned", "gated", "stored"))
        w_in = E.a["mlstm_w_in"][0].rearrange("(k p) m -> p k m", p=P)
        COL = {"k": D, "v": 2 * D, "q": 0, "o": 3 * D, "g": 4 * D}
        kinds = ["k", "v", "q", "o", "g"]
        NU = 5 * NG
        VG = [(0, 4), (4, 8), (8, 12), (12, 16), (16, 17)]
        VB = [4, 5, 6, 7, 4]

        def span(g):
            return slice(GROUPS[g][0] * P, GROUPS[g][1] * P), (GROUPS[g][1] - GROUPS[g][0]) * P

        E.start_at_one()
        with nc.Block() as block:
            @block.sync
            def _(sp):
                with sp.Fori(0, MH) as h:
                    def load(m):
                        J.sp_load(sp, h * 5 + m, [(0, w_in[:, :, ds(h * P + COL[kinds[m]], P)])])
                    load(0)
                    load(1)
                    sp.wait_ge(s_num, at(h * NT))
                    settle(E, sp)
                    with nc.allow_non_contiguous_dma(reason="normaliser columns"):
                        for d, slot in ((0, 0), (1, NS)):
                            sp.dma_start(CC[:, d, slot, 0:MHD], E.a["state_C"][0, 0, d, ds(h, 1)].rearrange("a d e -> d (a e)")).then_inc(s_st, 16)
                            sp.dma_start(CC[:, d, slot, MHD:E1], E.a["state_n"][0, 0, d, ds(h, 1)].rearrange("a d -> d a")).then_inc(s_st, 16)
                    for m in (2, 3, 4):
                        load(m)
                    with nc.allow_non_contiguous_dma(reason="normaliser columns"):
                        sp.wait_ge(s_kvb, at(h * NT + NT))
                        settle(E, sp)
                        for d in range(2):
                            sp.dma_start(E.new_C[0, 0, d, ds(h, 1)].rearrange("a d e -> d (a e)"), cout[:, d, 0:MHD]).then_inc(s_cst, 16)
                            sp.dma_start(E.new_n[0, 0, d, ds(h, 1)].rearrange("a d -> d a"), cout[:, d, MHD:E1]).then_inc(s_cst, 16)
                    for c in range(NT):
                        x = c % 3
                        sp.wait_ge(s_num, at(h * NT + max(c - 2, 0)))
                        settle(E, sp)
                        row = E.rows_dram[ds(h, 1), c, :, :].rearrange("a q t -> a (q t)")
                        sp.dma_start(bc[x][:, :, :].rearrange("p q t -> p (q t)"), row.partition_broadcast(P)).then_inc(s_bc[x], 16)
                    sp.wait_ge(s_og, at(h * NT + NT))
                    settle(E, sp)
                    sp.dma_start(E.ogT_dram[ds(h, 1), :, :].rearrange("a p t -> (a p) t"), gT[:, :]).then_inc(s_ogst, 16)
                sp.wait_ge(s_ogst, at(16 * MH))
                sp.wait_ge(s_cst, at(64 * MH))

            @block.gpsimd
            def _(pool):
                pool.memset(v1[:, :, MHD:E1], 1.0).then_inc(s_ones, 1)
                with pool.Fori(0, MH) as h:
                    J.pool_hi(pool, h * 5, h * 5 + 1)
                    pool.wait_ge(s_og, at(h * NT))
                    settle(E, pool)
                    pool.tensor_copy(hc[:, :, :, :], E.cols[:, :, :, :, ds(h, 1)].rearrange("p c q d a -> p c q (d a)")).then_inc(s_hc, 1)
                    pool.tensor_copy(dech[:, :, :], E.decay[:, :, ds(h, 1), :].rearrange("p d a c -> p d (a c)")).then_inc(s_hc, 1)
                    for m in range(1, 5):
                        J.pool_hi(pool, h * 5 + m, h * 5 + m + 1)
                    pool.wait_ge(s_relA, at(h * (4 * NG) + 3 * NG))
                    for c in range(NT):
                        x = c % 3
                        per = [6, 6, 5][x]
                        pool.wait_ge(s_bc[x], at(h * (16 * per) + 16 * (c // 3 + 1)))
                        pool.tensor_tensor(bc[x][:, 0:2, :], bc[x][:, 0:2, :], E.causal[:, :, :], ALU.add).then_inc(s_E, 1)
                        q = qT[:, c * P:(c + 1) * P].unsqueeze(1).to_broadcast([P, 2, P])
                        pool.tensor_tensor(bc[x][:, 2:4, :], bc[x][:, 2:4, :], q, ALU.mult).then_inc(s_qw, 1)

            @block.scalar
            def _(act):
                with act.Fori(0, MH) as h:
                    def evac(u):
                        m, g = u // NG, u % NG
                        tok, w = span(g)
                        act.wait_ge(J.s_unit, at(h * NU + u + 1))
                        src = E.bank[u % 4][:, 0:w]
                        if kinds[m] == "k":
                            act.activation(kT[:, tok], src, ACT.Copy, scale=MHD ** -0.5).then_inc(s_relA, 1)
                        elif kinds[m] == "v":
                            act.copy(gT[:, tok], src).then_inc(s_relA, 1)
                        elif kinds[m] == "q":
                            act.copy(qT[:, tok], src).then_inc(s_relA, 1)
                        elif kinds[m] == "o":
                            act.activation(gT[:, tok], src, ACT.Exp, scale=-1.0).then_inc(s_relA, 1)
                        else:
                            act.wait_ge(s_relD, at(h * NG + g))
                            act.activation(gexp[:, 0:w], src, ACT.Exp, scale=-1.0).then_inc(s_gexp, 1)

                    act.wait_ge(s_S, at(h * NT))
                    for u in range(NG):
                        evac(u)
                    act.wait_ge(s_ogst, at(h * 16))
                    for u in range(NG, 2 * NG):
                        evac(u)
                    act.wait_ge(s_num, at(h * NT))
                    for r, (a, z) in enumerate(VG):
                        act.wait_ge(s_vT, at(h * 5 + r + 1))
                        act.copy(v1[:, a:z, 0:MHD], E.bank[VB[r]][:, 0:(z - a) * P].rearrange("p (c e) -> p c e", e=P)).then_inc(s_v1, 1)
                    act.wait_ge(s_qw, at(h * NT))
                    act.wait_ge(s_hc, at(h * 2 + 2))
                    for s in range(NT + 1):
                        if 2 * NG + s < NU:
                            evac(2 * NG + s)
                        c = s - 1
                        if c >= 0:
                            act.wait_ge(s_kv, at(h * NT + c + 1))
                            if c < CTX:
                                dst = bass.AP(tensor=CC[:, :, :, :].tensor, offset=(c + 1) * E1,
                                              ap=[[2 * (NS + 1) * E1, P], [NS * E1, 2], [1, E1]])
                            else:
                                act.wait_ge(s_cst, at(h * 64))
                                dst = cout[:, :, :]
                            act.copy(dst, E.bank[6 + c % 2][:, 0:2 * E1].rearrange("p (d e) -> p d e", d=2)).then_inc(s_kvb, 1)
                    for s in range(NT + 1):
                        if s < NT:
                            act.wait_ge(s_E, at(h * NT + s + 1))
                            for d in range(2):
                                x = bc[s % 3][:, d, :]
                                ins = act.activation(x, x, ACT.Exp, bias=hc[:, s, U_COL, d:d + 1], scale=-1.0)
                            ins.then_inc(s_W, 1)
                        c = s - 1
                        if c >= 0:
                            act.wait_ge(s_rec, at(h * NT + c + 1))
                            act.wait_ge(s_hm, at(h * NT + max(c - 1, 0)))
                            act.activation(part[c % 2][:, :], E.bank[2 + c % 2][:, 0:MHD], ACT.Copy,
                                           scale=rec[c % 2][:, 0:1]).then_inc(s_part, 1)

            @block.vector
            def _(dve):
                with dve.Fori(0, MH) as h:
                    J.dve_lo(dve, h * 5)
                    J.dve_lo(dve, h * 5 + 1)
                    J.dve_lo(dve, h * 5 + 2)
                    dve.wait_ge(s_hc, at(h * 2 + 2))
                    dve.wait_ge(s_st, at(h * 64 + 64))
                    for s in range(NT + 1):
                        u = 2 * NG + s
                        if u < NU:
                            m, g = u // NG, u % NG
                            if g == NG - 1 and m < 4:
                                J.dve_lo(dve, h * 5 + m + 1)
                            if m == 4:
                                tok, w = span(g)
                                k = h * (3 * NG) + 3 * g
                                dve.wait_ge(s_relA, at(h * (4 * NG) + 4 * NG))
                                dve.tensor_scalar(gT[:, tok], gT[:, tok], 1.0, None, ALU.add).then_inc(s_gd, 1)
                                dve.wait_ge(s_gexp, at(h * NG + g + 1))
                                dve.wait_ge(s_gd, at(k + 1))
                                dve.scalar_tensor_tensor(gexp[:, 0:w], gexp[:, 0:w], 1.0, gT[:, tok], ALU.add, ALU.mult).then_inc(s_gd, 1)
                                dve.wait_ge(s_gd, at(k + 2))
                                dve.reciprocal(gexp[:, 0:w], gexp[:, 0:w]).then_inc(s_gd, 1)
                                dve.wait_ge(s_gd, at(k + 3))
                                dve.tensor_tensor(gT[:, tok], E.bank[u % 4][:, 0:w], gexp[:, 0:w], ALU.mult).then_inc(s_relD, 1)
                        if s < NT:
                            dve.wait_ge(s_kT, at(h * NT + s + 1))
                            dve.wait_ge(s_kv, at(h * NT + max(s - 1, 0)))
                            keys = E.bank[4 + s % 2][:, 0:P].unsqueeze(1).to_broadcast([P, 2, P])
                            weights = hc[:, s, WK_COL, :].unsqueeze(2).to_broadcast([P, 2, P])
                            dve.tensor_tensor(kw[s % 2][:, :, :], keys, weights, ALU.mult).then_inc(s_kw, 1)
                        c = s - 2
                        if 0 <= c < NS - 1:
                            dve.wait_ge(s_kvb, at(h * NT + c + 1))
                            dve.wait_ge(s_cf, at(h * (NS - 1) + c))
                            dve.scalar_tensor_tensor(CC[:, 0, c + 1, :], CC[:, 0, c, :], dech[:, 0, c:c + 1],
                                                     CC[:, 0, c + 1, :], ALU.mult, ALU.add).then_inc(s_cf, 1)
                    dve.wait_ge(s_kvb, at(h * NT + NT))
                    for n, c in enumerate(range(NS - 1, 0, -1)):
                        dve.wait_ge(s_rev, at(h * (NS - 1) + n))
                        dve.scalar_tensor_tensor(CC[:, 1, c, :], CC[:, 1, c + 1, :], dech[:, 1, n:n + 1],
                                                 CC[:, 1, c, :], ALU.mult, ALU.add).then_inc(s_rev, 1)
                    for s in range(NT + 2):
                        if s < NT:
                            dve.wait_ge(s_S, at(h * NT + s + 1))
                            dve.wait_ge(s_W, at(h * NT + s + 1))
                            x = bc[s % 3][:, 0:2, :]
                            S = E.bank[s % 2][:, 0:P].unsqueeze(1).to_broadcast([P, 2, P])
                            dve.tensor_tensor(x, S, x, ALU.mult).then_inc(s_P, 1)
                        c = s - 1
                        if 0 <= c < NT:
                            num = E.bank[2 + c % 2][:, 0:2 * E1].rearrange("p (d e) -> p d e", d=2)
                            dve.wait_ge(s_num, at(h * NT + c + 1))
                            floor = hc[:, c, EM_COL, :].unsqueeze(2)
                            d = den[c % 2][:, :].unsqueeze(2)
                            dve.scalar_tensor_tensor(d, num[:, :, MHD:E1], -1.0, floor, ALU.mult, ALU.max).then_inc(s_den, 1)
                            dve.wait_ge(s_den, at(h * (2 * NT) + 2 * c + 1))
                            dve.tensor_tensor(d, num[:, :, MHD:E1], d, ALU.max).then_inc(s_den, 1)
                            dve.wait_ge(s_den, at(h * (2 * NT) + 2 * c + 2))
                            dve.wait_ge(s_part, at(h * NT + max(c - 1, 0)))
                            dve.reciprocal(rec[c % 2][:, :], den[c % 2][:, :]).then_inc(s_rec, 1)
                            dve.wait_ge(s_part, at(h * NT + c + 1))
                            dve.wait_ge(s_hT, at(h * NT + max(c - 1, 0)))
                            dve.scalar_tensor_tensor(hm[c % 2][:, :], num[:, 1, 0:MHD], rec[c % 2][:, 1:2],
                                                     part[c % 2][:, :], ALU.mult, ALU.add).then_inc(s_hm, 1)
                        c = s - 2
                        if c >= 0:
                            dve.wait_ge(s_hT, at(h * NT + c + 1))
                            gtile = gT[:, c * P:(c + 1) * P]
                            dve.tensor_tensor(gtile, E.bank[4 + c % 2][:, 0:P], gtile, ALU.mult).then_inc(s_og, 1)

            @block.tensor
            def _(pe):
                pe.sem_inc(J.s_used, 2)
                pe.wait_ge(s_ones, at(1))
                with pe.Fori(0, MH) as h:
                    def unit(u):
                        if u < 4:
                            pe.wait_ge(s_relD, at(h * NG))
                            pe.wait_ge(s_P, at(h * NT))
                            pe.wait_ge(s_hm, at(h * NT))
                        elif u - 4 < 4 * NG:
                            pe.wait_ge(s_relA, at(h * (4 * NG) + u - 3))
                        else:
                            pe.wait_ge(s_relD, at(h * NG + u - 3 - 4 * NG))
                        J.pe_unit(pe, h * 5 + u // NG, u % NG, E.bank[u % 4])

                    for u in range(2 * NG):
                        unit(u)
                    pe.wait_ge(s_relA, at(h * (4 * NG) + 2 * NG))
                    pe.wait_ge(s_og, at(h * NT))
                    for r, (a, z) in enumerate(VG):
                        if r == 4:
                            pe.wait_ge(s_v1, at(h * 5 + 1))
                        for t in range(a, z):
                            ins = pe.transpose(E.bank[VB[r]][:, (t - a) * P:(t - a + 1) * P], gT[:, t * P:(t + 1) * P], E.ident[:, :])
                        ins.then_inc(s_vT, 1)
                    for s in range(NT + 1):
                        if 2 * NG + s < NU:
                            unit(2 * NG + s)
                        if s < NT:
                            if s == 0:
                                pe.wait_ge(s_v1, at(h * 5 + 5))
                            if s >= 2:
                                pe.wait_ge(s_kw, at(h * NT + s - 1))
                            pe.transpose(E.bank[4 + s % 2][:, 0:P], kT[:, s * P:(s + 1) * P], E.ident[:, :]).then_inc(s_kT, 1)
                        c = s - 1
                        if c >= 0:
                            pe.wait_ge(s_kw, at(h * NT + c + 1))
                            if c >= 2:
                                pe.wait_ge(s_kvb, at(h * NT + c - 1))
                            for d in range(2):
                                ins = pe.matmul(E.bank[6 + c % 2][:, d * E1:(d + 1) * E1], kw[c % 2][:, d, :],
                                                v1[:, c, :], start=True, stop=True, skip_group_check=True)
                            ins.then_inc(s_kv, 1)
                    pe.wait_ge(s_relA, at(h * (4 * NG) + 4 * NG))
                    pe.wait_ge(s_relD, at(h * NG + NG))
                    for s in range(NT + 2):
                        if s < NT:
                            if s >= 2:
                                pe.wait_ge(s_P, at(h * NT + s - 1))
                            tok = slice(s * P, (s + 1) * P)
                            pe.matmul(E.bank[s % 2][:, 0:P], kT[:, tok], qT[:, tok], start=True, stop=True).then_inc(s_S, 1)
                        c = s - 1
                        if 0 <= c < NT:
                            pe.wait_ge(s_P, at(h * NT + c + 1))
                            pe.wait_ge(s_qw, at(h * NT + c + 1))
                            if c == 0:
                                pe.wait_ge(s_cf, at(h * (NS - 1) + NS - 1))
                                pe.wait_ge(s_rev, at(h * (NS - 1) + NS - 1))
                            if c >= 2:
                                pe.wait_ge(s_hm, at(h * NT + c - 1))
                            for d in range(2):
                                out = E.bank[2 + c % 2][:, d * E1:(d + 1) * E1]
                                ins = pe.matmul(out, bc[c % 3][:, d, :], v1[:, c, :], start=True, stop=(c == CTX),
                                                skip_group_check=True)
                                if c < CTX:
                                    ins = pe.matmul(out, bc[c % 3][:, 2 + d, :], CC[:, d, c + d, :], start=False, stop=True,
                                                    skip_group_check=True)
                            ins.then_inc(s_num, 1)
                        c = s - 2
                        if c >= 0:
                            pe.wait_ge(s_hm, at(h * NT + c + 1))
                            if c >= 2:
                                pe.wait_ge(s_og, at(h * NT + c - 1))
                            pe.transpose(E.bank[4 + c % 2][:, 0:P], hm[c % 2][:, :], E.ident[:, :]).then_inc(s_hT, 1)


def build(nc, a, outs, phases=("pre", "attn", "out0", "gates", "mlstm", "out1"), debug=None):
    E = Env()
    E.nc, E.a = nc, a
    (E.out_prompt, E.out_sample, new_k, new_v, E.new_C, E.new_n, E.new_m) = outs
    E.out_prompt = E.out_prompt[0]
    E.out_sample = E.out_sample[0]
    E.new_k = new_k[0, 0].rearrange("s h d -> s (h d)")
    E.new_v = new_v[0, 0].rearrange("s h d -> s (h d)")
    E.cache_v = a["cache_v"][0, 0].rearrange("(t p) h d -> p t (h d)", p=P)
    E.x_tile = lambda n: a["x_sample"][0, ds(n * P, P), :] if not isinstance(n, int) else a["x_sample"][0, n * P:(n + 1) * P, :]
    dram = lambda n, s: nc.dram_tensor(n, s, F32, kind="Internal").ap()
    E.gates_dram = dram("gate_rows", [2, 2, D])
    E.ckt_dram = dram("cached_keys_turned", [P, NKV * PAST])
    E.ogT_dram = dram("gated_output", [KT, P, T])
    E.x1_dram = dram("layer0_output", [T, D])
    E.rows_dram = dram("gate_rows_mlstm", [MH, NT, 4, P])
    E.decay_dram = dram("decays", [2, MH, NT])
    if debug:
        for k, v in debug.items():
            if k == "ogT": E.ogT_dram = v
            if k == "x1": E.x1_dram = v
            if k == "rows": E.rows_dram = v
    with ExitStack() as ctx:
        sb = lambda n, s, d=F32: ctx.enter_context(nc.sbuf_tensor(n, s, d))
        E.s_tick = ctx.enter_context(nc.semaphore("tick"))
        phase_semaphores = []

        def semaphore(name):
            phase_semaphores.append(nc.alloc_semaphore(name=name))
            return phase_semaphores[-1]
        E.semaphore = semaphore

        def start_at_one():
            for s in phase_semaphores:
                nc.gpsimd.sem_inc(s, 1)
            nc.all_engine_barrier()
        E.start_at_one = start_at_one

        def run(phase, *args):
            phase(E, *args)
            nc.clear_and_free_semaphores(list(phase_semaphores))
            nc.all_engine_barrier()
            phase_semaphores.clear()
        E.PS = ctx.enter_context(nc.psum_tensor("psum", [P, 8, 512], F32))
        E.bank = [E.PS[:, b, :] for b in range(8)]
        E.ident = sb("ident", [P, P])
        E.eps = sb("eps", [P, 1])
        E.one = sb("one", [P, 1])
        E.hscale = sb("hscale", [P, 2, 2, KT])
        E.hshift = sb("hshift", [P, 2, 2, KT])
        with ExitStack() as c1:
            E.h_hi = c1.enter_context(nc.sbuf_tensor("h_hi", [P, KT, T], F32R))
            E.h_lo = c1.enter_context(nc.sbuf_tensor("h_lo", [P, KT, T], F32R))
            with ExitStack() as c2:
                E.wmask = c2.enter_context(nc.sbuf_tensor("wmask", [P, 3, 3 * P], BF16))
                E.identb = c2.enter_context(nc.sbuf_tensor("identb", [P, P], BF16))
                with ExitStack() as c3:
                    E.wmaskf = c3.enter_context(nc.sbuf_tensor("wmaskf", [P, 3, 3 * P], F32))
                    run(phase_pre)
                if "attn" in phases:
                    run(phase_attn)
            if "out0" in phases:
                run(phase_out, 0)
            with ExitStack() as c2:
                E.causal = c2.enter_context(nc.sbuf_tensor("causal", [P, 2, P], F32))
                E.cols = c2.enter_context(nc.sbuf_tensor("gate_columns", [P, NT, 3, 2, MH], F32))
                E.decay = c2.enter_context(nc.sbuf_tensor("decay_factors", [P, 2, MH, NT], F32))
                if "gates" in phases:
                    run(phase_gates)
                if "mlstm" in phases:
                    run(phase_mlstm)
        if "out1" in phases:
            run(phase_out, 1)


_INS = ["x_prompt", "x_sample", "cache_k", "cache_v", "state_C", "state_n", "state_m", "c", "c_ctx",
        "attn_norm_w", "attn_ada_w", "attn_ada_b", "attn_w_in", "attn_sink", "attn_w_out",
        "mlstm_norm_w", "mlstm_ada_w", "mlstm_ada_b", "mlstm_w_in", "mlstm_b_gates", "mlstm_w_out",
        "final_norm_w"]
_OUTS = [(1, P, D), (1, SAMPLE, D), (1, 1, P, NKV, HD), (1, 1, P, NKV, HD),
         (1, 1, 2, MH, MHD, MHD), (1, 1, 2, MH, MHD), (1, 1, 2, MH)]


def shape_constants():
    import numpy as np
    f = np.float32
    q, j = np.arange(P)[:, None], np.arange(P)[None, :]
    prev = np.where(j >= q, 0, -BIG).astype(f)
    nxt = np.where(j <= q, 0, -BIG).astype(f)
    none = np.full((P, P), -BIG, f)
    own = np.zeros((P, P), f)
    window = np.stack([np.concatenate(x, 1) for x in ((none, own, nxt), (prev, own, nxt), (prev, own, none))], 1)
    causal = np.stack([np.where(q <= j, 0, BIG), np.where(q >= j, 0, BIG)], 1).astype(f)
    nf = HD // 4
    inv = (f(10000.0) ** (-np.arange(nf, dtype=f) / f(nf))).astype(f)
    t = np.arange(SAMPLE)
    row, col = (t // 64).astype(f), (t % 64).astype(f)
    ar, ac = inv[:, None] * row[None, :], inv[:, None] * col[None, :]
    ang = np.concatenate([ar, ar, ac, ac] * 2, 0).astype(f)
    sign = np.concatenate([-np.ones(nf), np.ones(nf)] * 4)[:, None].astype(f)
    rotary = np.stack([np.cos(ang), np.sin(ang) * sign], 1).astype(f)
    return {"ident": np.eye(P, dtype=f), "window_mask": window, "causal_mask": causal, "rotary": rotary}


def kernel(**inputs):
    import numpy as np
    import concourse.bacc as bacc
    from concourse.bass_utils import run_bass_kernel_spmd

    nc = bacc.Bacc("TRN2", target_bir_lowering=False, num_devices=1, dynamic_dma_scratch_size=1024)
    arrays = {k: np.ascontiguousarray(inputs[k]) for k in _INS}
    arrays.update(shape_constants())
    a = {k: nc.dram_tensor(f"in_{k}", v.shape, F32, kind="ExternalInput").ap() for k, v in arrays.items()}
    outs = [nc.dram_tensor(f"out_{i}", s, F32, kind="ExternalOutput").ap() for i, s in enumerate(_OUTS)]
    build(nc, a, outs)
    r = run_bass_kernel_spmd(nc, [{f"in_{k}": v for k, v in arrays.items()}], core_ids=[0])
    return tuple(r.results[0][f"out_{i}"] for i in range(len(_OUTS)))
```

```python
from contextlib import ExitStack

import concourse.bass as bass
from concourse import mybir

F32 = mybir.dt.float32
F32R = mybir.dt.float32r
BF16 = mybir.dt.bfloat16
ALU = mybir.AluOpType
ACT = mybir.ActivationFunctionType
AX = mybir.AxisListType
ds = bass.ds

P = 128
D = 1024
KT = D // P
SAMPLE = 2048
NS = SAMPLE // P
CTX = NS
NT = NS + 1
T = NT * P
PAST = 256
HD = 64
NKV = 4
NHEAD = 16
MH = 8
MHD = 128
EPS = 1e-6
BIG = 1.0e30

GROUPS = [(0, 4), (4, 8), (8, 11), (11, 14), (14, 17)]
NG = len(GROUPS)
KPAD = PAST
KLAT = KPAD + P
KREQ = KLAT + SAMPLE + P
KCOLS = KREQ + P
VT_LAT = KLAT // P
VT_REQ = KREQ // P
VTILES = KCOLS // P
VGROUPS = [(0, 8), (8, 16), (16, 17)]


class Env:
    pass


def pair_loop(eng, body):
    with eng.Fori(0, NS // 2) as i:
        for j in range(2):
            body(i * 2 + j, j, i, False)
    body(CTX, 0, NS // 2, True)


def over(n):
    return n + 3


def free(n):
    return n + 1


def all_heads(eng, n, body):
    with eng.Fori(0, n - 1) as h:
        body(h, False)
    body(n - 1, True)


def at(n):
    return n + 1


def settle(E, eng):
    eng.sem_inc(E.s_tick, 1)


class NormTranspose:

    def __init__(self, E, ctx, layer, src, src_ready):
        nc = E.nc
        self.E, self.layer, self.src, self.src_ready = E, layer, src, src_ready
        sb = lambda n, s, d=F32: ctx.enter_context(nc.sbuf_tensor(f"{n}{layer}", s, d))
        sem = lambda n: E.semaphore(f"{n}{layer}")
        self.xn = [sb(f"xn{j}_", [P, D]) for j in range(2)]
        self.htmp = [sb(f"htmp{j}_", [P, KT, P]) for j in range(2)]
        self.ss = sb("ss", [P, 2])
        self.std = sb("std", [P, 2])
        self.rs = sb("rs", [P, 2])
        self.s_sq = sem("sum_of_squares")
        self.s_std = sem("root_mean_square")
        self.s_rs = sem("rms_reciprocal")
        self.s_xn = sem("normalised")
        self.s_tp = sem("transposed")
        self.s_ha = sem("modulated_act")
        self.s_hd = sem("modulated_dve")
        self.s_hi = sem("hi_part")
        self.s_lo = sem("lo_part")
        self.bank = [E.bank[4:6], E.bank[6:8]]

    def credits_act(self, eng):
        for s in (self.s_sq, self.s_std, self.s_ha):
            eng.sem_inc(s, 2)

    def credits_dve(self, eng):
        for s in (self.s_rs, self.s_xn, self.s_hd, self.s_lo):
            eng.sem_inc(s, 2)

    def act_stats(self, eng, n, j):
        self.src_ready(eng, n, j)
        eng.wait_ge(self.s_tp, free(n))
        eng.activation(self.xn[j][:, :], self.src[j][:, :], ACT.Square,
                       accum_out=self.ss[:, j:j + 1]).then_inc(self.s_sq, 1)
        eng.wait_ge(self.s_sq, over(n))
        eng.wait_ge(self.s_rs, free(n))
        eng.activation(self.std[:, j:j + 1], self.ss[:, j:j + 1], ACT.Sqrt,
                       bias=self.E.eps[:, 0:1], scale=1.0 / D).then_inc(self.s_std, 1)

    def dve_normalise(self, eng, n, j):
        self.src_ready(eng, n, j)
        eng.wait_ge(self.s_std, over(n))
        eng.wait_ge(self.s_xn, free(n))
        eng.reciprocal(self.rs[:, j:j + 1], self.std[:, j:j + 1]).then_inc(self.s_rs, 1)
        eng.wait_ge(self.s_rs, over(n))
        eng.wait_ge(self.s_tp, free(n))
        eng.tensor_scalar(self.xn[j][:, :], self.src[j][:, :], self.rs[:, j:j + 1], None,
                          ALU.mult).then_inc(self.s_xn, 1)

    def pe_transpose(self, eng, n, j):
        eng.wait_ge(self.s_xn, over(n))
        eng.wait_ge(self.s_ha, free(n))
        eng.wait_ge(self.s_hd, free(n))
        for k in range(KT):
            out = self.bank[j][k // 4][:, (k % 4) * P:(k % 4 + 1) * P]
            last = eng.transpose(out, self.xn[j][:, k * P:(k + 1) * P], self.E.ident[:, :])
        last.then_inc(self.s_tp, 1)

    def act_modulate(self, eng, n, j, cond):
        E, l = self.E, self.layer
        eng.wait_ge(self.s_tp, over(n))
        eng.wait_ge(self.s_lo, free(n))
        for k in range(4):
            last = eng.activation(self.htmp[j][:, k, :], self.bank[j][0][:, k * P:(k + 1) * P],
                                  ACT.Identity, bias=E.hshift[:, l, cond, k:k + 1],
                                  scale=E.hscale[:, l, cond, k:k + 1])
        last.then_inc(self.s_ha, 1)

    def dve_modulate(self, eng, n, j, cond):
        E, l = self.E, self.layer
        eng.wait_ge(self.s_tp, over(n))
        for k in range(4, KT):
            last = eng.tensor_scalar(self.htmp[j][:, k, :], self.bank[j][1][:, (k - 4) * P:(k - 3) * P],
                                     E.hscale[:, l, cond, k:k + 1], E.hshift[:, l, cond, k:k + 1],
                                     ALU.mult, ALU.add)
        last.then_inc(self.s_hd, 1)

    def pool_hi(self, eng, n, j):
        eng.wait_ge(self.s_ha, over(n))
        eng.wait_ge(self.s_hd, over(n))
        settle(self.E, eng)
        eng.tensor_copy(self.E.h_hi[:, :, ds(n * P, P)], self.htmp[j][:, :, :]).then_inc(self.s_hi, 1)

    def dve_lo(self, eng, n, j):
        eng.wait_ge(self.s_hi, over(n))
        eng.tensor_tensor(self.E.h_lo[:, :, ds(n * P, P)], self.htmp[j][:, :, :],
                          self.E.h_hi[:, :, ds(n * P, P)], ALU.subtract).then_inc(self.s_lo, 1)


def phase_pre(E):
    nc = E.nc
    with ExitStack() as ctx:
        sb = lambda n, s, d=F32: ctx.enter_context(nc.sbuf_tensor(n, s, d))
        sem = lambda n: E.semaphore(n)
        s_const, s_cmask, s_cond, s_bias_zero, s_bias = (sem(x) for x in (
            "const_loaded", "bf16_masks", "cond_loaded", "bias_rows_zeroed", "bias_rows_loaded"))
        s_exp, s_silu, s_vec, s_vecs = (sem(x) for x in ("cond_exp", "cond_silu", "vec_turned", "vec_copied"))
        s_ck, s_ckt, s_ckc, s_cko = (sem(x) for x in ("ck_loaded", "ck_turned", "ck_copied", "ck_stored"))
        s_ada = [sem(f"ada_loaded{j}") for j in range(2)]
        s_prod, s_row, s_turned, s_mod = (sem(x) for x in (
            "adaln_products", "adaln_rows", "adaln_turned", "mod_vectors"))
        s_gst = sem("gate_rows_stored")
        s_x = [sem(f"x_loaded{j}") for j in range(2)]

        xb = [sb(f"xb{j}", [P, D]) for j in range(2)]
        ada = [sb(f"ada{j}", [P, KT, 512]) for j in range(2)]
        vecrows = sb("vecrows", [48, P])
        vecs = sb("vecs", [P, 48])
        cnd = sb("cnd", [P, 2, KT])
        cnd_e = sb("cnd_e", [P, 2, KT])
        silu_c = sb("silu_c", [P, KT, 2])
        silu_pad = sb("silu_pad", [P, KT, 33])
        grow = sb("grow", [33, D])
        gbias = sb("gbias", [33, D])
        ckr = sb("ckr", [P, 2, NKV, 2, HD])
        ckt = xb[0]

        def x_ready(eng, n, j):
            eng.wait_ge(s_x[j], (n - j) * 8 + 16)

        N = NormTranspose(E, ctx, 0, xb, x_ready)
        mod_rows = [sb(f"mod_rows{j}", [33, 512]) for j in range(2)]
        modps, vecps = [E.bank[0], E.bank[1]], E.bank[6]
        rowps = [E.bank[2], E.bank[3]]

        with nc.Block() as block:
            @block.sync
            def _(sp):
                sp.dma_start(E.ident[:, :], E.a["ident"]).then_inc(s_const, 16)
                sp.dma_start(E.wmaskf[:, :, :], E.a["window_mask"]).then_inc(s_const, 16)
                with nc.allow_non_contiguous_dma(reason="short vectors"):
                    sp.dma_start(vecrows[0:8, :], E.a["attn_norm_w"].rearrange("a (k p) -> (a k) p", p=P)).then_inc(s_const, 16)
                    sp.dma_start(vecrows[8:24, :], E.a["attn_ada_b"][:, 0:2 * D].rearrange("a (k p) -> (a k) p", p=P)).then_inc(s_const, 16)
                    sp.dma_start(vecrows[24:32, :], E.a["mlstm_norm_w"].rearrange("a (k p) -> (a k) p", p=P)).then_inc(s_const, 16)
                    sp.dma_start(vecrows[32:48, :], E.a["mlstm_ada_b"][:, 0:2 * D].rearrange("a (k p) -> (a k) p", p=P)).then_inc(s_const, 16)
                    sp.dma_start(cnd[:, 0, :], E.a["c"].rearrange("a (p k) -> p (a k)", k=KT)).then_inc(s_cond, 16)
                    sp.dma_start(cnd[:, 1, :], E.a["c_ctx"].rearrange("(p k) -> p k", k=KT)).then_inc(s_cond, 16)
                for r in range(2):
                    for k in range(2):
                        sp.dma_start(ckr[:, k, :, r, :], E.a["cache_k"][0, 0, k * P:(k + 1) * P]).then_inc(s_ck, 16)
                for n in range(12):
                    layer, c = n // 6, n % 6
                    w = E.a["attn_ada_w"] if layer == 0 else E.a["mlstm_ada_w"]
                    if n >= 2:
                        sp.wait_ge(s_prod, n - 1)
                    sp.dma_start(ada[n % 2][:, :, :], w[0].rearrange("(p k) m -> p k m", k=KT)[:, :, c * 512:(c + 1) * 512]).then_inc(s_ada[n % 2], 16)
                    if n == 3:
                        sp.wait_ge(s_ckc, 1)
                        sp.dma_start(E.ckt_dram, ckt[:, :]).then_inc(s_cko, 16)
                    if c == 4:
                        if layer == 1:
                            sp.wait_ge(s_gst, 32)
                        sp.wait_ge(s_bias_zero, layer + 1)
                        b = E.a["attn_ada_b"] if layer == 0 else E.a["mlstm_ada_b"]
                        sp.dma_start(gbias[0:1, :], b[:, 2 * D:3 * D]).then_inc(s_bias, 16)
                        sp.dma_start(gbias[32:33, :], b[:, 2 * D:3 * D]).then_inc(s_bias, 16)
                    if n == 7:
                        sp.wait_ge(s_row, 6)
                        for r in range(2):
                            sp.dma_start(E.gates_dram[0, r:r + 1, :], grow[32 * r:32 * r + 1, :]).then_inc(s_gst, 16)
                    if n == 11:
                        sp.wait_ge(s_row, 12)
                        for r in range(2):
                            sp.dma_start(E.gates_dram[1, r:r + 1, :], grow[32 * r:32 * r + 1, :]).then_inc(s_gst, 16)
                        sp.wait_ge(s_gst, 64)

            @block.gpsimd
            def _(pool):
                pool.sem_inc(N.s_hi, 2)
                pair_loop(pool, lambda n, j, i, last: N.pool_hi(pool, n, j))

            @block.scalar
            def _(act):
                N.credits_act(act)
                act.wait_ge(s_cond, 32)
                act.activation(cnd_e[:, :, :], cnd[:, :, :], ACT.Exp, scale=-1.0).then_inc(s_exp, 1)
                act.wait_ge(s_cko, 16)
                for j in range(2):
                    act.dma_start(xb[j][:, :], E.a["x_sample"][0, j * P:(j + 1) * P, :]).then_inc(s_x[j], 16)

                act.wait_ge(s_mod, 1)
                N.act_stats(act, 0, 0)

                def tile(n, j, next_x):
                    act.wait_ge(N.s_xn, over(n))
                    act.dma_start(xb[j][:, :], next_x).then_inc(s_x[j], 16)
                    N.act_stats(act, n + 1, 1 - j)
                    N.act_modulate(act, n, j, 0)
                with act.Fori(0, NS // 2 - 1) as i:
                    for j in range(2):
                        tile(i * 2 + j, j, E.x_tile(i * 2 + (j + 2)))
                tile(NS - 2, 0, E.a["x_prompt"][0])
                N.act_stats(act, CTX, 0)
                N.act_modulate(act, NS - 1, 1, 0)
                N.act_modulate(act, CTX, 0, 1)

            @block.vector
            def _(dve):
                N.credits_dve(dve)
                dve.memset(silu_pad[:, :, :], 0.0).then_inc(s_silu, 1)
                dve.memset(gbias[:, :], 0.0).then_inc(s_bias_zero, 2)
                dve.memset(E.one[:, :], 1.0)
                dve.memset(E.eps[:, :], EPS).then_inc(s_silu, 1)
                dve.wait_ge(s_const, 96)
                dve.tensor_copy(E.wmask[:, :, :], E.wmaskf[:, :, :]).then_inc(s_cmask, 1)
                dve.tensor_copy(E.identb[:, :], E.ident[:, :]).then_inc(s_cmask, 1)
                dve.wait_ge(s_exp, 1)
                dve.tensor_scalar(cnd_e[:, :, :], cnd_e[:, :, :], 1.0, None, ALU.add).then_inc(s_silu, 1)
                dve.wait_ge(s_silu, 3)
                dve.reciprocal(cnd_e[:, :, :], cnd_e[:, :, :]).then_inc(s_silu, 1)
                dve.wait_ge(s_silu, 4)
                dve.tensor_tensor(silu_c[:, :, :].rearrange("p k c -> p c k"), cnd[:, :, :], cnd_e[:, :, :], ALU.mult).then_inc(s_silu, 1)
                dve.wait_ge(s_silu, 5)
                for r in range(2):
                    dve.tensor_copy(silu_pad[:, :, 32 * r:32 * r + 1], silu_c[:, :, r:r + 1]).then_inc(s_silu, 1)
                dve.wait_ge(s_vec, 1)
                dve.tensor_copy(vecs[:, :], vecps[:, 0:48]).then_inc(s_vecs, 1)
                for h in range(2):
                    dve.wait_ge(s_ckt, h + 1)
                    v = ckt[:, :].rearrange("p (h t) -> p h t", h=NKV)[:, :, h * P:(h + 1) * P]
                    ins = dve.tensor_copy(v, E.bank[4 + h][:, :].rearrange("p (h t) -> p h t", h=NKV))
                ins.then_inc(s_ckc, 1)
                dve.wait_ge(s_vecs, 1)

                def mods(layer):
                    dve.wait_ge(s_turned, 4 * layer + 4)
                    v0 = layer * 24
                    for c in range(2):
                        column = lambda b: modps[b][:, 0:8 * 33].rearrange("p (k r) -> p k r", r=33)[:, :, 32 * c]
                        dve.tensor_tensor(E.hshift[:, layer, c, :], column(0), vecs[:, v0 + 8:v0 + 16], ALU.add)
                        ins = dve.tensor_tensor(E.hscale[:, layer, c, :], column(1), vecs[:, v0 + 16:v0 + 24], ALU.add)
                    ins.then_inc(s_vecs, 1)
                    dve.wait_ge(s_vecs, 2 + layer)
                    for c in range(2):
                        ins = dve.scalar_tensor_tensor(E.hscale[:, layer, c, :], E.hscale[:, layer, c, :], 1.0,
                                                       vecs[:, v0:v0 + 8], ALU.add, ALU.mult)
                    ins.then_inc(s_mod, 1)

                for n in range(12):
                    layer, c = n // 6, n % 6
                    dve.wait_ge(s_prod, n + 1)
                    if c < 4:
                        t = 4 * layer + c
                        if t >= 2:
                            dve.wait_ge(s_turned, t - 1)
                        dve.tensor_copy(mod_rows[t % 2][:, :], rowps[n % 2][0:33, :]).then_inc(s_row, 1)
                    else:
                        if c == 4:
                            dve.wait_ge(s_bias, 32 * (layer + 1))
                            if layer == 1:
                                dve.wait_ge(s_gst, 32)
                        cols = slice((c - 4) * 512, (c - 3) * 512)
                        dve.tensor_tensor(grow[:, cols], rowps[n % 2][0:33, :], gbias[:, cols], ALU.add).then_inc(s_row, 1)
                    if c == 4:
                        mods(layer)
                dve.wait_ge(s_mod, 1)

                N.dve_normalise(dve, 0, 0)
                N.dve_normalise(dve, 1, 1)
                N.dve_modulate(dve, 0, 0, 0)

                def tile(n, j):
                    N.dve_normalise(dve, n + 1, 1 - j)
                    N.dve_lo(dve, n - 1, 1 - j)
                    N.dve_modulate(dve, n, j, 0)
                with dve.Fori(0, NS // 2 - 1) as i:
                    tile(i * 2 + 1, 1)
                    tile(i * 2 + 2, 0)
                tile(NS - 1, 1)
                N.dve_lo(dve, NS - 1, 1)
                N.dve_modulate(dve, CTX, 0, 1)
                N.dve_lo(dve, CTX, 0)

            @block.tensor
            def _(pe):
                pe.sem_inc(N.s_tp, 2)
                pe.wait_ge(s_const, 96)
                pe.transpose(vecps[:, 0:48], vecrows[:, :], E.ident[0:48, 0:48]).then_inc(s_vec, 1)
                pe.wait_ge(s_ck, 64)
                for t in range(2):
                    for h in range(NKV):
                        ins = pe.transpose(E.bank[4 + t][:, h * P:(h + 1) * P],
                                           ckr[:, t, h, :, :].rearrange("p r d -> p (r d)"), E.ident[:, :])
                    ins.then_inc(s_ckt, 1)
                pe.wait_ge(s_silu, 7)
                def turn(n):
                    layer, c = n // 6, n % 6
                    pe.wait_ge(s_row, n + 1)
                    if layer == 1:
                        pe.wait_ge(s_mod, 1)
                    for b in range(4):
                        at0 = ((c % 2) * 4 + b) * 33
                        ins = pe.transpose(modps[c // 2][:, at0:at0 + 33], mod_rows[c % 2][:, b * P:(b + 1) * P],
                                           E.ident[0:33, 0:33])
                    ins.then_inc(s_turned, 1)

                for n in range(12):
                    layer, c = n // 6, n % 6
                    pe.wait_ge(s_ada[n % 2], 16 * (n // 2 + 1))
                    if n >= 2:
                        pe.wait_ge(s_row, n - 1)
                    for k in range(KT):
                        ins = pe.matmul(rowps[n % 2][0:33, :], silu_pad[:, k, :], ada[n % 2][:, k, :],
                                        start=(k == 0), stop=(k == KT - 1))
                    ins.then_inc(s_prod, 1)
                    if 1 <= c <= 4:
                        turn(n - 1)
                pe.wait_ge(s_ckc, 1)
                pair_loop(pe, lambda n, j, i, last: N.pe_transpose(pe, n, j))


class Projection:

    def __init__(self, E, ctx, tag, blocks_per_iter):
        nc = E.nc
        self.E, self.B = E, blocks_per_iter
        sb = lambda n, s, d=F32: ctx.enter_context(nc.sbuf_tensor(f"{tag}_{n}", s, d))
        sem = lambda n: E.semaphore(f"{tag}_{n}")
        self.raw = sb("w_raw", [P, KT, P])
        self.hi = sb("w_hi", [P, KT, P], F32R)
        self.lo = sb("w_lo", [P, KT, P], F32R)
        self.s_raw = sem("w_loaded")
        self.s_hi = sem("w_hi_ready")
        self.s_lo = sem("w_lo_ready")
        self.s_used = sem("w_first_half_used")
        self.s_unit = sem("unit_done")

    def sp_load(self, sp, n, pieces):
        sp.wait_ge(self.s_lo, at(n * 2))
        settle(self.E, sp)
        for c0, src in pieces:
            w = src.shape[-1]
            sp.dma_start(self.raw[:, :, c0:c0 + w], src).then_inc(self.s_raw, 16)

    def pool_hi(self, pool, n, loads):
        pool.wait_ge(self.s_raw, at(loads * 16))
        for half in range(2):
            if half == 0:
                pool.wait_ge(self.s_used, at(n))
            else:
                pool.wait_ge(self.s_unit, at(n * NG))
            settle(self.E, pool)
            k = slice(4 * half, 4 * half + 4)
            pool.tensor_copy(self.hi[:, k, :], self.raw[:, k, :]).then_inc(self.s_hi, 1)

    def act_hi(self, act, n, loads):
        act.wait_ge(self.s_raw, at(loads * 16))
        for half in range(2):
            if half == 0:
                act.wait_ge(self.s_used, at(n))
            else:
                act.wait_ge(self.s_unit, at(n * NG))
            k = slice(4 * half, 4 * half + 4)
            act.copy(self.hi[:, k, :], self.raw[:, k, :]).then_inc(self.s_hi, 1)

    def dve_lo(self, dve, n):
        for half in range(2):
            dve.wait_ge(self.s_hi, at(n * 2 + half + 1))
            k = slice(4 * half, 4 * half + 4)
            dve.tensor_tensor(self.lo[:, k, :], self.raw[:, k, :], self.hi[:, k, :],
                              ALU.subtract).then_inc(self.s_lo, 1)

    def pe_unit(self, pe, n, g, bank):
        E = self.E
        t0, t1 = GROUPS[g]
        tok = slice(t0 * P, t1 * P)
        out = bank[:, 0:(t1 - t0) * P]
        for k in range(KT):
            if g == 0 and k % 4 == 0:
                pe.wait_ge(self.s_lo, at(n * 2 + k // 4 + 1))
            pe.matmul(out, self.lo[:, k, :], E.h_hi[:, k, tok], start=(k == 0), stop=False)
            pe.matmul(out, self.hi[:, k, :], E.h_lo[:, k, tok], start=False, stop=False)
            ins = pe.matmul(out, self.hi[:, k, :], E.h_hi[:, k, tok], start=False, stop=(k == KT - 1))
            if g == NG - 1 and k == 3:
                ins.then_inc(self.s_used, 1)
        ins.then_inc(self.s_unit, 1)


def phase_attn(E):
    nc = E.nc
    SWAP = [(p + 16) % 32 for p in range(32)]
    with ExitStack() as ctx:
        sb = lambda n, s, d=F32: ctx.enter_context(nc.sbuf_tensor(n, s, d))
        sem = lambda n: E.semaphore(n)
        kT = sb("kT", [P, KCOLS])
        vS = sb("vS", [P, VTILES, 2, HD])
        qT = sb("qT", [P, T])
        gT = sb("gT", [P, T])
        cs = [sb(f"cs{b}", [P, 2, 512]) for b in range(2)]
        shuf = [sb(f"shuf{b}", [P, 512]) for b in range(2)]
        prob = [sb(f"prob{b}", [P, 640]) for b in range(4)]
        gth = prob[0:2]
        probT = [sb(f"probT{b}", [P, 5, 2, P]) for b in range(2)]
        sink = sb("sink", [P, NHEAD])
        nsink = sb("nsink", [P, NHEAD])
        mx = sb("mx", [P, 2])
        negm = sb("negm", [P, 2, 2])
        rsum = sb("rsum", [P, 2, 2])
        sarg = sb("sarg", [P, 2, 2])
        esink = sb("esink", [P, 2, 2])
        den = sb("den", [P, 2, 2])
        rden = sb("rden", [P, 2, 2])
        kvout = sb("kvout", [P, 2, HD])

        J = Projection(E, ctx, "attn", 5)
        s_cs = [sem(f"rotary_loaded{b}") for b in range(2)]
        (s_shuf, s_cos, s_rope, s_gth, s_release, s_kdup, s_vT, s_vS, s_kvo, s_kvst, s_ckl, s_cvl,
         s_const, s_pad, s_sin) = (sem(x) for x in (
            "shuffled", "times_cos", "rotated", "gate_tanh", "proj_bank_free", "k_doubled",
            "v_turned", "v_stored", "kv_out_ready", "kv_out_stored", "cached_k_loaded", "cached_v_loaded",
            "sink_loaded", "pads_zero", "times_sin"))
        s_pTc2 = sem("probsT_last_ready")
        (s_S, s_mx, s_nm, s_p, s_pn, s_pT, s_pTc, s_pv, s_sarg, s_es, s_den, s_rd, s_og, s_ogst) = (
            sem(x) for x in ("scores", "row_max", "neg_max", "probs", "probs_normalised", "probs_turned",
                             "probsT_ready", "pv_done", "sink_minus_max", "sink_exp", "denominator", "recip_den",
                             "o_gated", "o_stored"))
        w_in = E.a["attn_w_in"][0].rearrange("(k p) m -> p k m", p=P)

        NU = 2 * NT
        kinds = ["kv", "q", "g", "q", "g"]
        ROPES = 3 * NG

        def kv_columns(kv):
            return [(0, w_in[:, :, ds(kv * HD + 2 * D, HD)]), (HD, w_in[:, :, ds(kv * HD + (2 * D + NKV * HD), HD)])]

        def scores_of(w):
            pair = E.PS[:, 2 * (w % 2):2 * (w % 2) + 2, :].rearrange("p a n -> p (a n)")
            return pair[:, 256:896] if w // 2 < CTX else pair[:, 512:512 + P]

        def lat_ctx(g):
            t0, t1 = GROUPS[g]
            lat = min(t1, NS) - t0
            return t0 * P, lat * P, (t1 - t0) * P - lat * P

        E.start_at_one()
        with nc.Block() as block:
            @block.sync
            def _(sp):
                sp.dma_start(sink[:, :], E.a["attn_sink"].partition_broadcast(P)).then_inc(s_const, 16)
                J.sp_load(sp, 0, kv_columns(0))

                def head(kv, last):
                    rope = 0

                    def load_weights(m):
                        col = (0 if kinds[m] == "q" else D) + (m - 1) // 2 * P
                        J.sp_load(sp, kv * 5 + m, [(0, w_in[:, :, ds(kv * (2 * P) + col, P)])])

                    for m, kind in enumerate(kinds):
                        if m < 4:
                            load_weights(m + 1)
                        if kind == "kv":
                            sp.wait_ge(s_S, at(kv * (2 * NU)))
                            settle(E, sp)
                            with nc.allow_non_contiguous_dma(reason="rows of one head"):
                                sp.dma_start(kT[:, 0:PAST], E.ckt_dram[:, ds(kv * PAST, PAST)]).then_inc(s_ckl, 16)
                                sp.wait_ge(s_pv, at(kv * (2 * NT)))
                                settle(E, sp)
                                for copy in range(2):
                                    sp.dma_start(vS[:, 0:2, copy, :], E.cache_v[:, :, ds(kv * HD, HD)]).then_inc(s_cvl, 16)
                        if kind != "g":
                            for g in range(NG):
                                t0, wl, wc = lat_ctx(g)
                                b = rope % 2
                                if rope >= 2:
                                    sp.wait_ge(s_rope, at(kv * ROPES + rope - 1))
                                else:
                                    sp.wait_ge(s_rope, at(kv * ROPES))
                                sp.dma_start(cs[b][:, :, 0:wl], E.a["rotary"][:, :, t0:t0 + wl]).then_inc(s_cs[b], 16)
                                rope += 1
                        if kind == "kv":
                            sp.wait_ge(s_kvo, at(kv * 2 + 2))
                            settle(E, sp)
                            with nc.allow_non_contiguous_dma(reason="rows of one head"):
                                sp.dma_start(E.new_k[:, ds(kv * HD, HD)], kvout[:, 0, :]).then_inc(s_kvst, 16)
                                sp.dma_start(E.new_v[:, ds(kv * HD, HD)], kvout[:, 1, :]).then_inc(s_kvst, 16)
                        if kind == "g":
                            sub = m // 2 - 1
                            if sub == 1 and not last:
                                J.sp_load(sp, kv * 5 + 5, kv_columns(kv + 1))
                            sp.wait_ge(s_og, at(kv * (2 * NT) + (sub + 1) * NT))
                            sp.dma_start(E.ogT_dram[ds(kv * 2 + sub, 1), :, :].rearrange("a p t -> (a p) t"), gT[:, :]).then_inc(s_ogst, 16)
                all_heads(sp, NKV, head)
                sp.wait_ge(s_ogst, at(16 * 2 * NKV))
                sp.wait_ge(s_kvst, at(32 * NKV))

            @block.gpsimd
            def _(pool):
                pool.memset(kT[:, KPAD:KPAD + P], 0.0).then_inc(s_pad, 1)
                pool.memset(kT[:, KREQ - P:KREQ], 0.0).then_inc(s_pad, 1)
                pool.memset(vS[:, KPAD // P, :, :], 0.0).then_inc(s_pad, 1)
                pool.memset(vS[:, KREQ // P - 1, :, :], 0.0).then_inc(s_pad, 1)
                J.pool_hi(pool, 0, 2)

                def head(kv, last):
                    rope = 0
                    for m, kind in enumerate(kinds):
                        if kind == "g":
                            if m < 4:
                                J.pool_hi(pool, kv * 5 + m + 1, kv * 6 + m + 3)
                            base = kv * (2 * NU) + (m // 2 - 1) * NU
                            bbase = kv * (2 * NT) + (m // 2 - 1) * NT
                            for w in range(NU):
                                b, hh = w // 2, w % 2
                                pool.wait_ge(s_rd, at(bbase + b + 1))
                                settle(E, pool)
                                x = prob[w % 4][:, 0:(640 if b < CTX else P)]
                                pool.tensor_scalar(x, x, rden[:, b % 2, hh:hh + 1], None, ALU.mult).then_inc(s_pn, 1)
                            if m == 4 and not last:
                                J.pool_hi(pool, kv * 5 + 5, kv * 6 + 8)
                            continue
                        rows, dst, off = (HD, kT, KLAT) if kind == "kv" else (P, qT, 0)
                        for g in range(NG):
                            t0, wl, wc = lat_ctx(g)
                            b = rope % 2
                            if g == NG - 1:
                                J.pool_hi(pool, kv * 5 + m + 1, kv * 6 + m + 3)
                            pool.wait_ge(s_shuf, at(kv * ROPES + rope + 1))
                            pool.wait_ge(s_cos, at(kv * ROPES + rope + 1))
                            prod = pool.tensor_tensor(shuf[b][0:rows, 0:wl], shuf[b][0:rows, 0:wl],
                                                      cs[b][0:rows, 1, 0:wl], ALU.mult)
                            prod.then_inc(s_sin, 1)
                            pool.wait_ge(s_sin, at(kv * ROPES + rope + 1))
                            o = dst[0:rows, off + t0:off + t0 + wl]
                            pool.tensor_tensor(o, o, shuf[b][0:rows, 0:wl], ALU.add).then_inc(s_rope, 1)
                            rope += 1

                all_heads(pool, NKV, head)

            @block.scalar
            def _(act):
                act.wait_ge(s_const, at(16))
                act.mul(nsink[:, :], sink[:, :], -1.0).then_inc(s_const, 1)
                with act.Fori(0, NKV) as kv:
                    for g in range(NG):
                        t0, wl, wc = lat_ctx(g)
                        act.wait_ge(s_rope, at(kv * ROPES + g + 1))
                        if wc:
                            act.wait_ge(s_release, at(kv * (5 * NG) + NG))
                        ins = act.copy(kT[HD:P, KLAT + t0:KLAT + t0 + wl], kT[0:HD, KLAT + t0:KLAT + t0 + wl])
                        if wc:
                            act.copy(kT[HD:P, KREQ:KREQ + P], kT[0:HD, KREQ:KREQ + P]).then_inc(s_kdup, 1)
                        else:
                            ins.then_inc(s_kdup, 1)
                    act.wait_ge(s_pv, at(kv * (2 * NT)))
                    for r, (a, z) in enumerate(VGROUPS):
                        act.wait_ge(s_vT, at(kv * 4 + r + 1))
                        n_lat = min(z, NS) - a
                        src = E.bank[4 + r][:, 0:(z - a) * HD].rearrange("p (t d) -> p t d", d=HD)
                        twice = lambda x, n: x.unsqueeze(2).to_broadcast([P, n, 2, HD])
                        if n_lat:
                            ins = act.copy(vS[:, VT_LAT + a:VT_LAT + a + n_lat, :, :], twice(src[:, 0:n_lat, :], n_lat))
                        if z > NS:
                            ins = act.copy(vS[:, VT_REQ:VT_REQ + 1, :, :], twice(src[:, CTX - a:CTX - a + 1, :], 1))
                        ins.then_inc(s_vS, 1)
                    act.wait_ge(s_kvst, at(kv * 32))
                    act.wait_ge(s_vT, at(kv * 4 + 4))
                    act.copy(kvout[:, 0, :], E.bank[7][:, 0:HD]).then_inc(s_kvo, 1)
                    act.copy(kvout[:, 1, :], E.bank[6][:, 0:HD]).then_inc(s_kvo, 1)
                    for sub in range(2):
                        for g in range(NG):
                            t0, t1 = GROUPS[g]
                            w = (t1 - t0) * P
                            u = NG * (2 + 2 * sub) + g
                            e = (sub * NG + g) % 2
                            act.wait_ge(J.s_unit, at(kv * (5 * NG) + u + 1))
                            act.wait_ge(s_release, at(kv * (5 * NG) + u - 1))
                            act.activation(gth[e][:, 0:w], E.bank[u % 4][:, 0:w], ACT.Tanh, scale=0.5).then_inc(s_gth, 1)
                        base = kv * (2 * NU) + sub * NU
                        bbase = kv * (2 * NT) + sub * NT

                        def sink_exp(b):
                            act.wait_ge(s_sarg, at(bbase + b + 1))
                            act.activation(esink[:, b % 2, :], sarg[:, b % 2, :], ACT.Exp).then_inc(s_es, 1)

                        def pT_copy(w):
                            b, hh = w // 2, w % 2
                            act.wait_ge(s_pT, at(base + w + 1))
                            if b < CTX:
                                act.wait_ge(s_pv, at(bbase + (b - 1 if b >= 2 else 0)))
                                act.copy(probT[b % 2][:, 3:5, hh, :],
                                         E.bank[5][:, 0:2 * P].rearrange("p (t q) -> p t q", t=2)).then_inc(s_pTc2, 1)
                            else:
                                act.sem_inc(s_pTc2, 1)

                        for s in range(NU + 3):
                            if s < NU:
                                w = s
                                b, hh = w // 2, w % 2
                                act.wait_ge(s_nm, at(base + w + 1))
                                act.wait_ge(s_pT, at(base + (w - 3 if w >= 4 else 0)))
                                act.wait_ge(s_den, at(bbase + (b - 1 if b >= 2 else 0)))
                                n = 640 if b < CTX else P
                                act.activation(prob[w % 4][:, 0:n], scores_of(w), ACT.Exp,
                                               bias=negm[:, b % 2, hh:hh + 1], scale=HD ** -0.5,
                                               accum_out=rsum[:, b % 2, hh:hh + 1]).then_inc(s_p, 1)
                                if hh == 1:
                                    sink_exp(b)
                            if s >= 3:
                                pT_copy(s - 3)

            @block.vector
            def _(dve):
                dve.wait_ge(s_const, at(17))

                def rope_unit(kv, rope, u, rows, dst, off, req, g):
                    t0, wl, wc = lat_ctx(g)
                    b = rope % 2
                    bank = E.bank[u % 4]
                    dve.wait_ge(J.s_unit, at(kv * (5 * NG) + u + 1))
                    dve.wait_ge(s_rope, at(kv * ROPES + (rope - 1 if rope >= 2 else 0)))
                    settle(E, dve)
                    dve.stream_shuffle(shuf[b][0:rows, 0:wl], bank[0:rows, 0:wl], SWAP).then_inc(s_shuf, 1)
                    dve.wait_ge(s_cs[b], at(kv * (16 * (8 - b)) + 16 * (rope // 2 + 1)))
                    ins = dve.tensor_tensor(dst[0:rows, off + t0:off + t0 + wl], bank[0:rows, 0:wl],
                                            cs[b][0:rows, 0, 0:wl], ALU.mult)
                    ins.then_inc(s_cos, 1)
                    if wc:
                        ins = dve.tensor_copy(dst[0:rows, req:req + P], bank[0:rows, wl:wl + P])
                    return ins

                J.dve_lo(dve, 0)

                def head(kv, last):
                    rope = 0
                    for m, kind in enumerate(kinds):
                        for g in range(NG):
                            u = NG * m + g
                            t0, t1 = GROUPS[g]
                            w = (t1 - t0) * P
                            tok = slice(t0 * P, t1 * P)
                            if g == NG - 1 and m < 4:
                                J.dve_lo(dve, kv * 5 + m + 1)
                            if kind == "kv":
                                if g == 0:
                                    dve.wait_ge(s_ogst, at(kv * 32))
                                    dve.wait_ge(s_S, at(kv * (2 * NU)))
                                rope_unit(kv, rope, u, HD, kT, KLAT, KREQ, g)
                                dve.tensor_copy(gT[HD:P, tok], E.bank[u % 4][HD:P, 0:w]).then_inc(s_release, 1)
                                rope += 1
                            elif kind == "q":
                                if g == 0 and m == 3:
                                    dve.wait_ge(s_S, at(kv * (2 * NU) + NU))
                                ins = rope_unit(kv, rope, u, P, qT, 0, CTX * P, g)
                                if lat_ctx(g)[2]:
                                    ins.then_inc(s_release, 1)
                                else:
                                    dve.wait_ge(s_cos, at(kv * ROPES + rope + 1))
                                    dve.sem_inc(s_release, 1)
                                rope += 1
                            else:
                                e = ((m // 2 - 1) * NG + g) % 2
                                if g == 0 and m == 2:
                                    dve.wait_ge(s_vT, at(kv * 4 + 4))
                                if g == 0 and m == 4:
                                    dve.wait_ge(s_ogst, at(kv * 32 + 16))
                                dve.wait_ge(s_gth, at(kv * (2 * NG) + (m // 2 - 1) * NG + g + 1))
                                dve.scalar_tensor_tensor(gT[:, tok], gth[e][:, 0:w], 1.0, E.bank[u % 4][:, 0:w],
                                                         ALU.add, ALU.mult).then_inc(s_release, 1)
                        if m not in (2, 4):
                            continue
                        sub = m // 2 - 1
                        base = kv * (2 * NU) + sub * NU
                        bbase = kv * (2 * NT) + sub * NT

                        def softmax_max(w):
                            b, hh = w // 2, w % 2
                            head = kv * 4 + (2 * sub + hh)
                            dve.wait_ge(s_S, at(base + w + 1))
                            dve.tensor_reduce(mx[:, w % 2:w % 2 + 1], scores_of(w), AX.X, ALU.max).then_inc(s_mx, 1)
                            dve.wait_ge(s_mx, at(base + w + 1))
                            dve.wait_ge(s_p, at(base + (2 * b - 2 if b >= 2 else 0)))
                            dve.wait_ge(s_sarg, at(bbase + (b - 1 if b >= 2 else 0)))
                            dve.tensor_scalar(negm[:, b % 2, hh:hh + 1], mx[:, w % 2:w % 2 + 1], -(HD ** -0.5),
                                              nsink[:, ds(head, 1)], ALU.mult, ALU.min).then_inc(s_nm, 1)
                            if hh == 1:
                                dve.wait_ge(s_nm, at(base + w + 1))
                                dve.wait_ge(s_es, at(bbase + (b - 1 if b >= 2 else 0)))
                                dve.tensor_tensor(sarg[:, b % 2, :], negm[:, b % 2, :],
                                                  sink[:, ds(kv * 4 + 2 * sub, 2)], ALU.add).then_inc(s_sarg, 1)

                        def pT_copy(w):
                            b, hh = w // 2, w % 2
                            dve.wait_ge(s_pT, at(base + w + 1))
                            dve.wait_ge(s_pv, at(bbase + (b - 1 if b >= 2 else 0)))
                            n = 3 if b < CTX else 1
                            dve.tensor_copy(probT[b % 2][:, 0:n, hh, :],
                                            E.bank[4][:, 0:n * P].rearrange("p (t q) -> p t q", t=n)).then_inc(s_pTc, 1)

                        def denominators(b):
                            p = b % 2
                            dve.wait_ge(s_p, at(base + 2 * b + 2))
                            dve.wait_ge(s_es, at(bbase + b + 1))
                            dve.tensor_tensor(den[:, p, :], rsum[:, p, :], esink[:, p, :], ALU.add).then_inc(s_den, 1)
                            dve.wait_ge(s_den, at(bbase + b + 1))
                            dve.wait_ge(s_pn, at(base + (2 * b - 2 if b >= 2 else 0)))
                            dve.reciprocal(rden[:, p, :], den[:, p, :]).then_inc(s_rd, 1)

                        def gate(b):
                            dve.wait_ge(s_pv, at(bbase + b + 1))
                            for hh in range(2):
                                g = gT[HD * hh:HD * hh + HD, b * P:(b + 1) * P]
                                ins = dve.scalar_tensor_tensor(
                                    g, E.bank[6 + b % 2][HD * hh:HD * hh + HD, hh * P:(hh + 1) * P], 0.5, g,
                                    ALU.mult, ALU.mult)
                            ins.then_inc(s_og, 1)

                        for s in range(NU + 5):
                            if s < NU:
                                softmax_max(s)
                            if s >= 2 and s % 2 == 0 and (s - 2) // 2 < NT:
                                denominators((s - 2) // 2)
                            if 3 <= s < NU + 3:
                                pT_copy(s - 3)
                            if s >= 6 and s % 2 == 0:
                                gate((s - 6) // 2)
                            if s == NU + 3 and m == 4 and not last:
                                J.dve_lo(dve, kv * 5 + 5)

                all_heads(dve, NKV, head)

            @block.tensor
            def _(pe):
                pe.wait_ge(s_pad, at(4))
                with pe.Fori(0, NKV) as kv:
                    for m, kind in enumerate(kinds):
                        for g in range(NG):
                            u = NG * m + g
                            if u >= 4:
                                pe.wait_ge(s_release, at(kv * (5 * NG) + u - 3))
                            if u < 4 and m == 0:
                                pe.wait_ge(s_p, at(kv * (2 * NU)))
                            if m == 3:
                                pe.wait_ge(s_p, at(kv * (2 * NU) + NU))
                            J.pe_unit(pe, kv * 5 + m, g, E.bank[u % 4])
                        if kind == "kv":
                            pe.wait_ge(s_release, at(kv * (5 * NG) + NG))
                            pe.wait_ge(s_og, at(kv * (2 * NT)))
                            pe.wait_ge(s_pTc, at(kv * (2 * NU)))
                            pe.wait_ge(s_pTc2, at(kv * (2 * NU)))
                            settle(E, pe)
                            for r, (a, z) in enumerate(VGROUPS):
                                for t in range(a, z):
                                    ins = pe.transpose(E.bank[4 + r][:, (t - a) * HD:(t - a + 1) * HD],
                                                       gT[HD:P, t * P:(t + 1) * P], E.ident[HD:P, HD:P])
                                ins.then_inc(s_vT, 1)
                            pe.wait_ge(s_kdup, at(kv * NG + NG))
                            pe.transpose(E.bank[7][:, 0:P], kT[:, KREQ:KREQ + P], E.ident[:, :]).then_inc(s_vT, 1)
                        if m not in (2, 4):
                            continue
                        sub = m // 2 - 1
                        base = kv * (2 * NU) + sub * NU
                        bbase = kv * (2 * NT) + sub * NT
                        pe.wait_ge(s_rope, at(kv * ROPES + NG * (2 + sub)))
                        pe.wait_ge(s_release, at(kv * (5 * NG) + NG * (m + 1)))
                        if sub == 0:
                            pe.wait_ge(s_kdup, at(kv * NG + NG))
                            pe.wait_ge(s_vS, at(kv * 3 + 3))
                            pe.wait_ge(s_kvo, at(kv * 2 + 2))
                            pe.wait_ge(s_ckl, at(kv * 16 + 16))
                            pe.wait_ge(s_cvl, at(kv * 32 + 32))

                        def scores(w):
                            b, hh = w // 2, w % 2
                            if w >= 2:
                                pe.wait_ge(s_p, at(base + w - 1))
                            r = slice(HD * hh, HD * hh + HD)
                            q = qT[r, b * P:(b + 1) * P]
                            s0, s1 = E.bank[2 * (w % 2)], E.bank[2 * (w % 2) + 1]
                            if b == CTX:
                                pe.matmul(s1[:, 0:P], q, kT[r, KREQ:KREQ + P], start=True, stop=True).then_inc(s_S, 1)
                                return
                            mask = 0 if b == 0 else 2 if b == NS - 1 else 1
                            k0 = KLAT + (b - 1) * P
                            pe.matmul(s0[:, 256:512], q, kT[r, 0:PAST], start=True, stop=True)
                            pe.matmul(s1[:, 0:3 * P], q, kT[r, k0:k0 + 3 * P], start=True, stop=False)
                            pe.matmul(s1[:, 0:3 * P], E.identb[:, :], E.wmask[:, mask, :], start=False,
                                      stop=True).then_inc(s_S, 1)

                        def turn(w):
                            b = w // 2
                            pe.wait_ge(s_pn, at(base + w + 1))
                            if w >= 1:
                                pe.wait_ge(s_pTc, at(base + w))
                                pe.wait_ge(s_pTc2, at(base + w))
                            for t in range(5 if b < CTX else 1):
                                out = E.bank[4 + t // 3][:, (t % 3) * P:(t % 3 + 1) * P]
                                ins = pe.transpose(out, prob[w % 4][:, t * P:(t + 1) * P], E.ident[:, :])
                            ins.then_inc(s_pT, 1)

                        def pv(b):
                            pe.wait_ge(s_pTc, at(base + 2 * b + 2))
                            pe.wait_ge(s_pTc2, at(base + 2 * b + 2))
                            pe.wait_ge(s_og, at(bbase + (b - 1 if b >= 2 else 0)))
                            tiles = [0, 1] + [VT_LAT + b + x for x in (-1, 0, 1)] if b < CTX else [VT_REQ]
                            for t, v in enumerate(tiles):
                                ins = pe.matmul(E.bank[6 + b % 2][:, 0:2 * P], vS[:, v, :, :].rearrange("p a d -> p (a d)"),
                                                probT[b % 2][:, t, :, :].rearrange("p h q -> p (h q)"),
                                                start=(t == 0), stop=(t == len(tiles) - 1))
                            ins.then_inc(s_pv, 1)

                        for s in range(NU + 4):
                            if s < NU:
                                scores(s)
                            if s >= 5 and s % 2 == 1:
                                pv((s - 5) // 2)
                            if 3 <= s < NU + 3:
                                turn(s - 3)


def phase_out(E, layer):
    nc = E.nc
    last_layer = layer == 1
    with ExitStack() as ctx:
        sb = lambda n, s, d=F32: ctx.enter_context(nc.sbuf_tensor(f"{n}_out{layer}", s, d))
        sem = lambda n: E.semaphore(f"{n}_out{layer}")
        w = sb("w", [P, KT, D])
        og = [sb(f"og{j}", [P, KT, P]) for j in range(2)]
        xb = [sb(f"xb{j}", [P, D]) for j in range(2)]
        scaled = sb("scaled", [P, D])
        gbc = sb("gbc", [P, D])
        s_w = [sem(f"w_loaded{half}") for half in range(2)]
        s_fw, s_g, s_y, s_t, s_x1 = (sem(x) for x in (
            "final_weight_loaded", "gate_loaded", "y_done", "y_gated", "residual_added"))
        s_og = [sem(f"og_loaded{j}") for j in range(2)]
        s_x = [sem(f"x_loaded{j}") for j in range(2)]
        s_st = [sem(f"stored{j}") for j in range(2)]
        if last_layer:
            w_hi, w_lo = sb("w_hi", [P, KT, D], F32R), sb("w_lo", [P, KT, D], F32R)
            og_hi = [sb(f"og_hi{j}", [P, KT, P], F32R) for j in range(2)]
            og_lo = [sb(f"og_lo{j}", [P, KT, P], F32R) for j in range(2)]
            fw = sb("fw", [P, D])
            y = [sb(f"y{j}", [P, D]) for j in range(2)]
            ss, std, rs = sb("ss", [P, 2]), sb("std", [P, 2]), sb("rs", [P, 2])
            s_whi, s_wlo, s_oghi, s_oglo, s_sq, s_std, s_rs, s_xn, s_junk = (sem(x) for x in (
                "w_hi_ready", "w_lo_ready", "og_hi_ready", "og_lo_ready", "sum_of_squares",
                "root_mean_square", "rms_reciprocal", "normalised", "junk"))
            x_read = s_xn

        def residual_ready(eng, n, j):
            eng.wait_ge(s_x1, over(n))

        if not last_layer:
            N = NormTranspose(E, ctx, 1, xb, residual_ready)
            x_read = N.s_xn
        def split_hi(act, n, j, i):
            act.wait_ge(s_og[j], i * 16 + 16)
            act.wait_ge(s_y, free(n))
            act.copy(og_hi[j][:, :, :], og[j][:, :, :]).then_inc(s_oghi, 1)

        def split_lo(dve, n, j):
            dve.wait_ge(s_oghi, over(n))
            dve.tensor_tensor(og_lo[j][:, :, :], og[j][:, :, :], og_hi[j][:, :, :], ALU.subtract).then_inc(s_oglo, 1)

        ybank = [E.PS[:, 0:2, :], E.PS[:, 2:4, :]]
        w_out = (E.a["mlstm_w_out"] if last_layer else E.a["attn_w_out"])[0]

        with nc.Block() as block:
            @block.sync
            def _(sp):
                sp.dma_start(gbc[:, :], E.gates_dram[layer, 0:1, :].partition_broadcast(P)).then_inc(s_g, 16)
                if last_layer:
                    sp.dma_start(fw[:, :], E.a["final_norm_w"].rearrange("(a n) -> a n", a=1).partition_broadcast(P)).then_inc(s_fw, 16)

                for s in s_st:
                    sp.sem_inc(s, 1)

                def tile(n, j, i, last):
                    sp.wait_ge(s_oglo if last_layer else s_y, free(n))
                    settle(E, sp)
                    with nc.allow_non_contiguous_dma(reason="512-byte rows"):
                        sp.dma_start(og[j][:, :, :], E.ogT_dram[:, :, ds(n * P, P)].rearrange("k p t -> p k t")).then_inc(s_og[j], 16)
                    sp.wait_ge(x_read, free(n))
                    settle(E, sp)
                    sp.wait_ge(s_st[j], i * 16 + 1)
                    settle(E, sp)
                    if last_layer:
                        src = E.x1_dram[ds(n * P, P), :]
                    else:
                        src = E.a["x_prompt"][0] if last else E.x_tile(n)
                    sp.dma_start(xb[j][:, :], src).then_inc(s_x[j], 16)
                    if last:
                        sp.wait_ge(s_t, over(NS - 1))
                        sp.dma_start(gbc[:, :], E.gates_dram[layer, 1:2, :].partition_broadcast(P)).then_inc(s_g, 16)
                pair_loop(sp, tile)
                sp.wait_ge(s_st[0], 16 * (NS // 2 + 1) + 1)
                sp.wait_ge(s_st[1], 16 * (NS // 2) + 1)

            @block.gpsimd
            def _(pool):
                pool.sem_inc(s_x1, 2)
                if not last_layer:
                    pool.sem_inc(N.s_hi, 2)

                def tile(n, j, i, last):
                    pool.wait_ge(s_t, over(n))
                    pool.wait_ge(s_x[j], i * 16 + 16)
                    pool.tensor_tensor(xb[j][:, :], xb[j][:, :], scaled[:, :], ALU.add).then_inc(s_x1, 1)
                    if not last_layer:
                        N.pool_hi(pool, n, j)
                pair_loop(pool, tile)

            @block.scalar
            def _(act):
                for half in range(2):
                    k = slice(4 * half, 4 * half + 4)
                    act.dma_start(w[:, k, :], w_out.rearrange("(k p) m -> p k m", p=P)[:, k, :]).then_inc(s_w[half], 16)
                if last_layer:
                    for s in (s_sq, s_std, s_oghi):
                        act.sem_inc(s, 2)
                    for k in range(KT):
                        if k % 4 == 0:
                            act.wait_ge(s_w[k // 4], 16)
                        act.copy(w_hi[:, k, :], w[:, k, :]).then_inc(s_whi, 1)
                        if k == 1:
                            split_hi(act, 0, 0, 0)
                else:
                    N.credits_act(act)

                def tile(n, j, i, last):
                    if last_layer and not last:
                        split_hi(act, n + 1, 1 - j, i + j)
                    residual_ready(act, n, j)
                    if not last_layer:
                        act.dma_start(E.x1_dram[ds(n * P, P), :], xb[j][:, :]).then_inc(s_st[j], 16)
                        N.act_stats(act, n, j)
                        N.act_modulate(act, n, j, 1 if last else 0)
                        return
                    act.wait_ge(s_xn, free(n))
                    act.wait_ge(s_st[j], i * 16 + 1)
                    act.activation(y[j][:, :], xb[j][:, :], ACT.Square, accum_out=ss[:, j:j + 1]).then_inc(s_sq, 1)
                    act.wait_ge(s_sq, over(n))
                    act.wait_ge(s_rs, free(n))
                    act.activation(std[:, j:j + 1], ss[:, j:j + 1], ACT.Sqrt, bias=E.eps[:, 0:1],
                                   scale=1.0 / D).then_inc(s_std, 1)
                    act.wait_ge(s_xn, over(n))
                    act.dma_start(E.out_prompt if last else E.out_sample[ds(n * P, P), :], y[j][:, :]).then_inc(s_st[j], 16)
                pair_loop(act, tile)

            @block.vector
            def _(dve):
                dve.sem_inc(s_t, 2)
                if last_layer:
                    for s in (s_oglo, s_rs, s_xn):
                        dve.sem_inc(s, 2)
                    for k in range(KT):
                        dve.wait_ge(s_whi, k + 1)
                        dve.tensor_tensor(w_lo[:, k, :], w[:, k, :], w_hi[:, k, :], ALU.subtract).then_inc(s_wlo, 1)
                        if k == 1:
                            split_lo(dve, 0, 0)
                    dve.wait_ge(s_fw, 16)
                else:
                    N.credits_dve(dve)

                def tile(n, j, i, last):
                    if last_layer and not last:
                        split_lo(dve, n + 1, 1 - j)
                    dve.wait_ge(s_y, over(n))
                    dve.wait_ge(s_g, 32 if last else 16)
                    dve.wait_ge(s_x1, free(n + 1))
                    dve.tensor_tensor(scaled[:, :].rearrange("p (a n) -> p a n", a=2), ybank[j],
                                      gbc[:, :].rearrange("p (a n) -> p a n", a=2), ALU.mult).then_inc(s_t, 1)
                    if not last_layer:
                        N.dve_normalise(dve, n, j)
                        N.dve_modulate(dve, n, j, 1 if last else 0)
                        N.dve_lo(dve, n, j)
                        return
                    dve.wait_ge(s_std, over(n))
                    dve.wait_ge(s_xn, free(n))
                    dve.reciprocal(rs[:, j:j + 1], std[:, j:j + 1]).then_inc(s_rs, 1)
                    dve.wait_ge(s_rs, over(n))
                    dve.wait_ge(s_sq, over(n))
                    dve.scalar_tensor_tensor(y[j][:, :], xb[j][:, :], rs[:, j:j + 1], fw[:, :],
                                             ALU.mult, ALU.mult).then_inc(s_xn, 1)
                pair_loop(dve, tile)

            @block.tensor
            def _(pe):
                pe.sem_inc(s_y, 2)
                if not last_layer:
                    pe.sem_inc(N.s_tp, 2)

                def products(n, j, i):
                    if last_layer:
                        pe.wait_ge(s_oglo, over(n))
                    else:
                        pe.wait_ge(s_og[j], i * 16 + 16)
                    pe.wait_ge(s_t, free(n))
                    for half in range(2):
                        out = E.bank[2 * j + half][:, :]
                        c = slice(half * 512, half * 512 + 512)
                        for k in range(KT):
                            first, end = k == 0, k == KT - 1
                            if half == 0 and last_layer:
                                pe.wait_ge(s_wlo, k + 1)
                            elif half == 0 and k % 4 == 0:
                                pe.wait_ge(s_w[k // 4], 16)
                            if last_layer:
                                pe.matmul(out, og_lo[j][:, k, :], w_hi[:, k, c], start=first, stop=False)
                                pe.matmul(out, og_hi[j][:, k, :], w_lo[:, k, c], start=False, stop=False)
                                ins = pe.matmul(out, og_hi[j][:, k, :], w_hi[:, k, c], start=False, stop=end)
                            else:
                                ins = pe.matmul(out, og[j][:, k, :], w[:, k, c], start=first, stop=end)
                    ins.then_inc(s_y, 1)

                if last_layer:
                    pair_loop(pe, lambda n, j, i, last: products(n, j, i))
                else:
                    products(0, 0, 0)
                    with pe.Fori(0, NS // 2) as i:
                        products(i * 2 + 1, 1, i)
                        N.pe_transpose(pe, i * 2, 0)
                        products(i * 2 + 2, 0, i + 1)
                        N.pe_transpose(pe, i * 2 + 1, 1)
                    N.pe_transpose(pe, CTX, 0)


FWD, BWD = 0, 32
ROWS = 64
U_COL, WK_COL, EM_COL = 0, 1, 2


def reversed_cols(tile, width, p0, rows, first, n):
    return bass.AP(tensor=tile[:, :].tensor, offset=p0 * width + first + n - 1, ap=[[width, rows], [-1, n]])


def phase_gates(E):
    nc = E.nc
    with ExitStack() as ctx:
        sb = lambda n, s, d=F32: ctx.enter_context(nc.sbuf_tensor(f"gt_{n}", s, d))
        sem = lambda n: E.semaphore(f"gt_{n}")
        raw, w_hi, w_lo = sb("w", [P, KT, P]), sb("w_hi", [P, KT, P], F32R), sb("w_lo", [P, KT, P], F32R)
        bias = sb("bias", [P, 1])
        nat4 = sb("nat4", [P, 512])
        ig, lf, b, M, tmp, z, r = (sb(n, [ROWS, T]) for n in ("ig", "lf", "b", "M", "tmp", "z", "r"))
        entry, last_M, dec, m_out = sb("entry", [ROWS, NT]), sb("last_M", [ROWS, NT]), sb("dec", [ROWS, NT]), sb("m_out", [ROWS, 1])
        s_zero, s_w, s_hi, s_lo, s_unit, s_nat, s_spread, s_m0, s_d, s_a, s_dma, s_tr, s_col = (
            sem(x) for x in ("zeroed", "w_loaded", "w_hi", "w_lo", "unit", "biased", "spread", "m0_loaded",
                             "dve_step", "act_step", "rows_stored", "turned", "columns"))
        w_in = E.a["mlstm_w_in"][0].rearrange("(k p) m -> p k m", p=P)
        chunks = lambda t: t[:, :].rearrange("p (c t) -> p c t", t=P)

        with nc.Block() as block:
            @block.sync
            def _(sp):
                sp.dma_start(E.causal[:, :, :], E.a["causal_mask"]).then_inc(s_m0, 16)
                sp.wait_ge(s_zero, 4)
                with nc.allow_non_contiguous_dma(reason="gate columns and short vectors"):
                    for q in range(4):
                        sp.dma_start(raw[:, :, 32 * q:32 * q + MH], w_in[:, :, 5 * D + MH * q:5 * D + MH * (q + 1)]).then_inc(s_w, 16)
                        sp.dma_start(bias[32 * q:32 * q + MH, :], E.a["mlstm_b_gates"][0, MH * q:MH * (q + 1)].rearrange("(p a) -> p a", a=1)).then_inc(s_w, 16)
                    for d, row in enumerate((FWD, BWD)):
                        sp.dma_start(entry[row:row + MH, 0:1], E.a["state_m"][0, 0, d].rearrange("(p a) -> p a", a=1)).then_inc(s_m0, 16)
                    sp.wait_ge(s_d, 10)
                    for d, row in enumerate((FWD, BWD)):
                        sp.dma_start(E.new_m[0, 0, d].rearrange("(p a) -> p a", a=1), m_out[row:row + MH, :]).then_inc(s_dma, 16)
                    sp.wait_ge(s_a, 4)
                    for d, row in enumerate((FWD, BWD)):
                        sp.dma_start(E.decay_dram[d], dec[row:row + MH, :]).then_inc(s_dma, 16)
                    rows = E.rows_dram.rearrange("h c q t -> q h c t")
                    sp.dma_start(rows[0], chunks(M)[FWD:FWD + MH]).then_inc(s_dma, 16)
                    sp.wait_ge(s_a, 5)
                    sp.dma_start(rows[2], chunks(tmp)[FWD:FWD + MH]).then_inc(s_dma, 16)
                    sp.wait_ge(s_d, 14)
                    sp.dma_start(rows[1], chunks(r)[BWD:BWD + MH]).then_inc(s_dma, 16)
                    sp.dma_start(rows[3], chunks(b)[BWD:BWD + MH]).then_inc(s_dma, 16)
                sp.wait_ge(s_dma, 128)
                sp.dma_start(E.decay[:, :, :, :], E.decay_dram.rearrange("d h c -> (d h c)").rearrange("(a n) -> a n", a=1).partition_broadcast(P)).then_inc(s_dma, 16)
                sp.wait_ge(s_dma, 144)

            @block.gpsimd
            def _(pool):
                pool.memset(raw[:, :, :], 0.0).then_inc(s_zero, 1)
                pool.memset(bias[:, :], 0.0).then_inc(s_zero, 1)
                pool.memset(entry[:, :], 0.0).then_inc(s_zero, 1)
                pool.memset(ig[:, :], 0.0).then_inc(s_zero, 1)
                pool.memset(lf[:, :], 0.0).then_inc(s_zero, 1)
                pool.memset(z[:, :], 0.0).then_inc(s_zero, 1)
                pool.memset(r[:, :], 1.0).then_inc(s_zero, 1)
                pool.wait_ge(s_zero, 7)
                pool.memset(chunks(r)[:, :, 0:1], 0.0).then_inc(s_zero, 1)
                pool.wait_ge(s_w, 128)
                pool.tensor_copy(w_hi[:, :, :], raw[:, :, :]).then_inc(s_hi, 1)

            @block.tensor
            def _(pe):
                pe.wait_ge(s_lo, 1)
                for g, (t0, t1) in enumerate(GROUPS):
                    tok = slice(t0 * P, t1 * P)
                    out = E.bank[g][:, 0:(t1 - t0) * P]
                    for k in range(KT):
                        pe.matmul(out, w_lo[:, k, :], E.h_hi[:, k, tok], start=(k == 0), stop=False)
                        pe.matmul(out, w_hi[:, k, :], E.h_lo[:, k, tok], start=False, stop=False)
                        ins = pe.matmul(out, w_hi[:, k, :], E.h_hi[:, k, tok], start=False, stop=(k == KT - 1))
                    ins.then_inc(s_unit, 1)
                for q, (src, ready) in enumerate(((lf, 18), (ig, 20), (M, 20))):
                    pe.wait_ge(s_d, ready)
                    if q == 0:
                        pe.wait_ge(s_nat, NG)
                    for c in range(NT):
                        g = 3 * q + c // 8
                        if g == 8 and c == 16:
                            pe.wait_ge(s_col, 1)
                        ins = pe.transpose(E.bank[g % 8][:, (c % 8) * ROWS:(c % 8 + 1) * ROWS],
                                           src[:, c * P:(c + 1) * P], E.ident[0:ROWS, 0:ROWS])
                    ins.then_inc(s_tr, 1)

            @block.scalar
            def _(act):
                act.wait_ge(s_w, 128)
                for g, (t0, t1) in enumerate(GROUPS):
                    act.wait_ge(s_unit, g + 1)
                    if g:
                        act.wait_ge(s_spread, g)
                    act.activation(nat4[:, 0:(t1 - t0) * P], E.bank[g][:, 0:(t1 - t0) * P], ACT.Identity,
                                   bias=bias[:, 0:1]).then_inc(s_nat, 1)
                act.wait_ge(s_spread, NG)
                act.activation(tmp[:, :], lf[:, :], ACT.Abs).then_inc(s_a, 1)
                act.wait_ge(s_a, 1)
                act.activation(tmp[:, :], tmp[:, :], ACT.Exp, scale=-1.0).then_inc(s_a, 1)
                act.wait_ge(s_a, 2)
                act.activation(tmp[:, :], tmp[:, :], ACT.Ln, bias=E.one[0:ROWS, 0:1]).then_inc(s_a, 1)
                act.wait_ge(s_d, 10)
                act.activation(dec[:, :], dec[:, :], ACT.Exp).then_inc(s_a, 1)
                act.wait_ge(s_d, 11)
                act.activation(tmp[:, :], tmp[:, :], ACT.Exp).then_inc(s_a, 1)
                act.wait_ge(s_d, 12)
                act.activation(z[:, :], z[:, :], ACT.Exp).then_inc(s_a, 1)
                act.wait_ge(s_d, 13)
                act.activation(lf[:, :], lf[:, :], ACT.Exp, scale=-1.0).then_inc(s_a, 1)

            @block.vector
            def _(dve):
                count = [0]

                def step(ins):
                    count[0] += 1
                    ins.then_inc(s_d, 1)
                    dve.wait_ge(s_d, count[0])

                dve.wait_ge(s_hi, 1)
                dve.tensor_tensor(w_lo[:, :, :], raw[:, :, :], w_hi[:, :, :], ALU.subtract).then_inc(s_lo, 1)
                dve.wait_ge(s_zero, 8)
                for g, (t0, t1) in enumerate(GROUPS):
                    dve.wait_ge(s_nat, g + 1)
                    lat = (min(t1, NS) - t0) * P
                    a = t0 * P
                    for dst, q in ((ig, 0), (lf, 1)):
                        dve.tensor_copy(dst[FWD:FWD + MH, a:t1 * P], nat4[32 * q:32 * q + MH, 0:(t1 - t0) * P])
                        if t1 > NS:
                            dve.tensor_copy(dst[BWD:BWD + MH, SAMPLE:T],
                                            reversed_cols(nat4, 512, 64 + 32 * q, MH, lat, P))
                        ins = dve.tensor_copy(dst[BWD:BWD + MH, SAMPLE - a - lat:SAMPLE - a],
                                              reversed_cols(nat4, 512, 64 + 32 * q, MH, 0, lat))
                    ins.then_inc(s_spread, 1)
                dve.wait_ge(s_a, 3)
                step(dve.scalar_tensor_tensor(lf[:, :], lf[:, :], 0.0, tmp[:, :], ALU.min, ALU.subtract))
                step(dve.tensor_tensor_scan(b[:, :], r[:, :], lf[:, :], 0.0, ALU.mult, ALU.add))
                step(dve.tensor_tensor(ig[:, :], ig[:, :], b[:, :], ALU.subtract))
                step(dve.tensor_copy(chunks(z)[:, 1:NS, 0:1], chunks(b)[:, 0:NS - 1, P - 1:P]))
                dve.wait_ge(s_m0, 48)
                step(dve.tensor_tensor_scan(M[:, 0:SAMPLE], z[:, 0:SAMPLE], ig[:, 0:SAMPLE], entry[:, 0:1],
                                            ALU.add, ALU.max))
                step(dve.tensor_tensor_scan(M[:, SAMPLE:T], z[:, SAMPLE:T], ig[:, SAMPLE:T], 0.0,
                                            ALU.add, ALU.max))
                step(dve.tensor_tensor(entry[:, 1:NS].unsqueeze(2), chunks(M)[:, 0:NS - 1, P - 1:P],
                                       chunks(b)[:, 0:NS - 1, P - 1:P], ALU.add))
                step(dve.tensor_copy(last_M[:, :].unsqueeze(2), chunks(M)[:, :, P - 1:P]))
                step(dve.tensor_tensor(m_out[:, :], M[:, T - 1:T], b[:, T - 1:T], ALU.add))
                step(dve.tensor_tensor(dec[:, :], entry[:, :], last_M[:, :], ALU.subtract))
                bc = lambda t: t[:, :].unsqueeze(2).to_broadcast([ROWS, NT, P])
                step(dve.tensor_tensor(chunks(tmp), bc(entry), chunks(M), ALU.subtract))
                step(dve.tensor_tensor(chunks(z), chunks(ig), bc(last_M), ALU.subtract))
                step(dve.tensor_tensor(lf[:, :], b[:, :], M[:, :], ALU.add))
                dve.wait_ge(s_a, 7)

                def turned(dst, src):
                    dve.tensor_copy(dst[BWD:BWD + MH, SAMPLE:T], reversed_cols(src, T, BWD, MH, SAMPLE, P))
                    return dve.tensor_copy(dst[BWD:BWD + MH, 0:SAMPLE], reversed_cols(src, T, BWD, MH, 0, SAMPLE))
                turned(r, M)
                step(turned(b, tmp))
                dve.wait_ge(s_dma, 128)
                step(dve.tensor_copy(M[:, :], lf[:, :]))
                step(turned(M, lf))
                step(dve.tensor_copy(lf[:, :], ig[:, :]))
                step(turned(lf, ig))
                step(dve.tensor_copy(ig[:, :], z[:, :]))
                step(turned(ig, z))
                for q in range(3):
                    dve.wait_ge(s_tr, q + 1)
                    for x in range(3):
                        n = min(8, NT - 8 * x)
                        src = E.bank[(3 * q + x) % 8][:, 0:n * ROWS].rearrange("p (c d y) -> p c d y", d=2, y=32)
                        ins = dve.tensor_copy(E.cols[:, 8 * x:8 * x + n, q, :, :], src[:, :, :, 0:MH])
                    ins.then_inc(s_col, 1)


def phase_mlstm(E):
    nc = E.nc
    NB = 5
    E1 = MHD + 1
    with ExitStack() as ctx:
        sb = lambda n, s, d=F32: ctx.enter_context(nc.sbuf_tensor(f"m_{n}", s, d))
        sem = lambda n: E.semaphore(f"m_{n}")
        kT, qT, gT = sb("kT", [P, T]), sb("qT", [P, T]), sb("gT", [P, T])
        v1 = sb("v1", [P, NT, E1])
        CC = sb("states", [P, 2, NS + 1, E1])
        cout = sb("cout", [P, 2, E1])
        gth = sb("gth", [P, 512])
        kw = [gth[:, j * 2 * MHD:(j + 1) * 2 * MHD].rearrange("p (d k) -> p d k", d=2) for j in range(2)]
        bc = [sb(f"bc{x}", [P, 4, P]) for x in range(NB)]
        hc = sb("hc", [P, NT, 3, 2])
        dech = sb("dech", [P, 2, NT])
        den = [sb(f"den{j}", [P, 2]) for j in range(2)]
        rec = [sb(f"rec{j}", [P, 2]) for j in range(2)]
        part = [sb(f"part{j}", [P, MHD]) for j in range(2)]
        hm = [sb(f"hm{j}", [P, MHD]) for j in range(2)]
        J = Projection(E, ctx, "mlstm", 5)
        (s_ones, s_relA, s_relD, s_vT, s_v1, s_hc, s_st, s_kT, s_kw, s_kv, s_cf, s_kvb, s_rev, s_cst,
         s_gth, s_gd) = (sem(x) for x in (
            "ones", "bank_free_act", "bank_free_dve", "v_turned", "v_stored", "head_columns", "state_loaded",
            "k_turned", "weighted_keys", "kv_products", "forward_state", "kv_stored",
            "backward_state", "state_stored", "gate_tanh", "gate_steps"))
        s_bc = [sem(f"rows_loaded{x}") for x in range(NB)]
        (s_E, s_qw, s_W, s_S, s_P, s_num, s_den, s_rec, s_part, s_hm, s_hT, s_og, s_ogst) = (sem(x) for x in (
            "exponent", "q_weighted", "weights", "scores", "products", "num_done", "den", "recip", "part",
            "h_ready", "h_turned", "gated", "stored"))
        w_in = E.a["mlstm_w_in"][0].rearrange("(k p) m -> p k m", p=P)
        COL = {"k": D, "v": 2 * D, "q": 0, "o": 3 * D, "g": 4 * D}
        kinds = ["k", "v", "q", "o", "g"]
        NU = 5 * NG
        VG = [(0, 4), (4, 8), (8, 12), (12, 16), (16, 17)]
        VB = [4, 5, 6, 7, 4]

        num_bank = lambda c: E.bank[(2, 3, 6, 7)[c % 4]]

        def span(g):
            return slice(GROUPS[g][0] * P, GROUPS[g][1] * P), (GROUPS[g][1] - GROUPS[g][0]) * P

        E.start_at_one()
        with nc.Block() as block:
            @block.sync
            def _(sp):
                J.sp_load(sp, 0, [(0, w_in[:, :, D:D + P])])
                with sp.Fori(0, MH) as h:
                    def load(m):
                        J.sp_load(sp, h * 5 + m, [(0, w_in[:, :, ds(h * P + COL[kinds[m]], P)])])
                    load(1)
                    sp.wait_ge(s_num, at(h * NT))
                    settle(E, sp)
                    with nc.allow_non_contiguous_dma(reason="normaliser columns"):
                        for d, slot in ((0, 0), (1, NS)):
                            sp.dma_start(CC[:, d, slot, 0:MHD], E.a["state_C"][0, 0, d, ds(h, 1)].rearrange("a d e -> d (a e)")).then_inc(s_st, 16)
                            sp.dma_start(CC[:, d, slot, MHD:E1], E.a["state_n"][0, 0, d, ds(h, 1)].rearrange("a d -> d a")).then_inc(s_st, 16)
                    for m in (2, 3, 4):
                        load(m)
                    with nc.allow_non_contiguous_dma(reason="normaliser columns"):
                        sp.wait_ge(s_kvb, at(h * NT + NT))
                        settle(E, sp)
                        for d in range(2):
                            sp.dma_start(E.new_C[0, 0, d, ds(h, 1)].rearrange("a d e -> d (a e)"), cout[:, d, 0:MHD]).then_inc(s_cst, 16)
                            sp.dma_start(E.new_n[0, 0, d, ds(h, 1)].rearrange("a d -> d a"), cout[:, d, MHD:E1]).then_inc(s_cst, 16)
                    J.sp_load(sp, h * 5 + 5, [(0, w_in[:, :, ds(h * P + (D + P), P)])])
                    for c in range(NT):
                        x = c % NB
                        sp.wait_ge(s_num, at(h * NT + max(c - NB + 1, 0)))
                        settle(E, sp)
                        row = E.rows_dram[ds(h, 1), c, :, :].rearrange("a q t -> a (q t)")
                        sp.dma_start(bc[x][:, :, :].rearrange("p q t -> p (q t)"), row.partition_broadcast(P)).then_inc(s_bc[x], 16)
                    sp.wait_ge(s_og, at(h * NT + NT))
                    settle(E, sp)
                    sp.dma_start(E.ogT_dram[ds(h, 1), :, :].rearrange("a p t -> (a p) t"), gT[:, :]).then_inc(s_ogst, 16)
                sp.wait_ge(s_ogst, at(16 * MH))
                sp.wait_ge(s_cst, at(64 * MH))

            @block.gpsimd
            def _(pool):
                pool.memset(v1[:, :, MHD:E1], 1.0).then_inc(s_ones, 1)
                J.pool_hi(pool, 0, 1)
                with pool.Fori(0, MH) as h:
                    pool.wait_ge(s_og, at(h * NT))
                    settle(E, pool)
                    pool.tensor_copy(hc[:, :, :, :], E.cols[:, :, :, :, ds(h, 1)].rearrange("p c q d a -> p c q (d a)")).then_inc(s_hc, 1)
                    pool.tensor_copy(dech[:, :, :], E.decay[:, :, ds(h, 1), :].rearrange("p d a c -> p d (a c)")).then_inc(s_hc, 1)
                    for m in range(1, 5):
                        J.pool_hi(pool, h * 5 + m, h * 5 + m + 1)
                    for c in range(NT):
                        x = c % NB
                        per = -((x - NT) // NB)
                        pool.wait_ge(s_bc[x], at(h * (16 * per) + 16 * (c // NB + 1)))
                        pool.tensor_tensor(bc[x][:, 0:2, :], bc[x][:, 0:2, :], E.causal[:, :, :], ALU.add).then_inc(s_E, 1)
                        q = qT[:, c * P:(c + 1) * P].unsqueeze(1).to_broadcast([P, 2, P])
                        pool.tensor_tensor(bc[x][:, 2:4, :], bc[x][:, 2:4, :], q, ALU.mult).then_inc(s_qw, 1)

            @block.scalar
            def _(act):
                with act.Fori(0, MH) as h:
                    def evac(u):
                        m, g = u // NG, u % NG
                        tok, w = span(g)
                        act.wait_ge(J.s_unit, at(h * NU + u + 1))
                        src = E.bank[u % 4][:, 0:w]
                        if kinds[m] == "k":
                            act.activation(kT[:, tok], src, ACT.Copy, scale=MHD ** -0.5).then_inc(s_relA, 1)
                        elif kinds[m] == "v":
                            act.copy(gT[:, tok], src).then_inc(s_relA, 1)
                        elif kinds[m] == "q":
                            act.copy(qT[:, tok], src).then_inc(s_relA, 1)
                        elif kinds[m] == "o":
                            act.activation(gT[:, tok], src, ACT.Tanh, scale=0.5).then_inc(s_relA, 1)
                        else:
                            act.wait_ge(s_relD, at(h * NG + g))
                            act.activation(gth[:, 0:w], src, ACT.Tanh, scale=0.5).then_inc(s_gth, 1)

                    act.wait_ge(s_S, at(h * NT))
                    for u in range(NG):
                        evac(u)
                    act.wait_ge(s_ogst, at(h * 16))
                    for u in range(NG, 2 * NG):
                        evac(u)
                    act.wait_ge(s_num, at(h * NT))
                    for r, (a, z) in enumerate(VG):
                        act.wait_ge(s_vT, at(h * 5 + r + 1))
                        act.copy(v1[:, a:z, 0:MHD], E.bank[VB[r]][:, 0:(z - a) * P].rearrange("p (c e) -> p c e", e=P)).then_inc(s_v1, 1)
                    act.wait_ge(s_qw, at(h * NT))
                    act.wait_ge(s_hc, at(h * 2 + 2))
                    for i in range(3 * NG):
                        evac(2 * NG + i)
                        for c in (2 * i - 1, 2 * i):
                            if 0 <= c < NT:
                                act.wait_ge(s_kv, at(h * NT + c + 1))
                                if c < CTX:
                                    dst = bass.AP(tensor=CC[:, :, :, :].tensor, offset=(c + 1) * E1,
                                                  ap=[[2 * (NS + 1) * E1, P], [NS * E1, 2], [1, E1]])
                                else:
                                    act.wait_ge(s_cst, at(h * 64))
                                    dst = cout[:, :, :]
                                act.copy(dst, E.bank[6 + c % 2][:, 0:2 * E1].rearrange("p (d e) -> p d e", d=2)).then_inc(s_kvb, 1)
                    def decay_weights(c):
                        act.wait_ge(s_E, at(h * NT + c + 1))
                        for d in range(2):
                            x = bc[c % NB][:, d, :]
                            ins = act.activation(x, x, ACT.Exp, bias=hc[:, c, U_COL, d:d + 1], scale=-1.0)
                        ins.then_inc(s_W, 1)

                    decay_weights(0)
                    for s in range(NT + 1):
                        if s + 1 < NT:
                            decay_weights(s + 1)
                        if s == 8:
                            J.act_hi(act, h * 5 + 5, h * 5 + 6)
                        c = s - 1
                        if c >= 0:
                            act.wait_ge(s_rec, at(h * NT + c + 1))
                            act.wait_ge(s_hm, at(h * NT + max(c - 1, 0)))
                            act.activation(part[c % 2][:, :], num_bank(c)[:, 0:MHD], ACT.Copy,
                                           scale=rec[c % 2][:, 0:1]).then_inc(s_part, 1)

            @block.vector
            def _(dve):
                J.dve_lo(dve, 0)
                with dve.Fori(0, MH) as h:
                    J.dve_lo(dve, h * 5 + 1)
                    J.dve_lo(dve, h * 5 + 2)
                    dve.wait_ge(s_hc, at(h * 2 + 2))
                    dve.wait_ge(s_st, at(h * 64 + 64))
                    for i in range(3 * NG):
                        u = 2 * NG + i
                        m, g = u // NG, u % NG
                        if g == NG - 1 and m < 4:
                            J.dve_lo(dve, h * 5 + m + 1)
                        if m == 4:
                            tok, w = span(g)
                            dve.wait_ge(s_gth, at(h * NG + g + 1))
                            dve.scalar_tensor_tensor(gth[:, 0:w], gth[:, 0:w], 1.0, E.bank[u % 4][:, 0:w],
                                                     ALU.add, ALU.mult).then_inc(s_gd, 1)
                            dve.wait_ge(s_gd, at(h * NG + g + 1))
                            dve.scalar_tensor_tensor(gT[:, tok], gT[:, tok], 1.0, gth[:, 0:w],
                                                     ALU.add, ALU.mult).then_inc(s_relD, 1)
                        for s in (2 * i, 2 * i + 1):
                            if s < NT:
                                dve.wait_ge(s_kT, at(h * NT + s + 1))
                                dve.wait_ge(s_kv, at(h * NT + max(s - 1, 0)))
                                keys = E.bank[4 + s % 2][:, 0:P].unsqueeze(1).to_broadcast([P, 2, P])
                                weights = hc[:, s, WK_COL, :].unsqueeze(2).to_broadcast([P, 2, P])
                                dve.tensor_tensor(kw[s % 2][:, :, :], keys, weights, ALU.mult).then_inc(s_kw, 1)
                        for c in (2 * i - 3, 2 * i - 2):
                            if 0 <= c < NS - 1:
                                dve.wait_ge(s_kvb, at(h * NT + c + 1))
                                dve.wait_ge(s_cf, at(h * (NS - 1) + c))
                                dve.scalar_tensor_tensor(CC[:, 0, c + 1, :], CC[:, 0, c, :], dech[:, 0, c:c + 1],
                                                         CC[:, 0, c + 1, :], ALU.mult, ALU.add).then_inc(s_cf, 1)
                        if i == 9:
                            dve.wait_ge(s_kvb, at(h * NT + NS))
                            for n, c in enumerate(range(NS - 1, 0, -1)):
                                dve.wait_ge(s_rev, at(h * (NS - 1) + n))
                                dve.scalar_tensor_tensor(CC[:, 1, c, :], CC[:, 1, c + 1, :], dech[:, 1, n:n + 1],
                                                         CC[:, 1, c, :], ALU.mult, ALU.add).then_inc(s_rev, 1)
                    for s in range(NT + 3):
                        if s == 12:
                            J.dve_lo(dve, h * 5 + 5)
                        if s < NT:
                            dve.wait_ge(s_S, at(h * NT + s + 1))
                            dve.wait_ge(s_W, at(h * NT + s + 1))
                            x = bc[s % NB][:, 0:2, :]
                            S = E.bank[s % 2][:, 0:P].unsqueeze(1).to_broadcast([P, 2, P])
                            dve.tensor_tensor(x, S, x, ALU.mult).then_inc(s_P, 1)
                        c = s - 1
                        if 0 <= c < NT:
                            num = num_bank(c)[:, 0:2 * E1].rearrange("p (d e) -> p d e", d=2)
                            dve.wait_ge(s_num, at(h * NT + c + 1))
                            floor = hc[:, c, EM_COL, :].unsqueeze(2)
                            d = den[c % 2][:, :].unsqueeze(2)
                            dve.scalar_tensor_tensor(d, num[:, :, MHD:E1], -1.0, floor, ALU.mult, ALU.max).then_inc(s_den, 1)
                            dve.wait_ge(s_den, at(h * (2 * NT) + 2 * c + 1))
                            dve.tensor_tensor(d, num[:, :, MHD:E1], d, ALU.max).then_inc(s_den, 1)
                            dve.wait_ge(s_den, at(h * (2 * NT) + 2 * c + 2))
                            dve.wait_ge(s_hm, at(h * NT + max(c - 1, 0)))
                            dve.reciprocal(rec[c % 2][:, :], den[c % 2][:, :]).then_inc(s_rec, 1)
                        c = s - 2
                        if 0 <= c < NT:
                            num = num_bank(c)[:, 0:2 * E1].rearrange("p (d e) -> p d e", d=2)
                            dve.wait_ge(s_part, at(h * NT + c + 1))
                            dve.wait_ge(s_hT, at(h * NT + max(c - 1, 0)))
                            dve.scalar_tensor_tensor(hm[c % 2][:, :], num[:, 1, 0:MHD], rec[c % 2][:, 1:2],
                                                     part[c % 2][:, :], ALU.mult, ALU.add).then_inc(s_hm, 1)
                        c = s - 3
                        if c >= 0:
                            dve.wait_ge(s_hT, at(h * NT + c + 1))
                            gtile = gT[:, c * P:(c + 1) * P]
                            dve.scalar_tensor_tensor(gtile, E.bank[4 + c % 2][:, 0:P], 0.25, gtile,
                                                     ALU.mult, ALU.mult).then_inc(s_og, 1)

            @block.tensor
            def _(pe):
                pe.wait_ge(s_ones, at(1))
                with pe.Fori(0, MH) as h:
                    def unit(u):
                        if u < 2:
                            pe.wait_ge(s_P, at(h * NT))
                        elif u < 4:
                            pe.wait_ge(s_hm, at(h * NT))
                        elif u - 4 < 4 * NG:
                            pe.wait_ge(s_relA, at(h * (4 * NG) + u - 3))
                        else:
                            pe.wait_ge(s_relD, at(h * NG + u - 3 - 4 * NG))
                        J.pe_unit(pe, h * 5 + u // NG, u % NG, E.bank[u % 4])

                    for u in range(2 * NG):
                        unit(u)
                    pe.wait_ge(s_relA, at(h * (4 * NG) + 2 * NG))
                    pe.wait_ge(s_og, at(h * NT))
                    for r, (a, z) in enumerate(VG):
                        if r == 4:
                            pe.wait_ge(s_v1, at(h * 5 + 1))
                        for t in range(a, z):
                            ins = pe.transpose(E.bank[VB[r]][:, (t - a) * P:(t - a + 1) * P], gT[:, t * P:(t + 1) * P], E.ident[:, :])
                        ins.then_inc(s_vT, 1)
                    def key_step(s):
                        if s < NT:
                            if s >= 2:
                                pe.wait_ge(s_kw, at(h * NT + s - 1))
                            pe.transpose(E.bank[4 + s % 2][:, 0:P], kT[:, s * P:(s + 1) * P], E.ident[:, :]).then_inc(s_kT, 1)
                        c = s - 1
                        if 0 <= c < NT:
                            pe.wait_ge(s_kw, at(h * NT + c + 1))
                            if c >= 2:
                                pe.wait_ge(s_kvb, at(h * NT + c - 1))
                            for d in range(2):
                                ins = pe.matmul(E.bank[6 + c % 2][:, d * E1:(d + 1) * E1], kw[c % 2][:, d, :],
                                                v1[:, c, :], start=True, stop=True, skip_group_check=True)
                            ins.then_inc(s_kv, 1)

                    for i in range(3 * NG):
                        unit(2 * NG + i)
                        if i == 0:
                            pe.wait_ge(s_v1, at(h * 5 + 5))
                        key_step(2 * i)
                        key_step(2 * i + 1)
                    pe.wait_ge(s_relA, at(h * (4 * NG) + 4 * NG))
                    pe.wait_ge(s_relD, at(h * NG + NG))
                    for s in range(NT + 3):
                        if s < NT:
                            if s >= 2:
                                pe.wait_ge(s_P, at(h * NT + s - 1))
                            tok = slice(s * P, (s + 1) * P)
                            pe.matmul(E.bank[s % 2][:, 0:P], kT[:, tok], qT[:, tok], start=True, stop=True).then_inc(s_S, 1)
                        c = s - 1
                        if 0 <= c < NT:
                            pe.wait_ge(s_P, at(h * NT + c + 1))
                            pe.wait_ge(s_qw, at(h * NT + c + 1))
                            if c == 0:
                                pe.wait_ge(s_cf, at(h * (NS - 1) + NS - 1))
                                pe.wait_ge(s_rev, at(h * (NS - 1) + NS - 1))
                            if c == 2:
                                pe.wait_ge(s_kvb, at(h * NT + NT))
                            if c >= 4:
                                pe.wait_ge(s_hm, at(h * NT + c - 3))
                            for d in range(2):
                                out = num_bank(c)[:, d * E1:(d + 1) * E1]
                                ins = pe.matmul(out, bc[c % NB][:, d, :], v1[:, c, :], start=True, stop=(c == CTX),
                                                skip_group_check=True)
                                if c < CTX:
                                    ins = pe.matmul(out, bc[c % NB][:, 2 + d, :], CC[:, d, c + d, :], start=False, stop=True,
                                                    skip_group_check=True)
                            ins.then_inc(s_num, 1)
                        c = s - 3
                        if c >= 0:
                            pe.wait_ge(s_hm, at(h * NT + c + 1))
                            if c >= 2:
                                pe.wait_ge(s_og, at(h * NT + c - 1))
                            pe.transpose(E.bank[4 + c % 2][:, 0:P], hm[c % 2][:, :], E.ident[:, :]).then_inc(s_hT, 1)


def build(nc, a, outs):
    E = Env()
    E.nc, E.a = nc, a
    (E.out_prompt, E.out_sample, new_k, new_v, E.new_C, E.new_n, E.new_m) = outs
    E.out_prompt = E.out_prompt[0]
    E.out_sample = E.out_sample[0]
    E.new_k = new_k[0, 0].rearrange("s h d -> s (h d)")
    E.new_v = new_v[0, 0].rearrange("s h d -> s (h d)")
    E.cache_v = a["cache_v"][0, 0].rearrange("(t p) h d -> p t (h d)", p=P)
    E.x_tile = lambda n: a["x_sample"][0, ds(n * P, P), :] if not isinstance(n, int) else a["x_sample"][0, n * P:(n + 1) * P, :]
    dram = lambda n, s: nc.dram_tensor(n, s, F32, kind="Internal").ap()
    E.gates_dram = dram("gate_rows", [2, 2, D])
    E.ckt_dram = dram("cached_keys_turned", [P, NKV * PAST])
    E.ogT_dram = dram("gated_output", [KT, P, T])
    E.x1_dram = dram("layer0_output", [T, D])
    E.rows_dram = dram("gate_rows_mlstm", [MH, NT, 4, P])
    E.decay_dram = dram("decays", [2, MH, NT])
    with ExitStack() as ctx:
        sb = lambda n, s, d=F32: ctx.enter_context(nc.sbuf_tensor(n, s, d))
        E.s_tick = ctx.enter_context(nc.semaphore("tick"))
        phase_semaphores = []

        def semaphore(name):
            phase_semaphores.append(nc.alloc_semaphore(name=name))
            return phase_semaphores[-1]
        E.semaphore = semaphore

        def start_at_one():
            for s in phase_semaphores:
                nc.gpsimd.sem_inc(s, 1)
            nc.all_engine_barrier()
        E.start_at_one = start_at_one

        def run(phase, *args):
            phase(E, *args)
            nc.clear_and_free_semaphores(list(phase_semaphores))
            nc.all_engine_barrier()
            phase_semaphores.clear()
        E.PS = ctx.enter_context(nc.psum_tensor("psum", [P, 8, 512], F32))
        E.bank = [E.PS[:, b, :] for b in range(8)]
        E.ident = sb("ident", [P, P])
        E.eps = sb("eps", [P, 1])
        E.one = sb("one", [P, 1])
        E.hscale = sb("hscale", [P, 2, 2, KT])
        E.hshift = sb("hshift", [P, 2, 2, KT])
        with ExitStack() as c1:
            E.h_hi = c1.enter_context(nc.sbuf_tensor("h_hi", [P, KT, T], F32R))
            E.h_lo = c1.enter_context(nc.sbuf_tensor("h_lo", [P, KT, T], F32R))
            with ExitStack() as c2:
                E.wmask = c2.enter_context(nc.sbuf_tensor("wmask", [P, 3, 3 * P], BF16))
                E.identb = c2.enter_context(nc.sbuf_tensor("identb", [P, P], BF16))
                with ExitStack() as c3:
                    E.wmaskf = c3.enter_context(nc.sbuf_tensor("wmaskf", [P, 3, 3 * P], F32))
                    run(phase_pre)
                run(phase_attn)
            run(phase_out, 0)
            with ExitStack() as c2:
                E.causal = c2.enter_context(nc.sbuf_tensor("causal", [P, 2, P], F32))
                E.cols = c2.enter_context(nc.sbuf_tensor("gate_columns", [P, NT, 3, 2, MH], F32))
                E.decay = c2.enter_context(nc.sbuf_tensor("decay_factors", [P, 2, MH, NT], F32))
                run(phase_gates)
                run(phase_mlstm)
        run(phase_out, 1)


_INS = ["x_prompt", "x_sample", "cache_k", "cache_v", "state_C", "state_n", "state_m", "c", "c_ctx",
        "attn_norm_w", "attn_ada_w", "attn_ada_b", "attn_w_in", "attn_sink", "attn_w_out",
        "mlstm_norm_w", "mlstm_ada_w", "mlstm_ada_b", "mlstm_w_in", "mlstm_b_gates", "mlstm_w_out",
        "final_norm_w"]
_OUTS = [(1, P, D), (1, SAMPLE, D), (1, 1, P, NKV, HD), (1, 1, P, NKV, HD),
         (1, 1, 2, MH, MHD, MHD), (1, 1, 2, MH, MHD), (1, 1, 2, MH)]


def shape_constants():
    import numpy as np
    f = np.float32
    q, j = np.arange(P)[:, None], np.arange(P)[None, :]
    prev = np.where(j >= q, 0, -BIG).astype(f)
    nxt = np.where(j <= q, 0, -BIG).astype(f)
    none = np.full((P, P), -BIG, f)
    own = np.zeros((P, P), f)
    window = np.stack([np.concatenate(x, 1) for x in ((none, own, nxt), (prev, own, nxt), (prev, own, none))], 1)
    causal = np.stack([np.where(q <= j, 0, BIG), np.where(q >= j, 0, BIG)], 1).astype(f)
    nf = HD // 4
    inv = (f(10000.0) ** (-np.arange(nf, dtype=f) / f(nf))).astype(f)
    t = np.arange(SAMPLE)
    row, col = (t // 64).astype(f), (t % 64).astype(f)
    ar, ac = inv[:, None] * row[None, :], inv[:, None] * col[None, :]
    ang = np.concatenate([ar, ar, ac, ac] * 2, 0).astype(f)
    sign = np.concatenate([-np.ones(nf), np.ones(nf)] * 4)[:, None].astype(f)
    rotary = np.stack([np.cos(ang), np.sin(ang) * sign], 1).astype(f)
    return {"ident": np.eye(P, dtype=f), "window_mask": window, "causal_mask": causal, "rotary": rotary}


def kernel(**inputs):
    import numpy as np
    import concourse.bacc as bacc
    from concourse.bass_utils import run_bass_kernel_spmd

    nc = bacc.Bacc("TRN2", target_bir_lowering=False, num_devices=1, dynamic_dma_scratch_size=1024)
    arrays = {k: np.ascontiguousarray(inputs[k]) for k in _INS}
    arrays.update(shape_constants())
    a = {k: nc.dram_tensor(f"in_{k}", v.shape, F32, kind="ExternalInput").ap() for k, v in arrays.items()}
    outs = [nc.dram_tensor(f"out_{i}", s, F32, kind="ExternalOutput").ap() for i, s in enumerate(_OUTS)]
    build(nc, a, outs)
    r = run_bass_kernel_spmd(nc, [{f"in_{k}": v for k, v in arrays.items()}], core_ids=[0])
    return tuple(r.results[0][f"out_{i}"] for i in range(len(_OUTS)))
```
